# Optimizing a Trainium2 kernel written in Bass

```python
import jax, jax.numpy as jnp
from jax import lax
import numpy as np

D_MODEL = 1024
BATCH = 1
SEQ = 256
DEPTH = 2

GRID_W = 64
CTX_LEN = 256
HEAD_DIM = 64
ATT_Q_HEADS = 8
ATT_KV_HEADS = 2
ATT_WINDOW = 128
ATT_BLOCK = 128
RET_HEADS = 4
RET_CHUNK = 128
RET_K_SCALE = HEAD_DIM ** -0.5
CONV_CH = 256
CONV_WIDTH = 31
ROPE_BASE = 10000.0
ROPE_FREQS = HEAD_DIM // 4
D_ATT = ATT_Q_HEADS * HEAD_DIM
D_RET = RET_HEADS * HEAD_DIM
D_MIX = D_ATT + D_RET + CONV_CH
ATT_KV_W = ATT_KV_HEADS * HEAD_DIM
C_ATT_K = 0
C_ATT_V = C_ATT_K + ATT_KV_W
C_RET_K = C_ATT_V + ATT_KV_W
C_RET_V = C_RET_K + D_RET
KV_COLS = C_RET_V + D_RET
C_ATT_Q = KV_COLS
C_RET_Q = C_ATT_Q + D_ATT
C_RET_G = C_RET_Q + D_RET
C_CONV = C_RET_G + D_RET
IN_COLS = C_CONV + 2 * CONV_CH
D_FF = 2816
N_EXPERTS = 8
TOP_K = 2
D_FF_EXPERT = 3584
N_DENSE = (DEPTH + 1) // 2
N_MOE = DEPTH // 2
EPS = 1e-6
NEG_INF = -1e30

kernel_name = 'hybrid_parallel_heads_dit_block'

def _rms(x, w):
    xf = x.astype(jnp.float32)
    y = xf * lax.rsqrt(jnp.mean(xf * xf, axis=-1, keepdims=True) + EPS)
    return (y * w.astype(jnp.float32)).astype(x.dtype)

def _modulate(x, w, shift, scale):
    return _rms(x, w) * (1 + scale) + shift

def _layernorm(x):
    xf = x.astype(jnp.float32)
    mu = jnp.mean(xf, axis=-1, keepdims=True)
    var = jnp.mean(jnp.square(xf - mu), axis=-1, keepdims=True)
    return (xf - mu) * lax.rsqrt(var + EPS)

def _adaln(cond, w, b):
    return jax.nn.silu(cond) @ w + b

def _heads(t, start, n_heads):
    return t[..., start:start + n_heads * HEAD_DIM].reshape(t.shape[:-1] + (n_heads, HEAD_DIM))

def _axial_rope(n):
    rows = n // GRID_W
    r = jnp.repeat(jnp.arange(rows), GRID_W).astype(jnp.float32)
    col = jnp.tile(jnp.arange(GRID_W), rows).astype(jnp.float32)
    freqs = ROPE_BASE ** (-jnp.arange(ROPE_FREQS, dtype=jnp.float32) / ROPE_FREQS)
    ang = jnp.stack([r[:, None] * freqs, col[:, None] * freqs], axis=1)
    return jnp.cos(ang)[:, None], jnp.sin(ang)[:, None]

def _apply_rope(x, cos, sin):
    xs = x.astype(jnp.float32).reshape(x.shape[:-1] + (2, 2, ROPE_FREQS))
    x1, x2 = xs[..., 0, :], xs[..., 1, :]
    out = jnp.stack([x1 * cos - x2 * sin, x2 * cos + x1 * sin], axis=-2)
    return out.reshape(x.shape).astype(x.dtype)

def _ctx_attention(q, k, v, sink):
    b, n, hq, d = q.shape
    g = ATT_KV_HEADS
    r = hq // g
    qg = q.reshape(b, n, g, r, d)
    s = jnp.einsum('bqgrd,bkgd->bgrqk', qg, k).astype(jnp.float32) * (d ** -0.5)
    s_sink = jnp.broadcast_to(sink.astype(jnp.float32).reshape(1, g, r, 1, 1), s.shape[:-1] + (1,))
    p = jax.nn.softmax(jnp.concatenate([s, s_sink], axis=-1), axis=-1)[..., :-1].astype(v.dtype)
    o = jnp.einsum('bgrqk,bkgd->bqgrd', p, v)
    return o.reshape(b, n, hq * d)

def _window_attention(q, k, v, k_ctx, v_ctx, sink):
    b, n, hq, d = q.shape
    g = ATT_KV_HEADS
    r = hq // g
    L = ATT_BLOCK
    nb = n // L
    halo = -(-ATT_WINDOW // L)
    qb = q.reshape(b, nb, L, g, r, d)

    def band(t):
        tp = jnp.pad(t, ((0, 0), (halo * L, halo * L), (0, 0), (0, 0))).reshape(b, nb + 2 * halo, L, g, d)
        return jnp.concatenate([tp[:, j:j + nb] for j in range(2 * halo + 1)], axis=2)

    kw, vw = band(k), band(v)
    kw_len = kw.shape[2]
    qpos = jnp.arange(nb)[:, None] * L + jnp.arange(L)[None, :]
    kpos = (jnp.arange(nb)[:, None] - halo) * L + jnp.arange(kw_len)[None, :]
    valid = ((kpos[:, None, :] >= 0) & (kpos[:, None, :] < n)
             & (jnp.abs(qpos[:, :, None] - kpos[:, None, :]) <= ATT_WINDOW))
    scale = d ** -0.5
    s_win = jnp.einsum('bnqgrd,bnkgd->bngrqk', qb, kw).astype(jnp.float32) * scale
    s_win = jnp.where(valid[None, :, None, None], s_win, NEG_INF)
    s_ctx = jnp.einsum('bnqgrd,bcgd->bngrqc', qb, k_ctx).astype(jnp.float32) * scale
    s_sink = jnp.broadcast_to(sink.astype(jnp.float32).reshape(1, 1, g, r, 1, 1), s_win.shape[:-1] + (1,))
    p = jax.nn.softmax(jnp.concatenate([s_win, s_ctx, s_sink], axis=-1), axis=-1).astype(v.dtype)
    o = (jnp.einsum('bngrqk,bnkgd->bnqgrd', p[..., :kw_len], vw)
         + jnp.einsum('bngrqc,bcgd->bnqgrd', p[..., kw_len:-1], v_ctx))
    return o.reshape(b, n, hq * d)

def _retention_chunks(q, k, v, log_g, s0, strict):
    b, n, h, dk = q.shape
    dv = v.shape[-1]
    L = RET_CHUNK
    nc = n // L
    qc = q.reshape(b, nc, L, h, dk)
    kc = k.reshape(b, nc, L, h, dk)
    vc = v.reshape(b, nc, L, h, dv)
    i = jnp.arange(L, dtype=jnp.float32)
    diff = i[:, None] - i[None, :]
    offset = 1.0 if strict else 0.0
    dmat = jnp.where((diff >= offset)[None], jnp.exp(jnp.maximum(diff, 0.0)[None] * log_g[:, None, None]), 0.0)
    a = jnp.einsum('bcihd,bcjhd->bchij', qc, kc) * dmat
    inner = jnp.einsum('bchij,bcjhe->bcihe', a, vc)
    kdec = jnp.exp((L - 1 - i)[None, :] * log_g[:, None])
    u = jnp.einsum('bcjhd,hj,bcjhe->cbhde', kc, kdec, vc)
    chunk_decay = jnp.exp(L * log_g)[None, :, None, None]

    def step(state, u_c):
        return chunk_decay * state + u_c, state

    final, r_in = lax.scan(step, s0.astype(u.dtype), u)
    xi = jnp.exp((i + 1)[None, :] * log_g[:, None])
    cross = jnp.einsum('bcihd,cbhde,hi->bcihe', qc, r_in, xi)
    return (inner + cross).reshape(b, n, h, dv), final

def _bidir_retention(q, k, v, lg_f, lg_b, s0_f, s0_b):
    o_f, s_f = _retention_chunks(q, k, v, lg_f, s0_f, strict=False)
    o_b, s_b = _retention_chunks(jnp.flip(q, 1), jnp.flip(k, 1), jnp.flip(v, 1), lg_b, s0_b, strict=True)
    return o_f + jnp.flip(o_b, 1), s_f, s_b

def _decayed_state(k, v, log_g, reverse):
    n = k.shape[1]
    pos = jnp.arange(n, dtype=jnp.float32)
    expo = pos if reverse else (n - 1) - pos
    w = jnp.exp(expo[None, :] * log_g[:, None])
    return jnp.einsum('bnhd,hn,bnhe->bhde', k, w, v)

def _retention_readout(o, gate, gn_w):
    y = _layernorm(o).reshape(o.shape[:-2] + (-1,)) * gn_w.astype(jnp.float32)
    return (jax.nn.silu(gate.astype(jnp.float32)) * y).astype(gate.dtype)

def _conformer_conv(u, w, bias, ln_w, ln_b):
    a, gt = jnp.split(u, 2, axis=-1)
    h = a * jax.nn.sigmoid(gt)
    pad = CONV_WIDTH // 2
    h = lax.conv_general_dilated(h, w[:, None, :].astype(h.dtype), window_strides=(1,),
                                 padding=[(pad, pad)], dimension_numbers=('NWC', 'WIO', 'NWC'),
                                 feature_group_count=CONV_CH) + bias
    h = _layernorm(h) * ln_w + ln_b
    return jax.nn.silu(h).astype(u.dtype)

def _swiglu(h, wg, wu, wd):
    return (jax.nn.silu(h @ wg) * (h @ wu)) @ wd

def _moe(h, router, wg, wu, wd):
    logits = (h @ router).astype(jnp.float32)
    top_v, top_i = lax.top_k(logits, TOP_K)
    w = jax.nn.softmax(top_v, axis=-1)
    combine = jnp.sum(jax.nn.one_hot(top_i, N_EXPERTS, dtype=jnp.float32) * w[..., None], axis=-2)
    out = jnp.zeros_like(h)
    for e in range(N_EXPERTS):
        out = out + combine[..., e:e + 1].astype(h.dtype) * _swiglu(h, wg[e], wu[e], wd[e])
    return out

def _channel_mixer(t, l, ffn_w_gate, ffn_w_up, ffn_w_down, router_w, moe_w_gate, moe_w_up, moe_w_down):
    i = l // 2
    if l % 2 == 0:
        return _swiglu(t, ffn_w_gate[i], ffn_w_up[i], ffn_w_down[i])
    return _moe(t, router_w[i], moe_w_gate[i], moe_w_up[i], moe_w_down[i])

def setup_inputs(seed: int = 0) -> dict:
    key = jax.random.key(seed)
    ks = jax.random.split(key, 32)
    f32 = jnp.float32

    def nrm(k, shape, scale):
        return jax.random.normal(k, shape, f32) * scale

    def gain(k, shape):
        return 1.0 + 0.05 * jax.random.normal(k, shape, f32)

    g0 = 1.0 - 2.0 ** (-5.0 - np.arange(RET_HEADS, dtype=np.float32))
    decay_logit = jnp.asarray(np.log(g0 / (1.0 - g0)), f32)
    return {
        'x': nrm(ks[0], (BATCH, SEQ, D_MODEL), 1.0),
        'c': nrm(ks[1], (BATCH, D_MODEL), 1.0),
        'ctx': nrm(ks[2], (BATCH, CTX_LEN, D_MODEL), 1.0),
        'c_ctx': nrm(ks[3], (D_MODEL,), 1.0),
        'ada_w': nrm(ks[4], (DEPTH, D_MODEL, 6 * D_MODEL), 0.5 * D_MODEL ** -0.5),
        'ada_b': nrm(ks[5], (DEPTH, 6 * D_MODEL), 0.02),
        'norm1_w': gain(ks[6], (DEPTH, D_MODEL)),
        'norm2_w': gain(ks[7], (DEPTH, D_MODEL)),
        'w_in': nrm(ks[8], (DEPTH, D_MODEL, IN_COLS), D_MODEL ** -0.5),
        'w_out': nrm(ks[9], (DEPTH, D_MIX, D_MODEL), D_MIX ** -0.5),
        'q_norm_w': gain(ks[10], (DEPTH, HEAD_DIM)),
        'k_norm_w': gain(ks[11], (DEPTH, HEAD_DIM)),
        'attn_sink': nrm(ks[12], (DEPTH, ATT_Q_HEADS), 0.5),
        'ret_decay_f': decay_logit + nrm(ks[13], (DEPTH, RET_HEADS), 0.1),
        'ret_decay_b': decay_logit + nrm(ks[14], (DEPTH, RET_HEADS), 0.1),
        'ret_gn_w': gain(ks[15], (DEPTH, D_RET)),
        'conv_w': nrm(ks[16], (DEPTH, CONV_WIDTH, CONV_CH), CONV_WIDTH ** -0.5),
        'conv_b': nrm(ks[17], (DEPTH, CONV_CH), 0.02),
        'conv_ln_w': gain(ks[18], (DEPTH, CONV_CH)),
        'conv_ln_b': nrm(ks[19], (DEPTH, CONV_CH), 0.02),
        'ffn_w_gate': nrm(ks[20], (N_DENSE, D_MODEL, D_FF), D_MODEL ** -0.5),
        'ffn_w_up': nrm(ks[21], (N_DENSE, D_MODEL, D_FF), D_MODEL ** -0.5),
        'ffn_w_down': nrm(ks[22], (N_DENSE, D_FF, D_MODEL), D_FF ** -0.5),
        'router_w': nrm(ks[23], (N_MOE, D_MODEL, N_EXPERTS), D_MODEL ** -0.5),
        'moe_w_gate': nrm(ks[24], (N_MOE, N_EXPERTS, D_MODEL, D_FF_EXPERT), D_MODEL ** -0.5),
        'moe_w_up': nrm(ks[25], (N_MOE, N_EXPERTS, D_MODEL, D_FF_EXPERT), D_MODEL ** -0.5),
        'moe_w_down': nrm(ks[26], (N_MOE, N_EXPERTS, D_FF_EXPERT, D_MODEL), D_FF_EXPERT ** -0.5),
    }

def reference(x, c, ctx, c_ctx, ada_w, ada_b, norm1_w, norm2_w, w_in, w_out, q_norm_w, k_norm_w,
              attn_sink, ret_decay_f, ret_decay_b, ret_gn_w, conv_w, conv_b, conv_ln_w, conv_ln_b,
              ffn_w_gate, ffn_w_up, ffn_w_down, router_w, moe_w_gate, moe_w_up, moe_w_down):
    b, n, _ = x.shape
    cos, sin = _axial_rope(n)
    zero_state = jnp.zeros((b, RET_HEADS, HEAD_DIM, HEAD_DIM), jnp.float32)
    for l in range(DEPTH):
        last = l == DEPTH - 1
        sh1, sc1, g1, sh2, sc2, g2 = jnp.split(_adaln(c, ada_w[l], ada_b[l])[:, None, :], 6, axis=-1)
        csh1, csc1, cg1, csh2, csc2, cg2 = jnp.split(_adaln(c_ctx, ada_w[l], ada_b[l]), 6, axis=-1)
        h = _modulate(x, norm1_w[l], sh1, sc1)
        hc = _modulate(ctx, norm1_w[l], csh1, csc1)
        p = h @ w_in[l]
        pc = hc @ (w_in[l][:, :KV_COLS] if last else w_in[l])

        k_c = _rms(_heads(pc, C_ATT_K, ATT_KV_HEADS), k_norm_w[l])
        v_c = _heads(pc, C_ATT_V, ATT_KV_HEADS)
        rk_c = _heads(pc, C_RET_K, RET_HEADS) * RET_K_SCALE
        rv_c = _heads(pc, C_RET_V, RET_HEADS)
        lg_f = jax.nn.log_sigmoid(ret_decay_f[l].astype(jnp.float32))
        lg_b = jax.nn.log_sigmoid(ret_decay_b[l].astype(jnp.float32))
        if last:
            s_f = _decayed_state(rk_c, rv_c, lg_f, reverse=False)
            s_b = _decayed_state(rk_c, rv_c, lg_b, reverse=True)
        else:
            ro_c, s_f, s_b = _bidir_retention(_heads(pc, C_RET_Q, RET_HEADS), rk_c, rv_c,
                                              lg_f, lg_b, zero_state, zero_state)

        q = _apply_rope(_rms(_heads(p, C_ATT_Q, ATT_Q_HEADS), q_norm_w[l]), cos, sin)
        k = _apply_rope(_rms(_heads(p, C_ATT_K, ATT_KV_HEADS), k_norm_w[l]), cos, sin)
        v = _heads(p, C_ATT_V, ATT_KV_HEADS)
        att = _window_attention(q, k, v, k_c, v_c, attn_sink[l])
        ro, _, _ = _bidir_retention(_heads(p, C_RET_Q, RET_HEADS), _heads(p, C_RET_K, RET_HEADS) * RET_K_SCALE,
                                    _heads(p, C_RET_V, RET_HEADS), lg_f, lg_b, s_f, s_b)
        ret = _retention_readout(ro, p[..., C_RET_G:C_RET_G + D_RET], ret_gn_w[l])
        cnv = _conformer_conv(p[..., C_CONV:IN_COLS], conv_w[l], conv_b[l], conv_ln_w[l], conv_ln_b[l])
        x = x + g1 * (jnp.concatenate([att, ret, cnv], axis=-1) @ w_out[l])

        if not last:
            q_c = _rms(_heads(pc, C_ATT_Q, ATT_Q_HEADS), q_norm_w[l])
            att_c = _ctx_attention(q_c, k_c, v_c, attn_sink[l])
            ret_c = _retention_readout(ro_c, pc[..., C_RET_G:C_RET_G + D_RET], ret_gn_w[l])
            cnv_c = _conformer_conv(pc[..., C_CONV:IN_COLS], conv_w[l], conv_b[l], conv_ln_w[l], conv_ln_b[l])
            ctx = ctx + cg1 * (jnp.concatenate([att_c, ret_c, cnv_c], axis=-1) @ w_out[l])

        h2 = _modulate(x, norm2_w[l], sh2, sc2)
        x = x + g2 * _channel_mixer(h2, l, ffn_w_gate, ffn_w_up, ffn_w_down,
                                    router_w, moe_w_gate, moe_w_up, moe_w_down)
        if not last:
            h2c = _modulate(ctx, norm2_w[l], csh2, csc2)
            ctx = ctx + cg2 * _channel_mixer(h2c, l, ffn_w_gate, ffn_w_up, ffn_w_down,
                                             router_w, moe_w_gate, moe_w_up, moe_w_down)
    return x


_drawn_inputs = setup_inputs


def setup_inputs(seed=0):
    import zlib

    import numpy as np

    out = dict(_drawn_inputs(seed))
    spreads = {}
    factors = {'norm1_w': 3.079,
     'q_norm_w': 7.627,
     'k_norm_w': 8.0,
     'attn_sink': 8.0,
     'ret_gn_w': 5.525,
     'conv_b': 8.0,
     'conv_ln_w': 3.882,
     'conv_ln_b': 20.521}
    for name, (base, spread) in spreads.items():
        noise = np.random.default_rng([zlib.crc32(name.encode()), seed]).standard_normal(out[name].shape)
        drawn = base * np.exp(spread * noise) if base else spread * noise
        out[name] = __import__('jax').numpy.asarray(drawn.astype(out[name].dtype))
    for name, factor in factors.items():
        out[name] = (out[name] * factor).astype(out[name].dtype)
    return out
```

```python
from contextlib import ExitStack

import concourse.bass as bass
from concourse import mybir

ALU = mybir.AluOpType
ACT = mybir.ActivationFunctionType
AX = mybir.AxisListType
F32 = mybir.dt.float32
I32 = mybir.dt.int32

P = 128
D_MODEL, SEQ, CTX_LEN, DEPTH = 1024, 256, 256, 2
HEAD_DIM, Q_HEADS, KV_HEADS, RET_HEADS = 64, 8, 2, 4
CONV_CH, CONV_WIDTH = 256, 31
D_FF, N_EXPERTS, D_FF_EXPERT = 2816, 8, 3584
GRID_W, ROPE_BASE, WINDOW = 64, 10000.0, 128
EPS = 1e-6

KT = D_MODEL // P
TT = SEQ // P
NT = 2 * TT
C_K, C_V, C_RK, C_RV, C_Q, C_RQ, C_RG, C_CONV, IN_COLS = 0, 128, 256, 512, 768, 1280, 1536, 1792, 2304
PCOLS = C_CONV
SLICE = 512
ITEM = KT * SLICE
RING = 6
MIX_RING = 4
FF_TILES = D_FF // P
EF_SLICES = D_FF_EXPERT // SLICE
PAIRS = N_EXPERTS // 2
PAIR_SLICES = 2 * EF_SLICES
PAIR_ITEMS = 3 * PAIR_SLICES
TAPS = 2 * CONV_WIDTH
BIG_NEG = -1.0e30
N_SMALL = 12


def shape_constants():
    import numpy as np

    part = np.arange(P)
    out = {}
    out["identity"] = np.eye(P)
    mask = np.zeros((P, TT, 2 * SEQ))
    for t in range(TT):
        far = np.abs((t * P + part)[:, None] - np.arange(SEQ)[None, :]) > WINDOW
        mask[:, t, :SEQ][far] = BIG_NEG
    out["mask"] = mask.reshape(P, -1)
    freqs = (ROPE_BASE ** (-np.arange(16, dtype=np.float32) / np.float32(16))).astype(np.float32)
    pos = np.arange(SEQ)
    ang = np.stack([(pos // GRID_W).astype(np.float32)[:, None] * freqs,
                    (pos % GRID_W).astype(np.float32)[:, None] * freqs], axis=1)
    cos, sin = np.cos(ang), np.sin(ang)
    c64 = np.stack([cos, cos], axis=2).reshape(TT, P, 64)
    s64 = np.stack([-sin, sin], axis=2).reshape(TT, P, 64)
    out["cos"] = c64.transpose(1, 0, 2).reshape(P, -1)
    out["sin"] = s64.transpose(1, 0, 2).reshape(P, -1)
    j = (np.arange(TT) * P)[None, :, None] + part[:, None, None]
    i = np.arange(SEQ)[None, None, :]
    out["ahead"] = np.maximum(i - j, 0).reshape(P, -1)
    out["behind"] = np.maximum(j - i, 0).reshape(P, -1)
    tok = (np.arange(TT) * P)[None, :] + part[:, None]
    e = np.stack([np.stack([SEQ - 1 - tok, tok], -1), np.stack([tok + 1, SEQ - tok], -1)], 1)
    out["exponents"] = e.reshape(P, -1)
    out["before"] = (part[:, None] < part[None, :]) * 1.0
    out["ones"] = np.ones((P, P))
    out["slots"] = np.tile(np.arange(P), (P, 1))
    out["experts"] = np.tile(np.arange(N_EXPERTS), (P, 1))
    at, places = 0, {}
    for name, a in out.items():
        places[name] = (at, a.shape[1])
        at += a.shape[1]
    return np.concatenate([a.astype(np.float32) for a in out.values()], axis=1), places


def build(nc, io, place):
    ctx = ExitStack()
    with ctx:
        def sb(name, shape, dt=F32):
            return ctx.enter_context(nc.sbuf_tensor(name, shape, dt))

        def sem(name):
            return ctx.enter_context(nc.semaphore(name))

        ring = sb("ring", [P, RING * ITEM])
        X = sb("X", [P, NT, D_MODEL])
        hTb = sb("hTb", [P, KT * NT * P])
        big = sb("big", [P, FF_TILES * 512])
        gb = sb("gb", [P, 2 * D_MODEL])
        nconst = sum(n for _, n in place.values())
        const = sb("const", [P, nconst])
        decay = sb("decay", [P, RET_HEADS, 512])
        ada = sb("ada", [P, 48, 2])
        scl = sb("scl", [P, 2, KT, 2])
        cload = sb("cload", [P, 2, KT])
        cond = sb("cond", [P, KT, 2])
        vrows = sb("vrows", [2 * KT + 2, P])
        vcols = sb("vcols", [P, 2 * KT + 2])
        convwr = sb("convwr", [CONV_WIDTH, CONV_CH])
        convw = sb("convw", [P, 2, CONV_WIDTH])
        routw = sb("routw", [P, KT, N_EXPERTS])
        qkw = sb("qkw", [P, 2, HEAD_DIM])
        sink = sb("sink", [P, Q_HEADS])
        nsink = sb("nsink", [P, Q_HEADS])
        dlog = sb("dlog", [P, 2, RET_HEADS])
        dneg = sb("dneg", [P, RET_HEADS, 2])
        dmin = sb("dmin", [P, RET_HEADS, 2])
        dln = sb("dln", [P, RET_HEADS, 2])
        dtok = sb("dtok", [P, 2, TT, RET_HEADS, 2])
        gnw = sb("gnw", [P, 256])
        lnw = sb("lnw", [P, 256])
        lnb = sb("lnb", [P, 256])
        ssq = sb("ssq", [P, NT])
        rstd = sb("rstd", [P, NT])
        qss = sb("qss", [P, NT, 10])
        qrs = sb("qrs", [P, NT, 10])
        nhalf = sb("nhalf", [P, 16])
        mx = sb("mx", [P, 2, Q_HEADS])
        negm = sb("negm", [P, 2, Q_HEADS])
        rsum = sb("rsum", [P, 2, Q_HEADS])
        esink = sb("esink", [P, 2, Q_HEADS])
        lnm = sb("lnm", [P, 16])
        lnv = sb("lnv", [P, 16])
        lnr = sb("lnr", [P, 16])
        bst = sb("bst", [P, NT, 6])
        bag = sb("bag", [P, NT, 2])
        lnt = sb("lnt", [P, 16])
        qst = sb("qst", [P, NT, 10])
        top = sb("top", [P, 7, TT, N_EXPERTS])
        best = sb("best", [P, 8, TT])
        most = sb("most", [P, 2])
        mosti = sb("mosti", [P, 1], I32)

        bank = [ctx.enter_context(nc.psum_tensor(f"bank{i}", [P, 512], F32)) for i in range(8)]
        VB, AB, OB = bank[0:4], bank[4:7], bank[7]

        def table(name):
            a, n = place[name]
            return const[:, a:a + n]

        ident = table("identity")
        mask = table("mask").rearrange("p (t k) -> p t k", t=TT)
        cos64 = table("cos").rearrange("p (t k) -> p t k", t=TT)
        sin64 = table("sin").rearrange("p (t a h f) -> p t a h f", t=TT, a=2, h=2)
        ahead, behind = table("ahead"), table("behind")
        expo = table("exponents").rearrange("p (w d) -> p w d", d=2)

        def slot(s, k=KT):
            return ring[:, s * ITEM:(s + 1) * ITEM].rearrange("p (k n) -> p k n", k=k)

        proj = big[:, 0:NT * PCOLS].rearrange("p (t c) -> p t c", t=NT)
        xn = big[:, NT * PCOLS:NT * PCOLS + 4096].rearrange("p (t c) -> p t c", t=NT)
        row = big[0:2, 0:6 * D_MODEL]
        hT = hTb[:, :].rearrange("p (k c) -> p k c", k=KT)
        mixT = hT

        def cut(region, start):
            at = [start]

            def take(n):
                at[0] += n
                return region[:, at[0] - n:at[0]]
            return take

        mixed = cut(ring, MIX_RING * ITEM)
        AD = mixed(2048).rearrange("p (h k) -> p h k", h=RET_HEADS)
        VW = mixed(1024).rearrange("p (t h d e) -> p t h d e", t=TT, h=RET_HEADS, d=2)
        SC = mixed(2048).rearrange("p (b k) -> p b k", b=4)
        PT = mixed(1024).rearrange("p (b k) -> p b k", b=2)
        CBW = SEQ + CONV_WIDTH - 1
        CB = mixed(2 * 2 * CBW).rearrange("p (c s n) -> p c s n", c=2, s=2)
        AKT = mixed(512)
        TMP = AD.rearrange("p h k -> p (h k)")[:, 0:1280]
        room = cut(big, NT * PCOLS)
        QK = room(NT * 640).rearrange("p (t h d) -> p t h d", t=NT, d=HEAD_DIM)
        RO = room(1024).rearrange("p (t c) -> p t c", t=NT)
        ST = room(512).rearrange("p (c n) -> p c n", c=2)
        low = cut(gb, 0)
        CA = low(1024).rearrange("p (c s n) -> p c s n", c=2, s=2)
        RW = low(1024).rearrange("p (t c) -> p t c", t=NT)
        heads = cut(hTb, 0)
        AQT = heads(2048).rearrange("p (r t n) -> p r t n", r=4, t=NT)
        RT = heads(2048).rearrange("p (b t n) -> p b t n", b=4, t=NT)
        CV = AD.rearrange("p h k -> p (h k)")[:, 0:1024].rearrange("p (t c) -> p t c", t=NT)
        HFF = big[:, :].rearrange("p (f n) -> p f n", f=FF_TILES)
        dec = decay[:, :, :].rearrange("p h k -> p (h k)")
        SG = dec[:, 0:1024].rearrange("p (b n) -> p b n", b=2)
        YG = dec[:, 1024:2048].rearrange("p (b n) -> p b n", b=2)
        ebig = cut(big, 0)
        PA = ebig(2048).rearrange("p (t e s) -> p t e s", t=TT, e=N_EXPERTS)
        SA = ebig(2048).rearrange("p (e n) -> p e n", e=N_EXPERTS)
        XE = ebig(2048).rearrange("p (b k s) -> p b k s", b=2, k=KT)
        YS = ebig(1024)
        xe_n = big[:, NT * PCOLS:NT * PCOLS + 2048].rearrange("p (t c) -> p t c", t=TT)
        HE = big[:, 9216:10240].rearrange("p (b n) -> p b n", b=2)
        HTE = big[:, 10240:11264].rearrange("p (b j n) -> p b j n", b=2, j=4)
        ehalf = cut(hTb, 0)
        SCAT = ehalf(512).rearrange("p (b n) -> p b n", b=2)
        SGE = ehalf(1024).rearrange("p (b n) -> p b n", b=2)
        ACC = ehalf(2048).rearrange("p (t c) -> p t c", t=TT)
        GB = gb[:, :].rearrange("p (s n) -> p s n", s=2)

        slot_loaded = [sem(f"slot_loaded{i}") for i in range(RING)]
        slot_used = sem("slot_used")
        v_full, v_done = sem("vector_bank_full"), sem("vector_bank_evacuated")
        a_full, a_done = sem("scalar_bank_full"), sem("scalar_bank_evacuated")
        tables_in, x_in, c_in = sem("tables_in"), sem("x_in"), sem("c_in")
        small_in, bias_in, router_in = sem("small_in"), sem("bias_in"), sem("router_in")
        cond_ready = sem("cond_ready")
        mod_ready = sem("modulation_ready")
        sq_ready, rstd_ready, xn_ready = sem("squares_ready"), sem("rstd_ready"), sem("normalized_ready")
        x_ready = sem("residual_ready")
        dneg_ready, dln_ready = sem("decay_arg_ready"), sem("decay_ln_ready")
        dexp_in, dexp_out = sem("decay_exponents_ready"), sem("decay_exp_ready")
        qss_ready, qrs_ready, qk_ready = sem("qk_squares_ready"), sem("qk_rstd_ready"), sem("qk_ready")
        vw_ready = sem("weighted_values_ready")
        pad_ready = sem("conv_pad_ready")
        negm_ready, exp_ready = sem("negmax_ready"), sem("exp_ready")
        sarg_ready, esink_ready = sem("sink_arg_ready"), sem("sink_exp_ready")
        att_done, att_read = sem("attention_products"), sem("attention_evacuated")
        ro_var, ro_rstd = sem("retention_variance_ready"), sem("retention_rstd_ready")
        cv_var, cv_rstd = sem("conv_variance_ready"), sem("conv_rstd_ready")
        ln_ready, rg_ready = sem("conv_norm_ready"), sem("retention_gate_ready")
        act_mix = sem("conv_silu_ready")
        out_ready = sem("output_ready")
        lexp_in, lexp_out = sem("gate_arg_ready"), sem("gate_exp_ready")
        mask_ready = sem("top2_masks_ready")
        scat_in = sem("scatter_rows_ready")
        most_ready = sem("most_tokens_ready")
        gate_full, gate_read = sem("gate_full"), sem("gate_silu_done")
        up_full, up_read = sem("up_full"), sem("up_multiplied")
        h_turned, ht_ready = sem("hidden_transposed"), sem("hidden_transposed_ready")
        down_done, y_ready = sem("down_done"), sem("expert_out_ready")
        gather_full, xe_lo, xe_hi = sem("gather_full"), sem("gathered_low_ready"), sem("gathered_high_ready")
        st_ready = sem("scatter_matrix_ready")
        scatter_full, scatter_read = sem("scatter_full"), sem("scatter_added")
        out_in = sem("out_stored")
        tap_done = sem("conv_tap_done")
        rank_moved = sem("rank_moved")
        v_step, a_step, p_step = sem("vector_step"), sem("scalar_step"), sem("gpsimd_step")

        block = ctx.enter_context(nc.Block())

        def counter(eng):
            seen = {}

            def after(s, n=1):
                seen[s] = seen.get(s, 0) + n
                eng.wait_ge(s, seen[s])
            return after

        def stepper(eng, s):
            n = [0]

            def step(ins):
                n[0] += 1
                ins.then_inc(s, 1)
                eng.wait_ge(s, n[0])
            return step

        def tiles_of(layer):
            return range(NT) if layer == 0 else range(TT)

        def cols(w, a, b):
            return w[:, a:b].rearrange("(k p) n -> p k n", p=P)

        IN_SLICES = [(C_Q, C_RQ), (0, 384), (384, 768), (C_RQ, C_CONV), (C_CONV, IN_COLS)]
        items = []
        for layer in range(DEPTH):
            n = 0
            for s in range(12):
                items.append((io["ada_w"][layer][:, s * SLICE:(s + 1) * SLICE]
                              .rearrange("(p k) n -> p k n", k=KT), SLICE, n % MIX_RING, 1))
                n += 1
            for a, b in IN_SLICES:
                items.append((cols(io["w_in"][layer], a, b), b - a, n % MIX_RING, 1))
                n += 1
            for h in range(2):
                items.append((cols(io["w_out"][layer], h * SLICE, (h + 1) * SLICE), SLICE, n % MIX_RING, 1))
                n += 1
            if layer == 0:
                for s in range(FF_TILES // 2):
                    items.append(("gate_up", s, s % RING, 2))
                n = FF_TILES // 2
                for h in range(2):
                    for f0 in range(0, FF_TILES, 8):
                        items.append((io["ffn_w_down"][0][f0 * P:min(f0 + 8, FF_TILES) * P, h * SLICE:(h + 1) * SLICE]
                                      .rearrange("(k p) n -> p k n", p=P), SLICE, n % RING, 1))
                        n += 1
        FIRST_EXPERT_ITEM = len(items)
        before_experts = [sum(it[3] for it in items if it[2] == s) for s in range(RING)]
        last_use = {}
        job = {}

        @block.tensor
        def _(pe):
            after = counter(pe)
            n_v, n_a, n_i, n_u = [0], [0], [0], [0]
            uses = [0] * RING

            def open_v(name=None):
                n = n_v[0]
                n_v[0] += 1
                if n >= len(VB):
                    pe.wait_ge(v_done, n - len(VB) + 1)
                if name:
                    job[name] = n
                return VB[n % len(VB)]

            def open_a(name=None):
                n = n_a[0]
                n_a[0] += 1
                if n >= len(AB):
                    pe.wait_ge(a_done, n - len(AB) + 1)
                if name:
                    job[name] = n
                return AB[n % len(AB)]

            def next_item():
                n = n_i[0]
                n_i[0] += 1
                s = items[n][2]
                uses[s] += items[n][3]
                pe.wait_ge(slot_loaded[s], 16 * uses[s])
                return n, s

            def ada_rows():
                pe.wait_ge(cond_ready, 1)
                for s in range(12):
                    n, place_ = next_item()
                    w = slot(place_)
                    b = open_v()
                    for k in range(KT):
                        mm = nc.tensor.matmul(b[0:2, :], cond[:, k, :], w[:, k, :], start=(k == 0), stop=(k == KT - 1))
                    mm.then_inc(v_full, 1)
                    last_use[n] = (v_full, n_v[0])
                pe.wait_ge(v_done, n_v[0])
                b = open_v()
                for c in range(48):
                    nc.tensor.matmul(b[:, 2 * c:2 * c + 2], row[:, c * P:(c + 1) * P], ident[0:2, 0:2],
                                     start=True, stop=True)
                after(small_in, 16 * N_SMALL)
                nc.tensor.transpose(b[:, 96:96 + 2 * KT + 2], vrows[:, :], ident[0:2 * KT + 2, 0:2 * KT + 2])\
                    .then_inc(v_full, 1)

            def turn_normalized(streams):
                for s in streams:
                    after(xn_ready, TT)
                    for kp in range(KT // 2):
                        b = open_v() if s == 0 else open_a()
                        for kk in range(2):
                            for t in range(TT):
                                k = 2 * kp + kk
                                mm = nc.tensor.transpose(b[:, (kk * TT + t) * P:(kk * TT + t + 1) * P],
                                                         xn[:, s * TT + t, k * P:(k + 1) * P], ident)
                        mm.then_inc(v_full if s == 0 else a_full, 1)

            def modulated_in(streams):
                pe.wait_ge(v_done, n_v[0])
                if 1 in streams:
                    pe.wait_ge(a_done, n_a[0])

            def project_in(layer):
                for a, b_ in IN_SLICES[:-1]:
                    n, place_ = next_item()
                    w = slot(place_)
                    tiles = range(NT) if layer == 0 or b_ <= C_Q else range(TT)
                    for t in tiles:
                        name = ("in", layer, a, t)
                        b = open_v(name) if t % 2 == 0 else open_a(name)
                        for k in range(KT):
                            mm = nc.tensor.matmul(b[:, 0:b_ - a], hT[:, k, t * P:(t + 1) * P],
                                                  ring[:, place_ * ITEM + k * (b_ - a):place_ * ITEM + (k + 1) * (b_ - a)],
                                                  start=(k == 0), stop=(k == KT - 1))
                        mm.then_inc(v_full if t % 2 == 0 else a_full, 1)
                    last_use[n] = (a_full, n_a[0])
                n, place_ = next_item()
                w = slot(place_)
                cols_ = (SEQ + CTX_LEN) if layer == 0 else SEQ
                for ct in range(2):
                    for half in (1, 0):
                        b = open_a(("conv_gate", layer, ct)) if half else open_v()
                        for k in range(KT):
                            c0 = half * CONV_CH + ct * P
                            mm = nc.tensor.matmul(b[:, 0:cols_], w[:, k, c0:c0 + P], hT[:, k, 0:cols_],
                                                  start=(k == 0), stop=(k == KT - 1))
                        mm.then_inc(a_full if half else v_full, 1)
                last_use[n] = (v_full, n_v[0])

            def turn_heads(layer):
                b = open_v()
                for ct in range(2):
                    mm = nc.tensor.transpose(b[:, ct * 32:ct * 32 + CONV_WIDTH],
                                             convwr[:, ct * P:(ct + 1) * P], ident[0:CONV_WIDTH, 0:CONV_WIDTH])
                mm.then_inc(v_full, 1)
                pe.wait_ge(a_done, n_a[0])
                for t in tiles_of(layer):
                    b = open_v()
                    for i, c in enumerate((C_RQ, C_RQ + P, C_RK, C_RK + P)):
                        mm = nc.tensor.transpose(b[:, i * P:(i + 1) * P], proj[:, t, c:c + P], ident)
                    mm.then_inc(v_full, 1)

            def turn_qk(layer):
                bk = OB
                for t in range(NT):
                    if t in tiles_of(layer):
                        b = open_a()
                    after(qk_ready)
                    if t in tiles_of(layer):
                        for r in range(4):
                            mm = nc.tensor.transpose(b[:, r * P:(r + 1) * P],
                                                     QK[:, t, 2 * r:2 * r + 2, :].rearrange("p h d -> p (h d)"), ident)
                        mm.then_inc(a_full, 1)
                    mm = nc.tensor.transpose(bk[:, t * P:(t + 1) * P],
                                             QK[:, t, 8:10, :].rearrange("p h d -> p (h d)"), ident)
                    mm.then_inc(att_done, 1)

            def states():
                b = open_v()
                after(vw_ready, TT)
                for pair in range(2):
                    for t in range(TT):
                        mm = nc.tensor.matmul(b[:, pair * 256:(pair + 1) * 256],
                                              proj[:, TT + t, C_RK + pair * P:C_RK + (pair + 1) * P],
                                              VW[:, t, 2 * pair:2 * pair + 2, :, :].rearrange("p h d e -> p (h d e)"),
                                              start=(t == 0), stop=(t == TT - 1))
                mm.then_inc(v_full, 1)

            def retention(layer):
                def scores(s, h):
                    b = open_v(("decayed", layer, s, h))
                    lo = 64 * (h % 2)
                    for jt in range(TT):
                        mm = nc.tensor.matmul(b[:, jt * SEQ:(jt + 1) * SEQ],
                                              RT[lo:lo + 64, 2 + h // 2, s * TT + jt, :],
                                              RT[lo:lo + 64, h // 2, s * TT:s * TT + TT, :].rearrange("p t n -> p (t n)"),
                                              start=True, stop=True)
                    mm.then_inc(v_full, 1)

                def apply(s, h, outs):
                    pe.wait_ge(v_done, job[("decayed", layer, s, h)] + 1)
                    for it in range(TT):
                        for jt in range(TT):
                            mm = nc.tensor.matmul(outs[it][:, h * 64:(h + 1) * 64],
                                                  AD[:, h, jt * SEQ + it * P:jt * SEQ + (it + 1) * P],
                                                  proj[:, s * TT + jt, C_RV + h * 64:C_RV + (h + 1) * 64],
                                                  start=(jt == 0), stop=(jt == TT - 1))
                        if h == RET_HEADS - 1:
                            mm.then_inc(a_full, 1)

                pe.wait_ge(v_done, n_v[0])
                for s in ((0, 1) if layer == 0 else (0,)):
                    scores(s, 0)
                    outs = [open_a(("inner", layer, s)), open_a()]
                    for h in range(RET_HEADS):
                        if h + 1 < RET_HEADS:
                            scores(s, h + 1)
                        apply(s, h, outs)
                for t in range(TT):
                    b = open_v()
                    for pair in range(2):
                        mm = nc.tensor.matmul(b[:, pair * 256:(pair + 1) * 256], RT[:, pair, t, :], ST[:, pair, :],
                                              start=True, stop=True)
                    mm.then_inc(v_full, 1)

            def attention(layer):
                its = [(t, r, g) for t in tiles_of(layer) for r in range(4) for g in range(2)]
                after(att_read)
                pe.wait_ge(a_done, n_a[0])

                def scores(n):
                    t, r, g = its[n]
                    b = open_v()
                    k0 = 0 if t < TT else SEQ
                    nc.tensor.matmul(b[:, k0:2 * SEQ], AQT[64 * g:64 * g + 64, r, t, :], AKT[64 * g:64 * g + 64, k0:],
                                     start=True, stop=True).then_inc(v_full, 1)

                def turn(n):
                    t, r, g = its[n]
                    b = open_a(("probs", layer, n))
                    after(exp_ready)
                    for kb in range(0 if t < TT else TT, NT):
                        mm = nc.tensor.transpose(b[:, kb * P:(kb + 1) * P], SC[:, n % 4, kb * P:(kb + 1) * P], ident)
                    mm.then_inc(a_full, 1)

                def values(n):
                    t, r, g = its[n]
                    head = g * 4 + r
                    if n % 8 == 0 and n:
                        after(att_read)
                    pe.wait_ge(a_done, job[("probs", layer, n)] + 1)
                    first = 0 if t < TT else TT
                    for kb in range(first, NT):
                        mm = nc.tensor.matmul(OB[:, head * 64:(head + 1) * 64], PT[:, n % 2, kb * P:(kb + 1) * P],
                                              proj[:, kb, C_V + 64 * g:C_V + 64 * g + 64],
                                              start=(kb == first), stop=(kb == NT - 1))
                    mm.then_inc(att_done, 1)

                for n in range(len(its) + 3):
                    if n < len(its):
                        scores(n)
                    if 2 <= n < len(its) + 2:
                        turn(n - 2)
                    if n >= 3:
                        values(n - 3)
                after(att_read)

            def turn_conv(layer):
                pe.wait_ge(tap_done, TAPS * (layer + 1))
                for t in tiles_of(layer):
                    b = open_v()
                    for ct in range(2):
                        mm = nc.tensor.transpose(b[:, ct * P:(ct + 1) * P],
                                                 CA[:, ct, t // TT, (t % TT) * P:(t % TT + 1) * P], ident)
                    mm.then_inc(v_full, 1)

            def turn_mix(layer):
                after(act_mix)
                for t in tiles_of(layer):
                    for half in range(2):
                        b = open_v() if half == 0 else open_a()
                        for i in range(4):
                            c = C_Q + (half * 4 + i) * P
                            mm = nc.tensor.transpose(b[:, i * P:(i + 1) * P], proj[:, t, c:c + P], ident)
                        mm.then_inc(v_full if half == 0 else a_full, 1)

            def spread_gate(group, streams):
                for s in streams:
                    for half in range(2):
                        b = open_a()
                        for i in range(4):
                            c = group * KT + half * 4 + i
                            mm = nc.tensor.matmul(b[:, i * P:(i + 1) * P], ada[:, c, s:s + 1].broadcast_to([P, P]), ident,
                                                  start=True, stop=True)
                        mm.then_inc(a_full, 1)

            def project_out(layer):
                pe.wait_ge(v_done, n_v[0])
                pe.wait_ge(a_done, n_a[0])
                for half in range(2):
                    n, place_ = next_item()
                    w = slot(place_)
                    for t in tiles_of(layer):
                        b = open_v()
                        for k in range(KT):
                            mm = nc.tensor.matmul(b[:, :], mixT[:, k, t * P:(t + 1) * P], w[:, k, :],
                                                  start=(k == 0), stop=(k == KT - 1))
                        mm.then_inc(v_full, 1)
                    last_use[n] = (v_full, n_v[0])
                job[("mixed", layer)] = n_v[0]

            def dense_ffn():
                for s in range(FF_TILES // 2):
                    n, place_ = next_item()
                    w = slot(place_)
                    for f in range(2):
                        for half in range(2):
                            b = open_a(("gate", 2 * s + f)) if half == 0 else open_v(("up", 2 * s + f))
                            for k in range(KT):
                                c0 = half * 256 + f * P
                                mm = nc.tensor.matmul(b[:, :], w[:, k, c0:c0 + P], hT[:, k, :],
                                                      start=(k == 0), stop=(k == KT - 1))
                            mm.then_inc(a_full if half == 0 else v_full, 1)
                    last_use[n] = (v_full, n_v[0])
                spread_gate(5, (0, 1))
                pe.wait_ge(v_done, n_v[0])
                pe.wait_ge(a_done, n_a[0])
                for half in range(2):
                    outs = [open_v() for _ in range(NT)]
                    for f0 in range(0, FF_TILES, 8):
                        n, place_ = next_item()
                        w = slot(place_)
                        for f in range(f0, min(f0 + 8, FF_TILES)):
                            for t in range(NT):
                                mm = nc.tensor.matmul(outs[t][:, :], HFF[:, f, t * P:(t + 1) * P], w[:, f - f0, :],
                                                      start=(f == 0), stop=(f == FF_TILES - 1))
                                if f == FF_TILES - 1:
                                    mm.then_inc(v_full, 1)
                        if f < FF_TILES - 1:
                            n_u[0] += 1
                            mm.then_inc(slot_used, 1)
                            last_use[n] = (slot_used, n_u[0])
                        else:
                            last_use[n] = (v_full, n_v[0])

            def routing():
                b = open_v()
                after(router_in, 16)
                for t in range(TT):
                    for k in range(KT):
                        mm = nc.tensor.matmul(b[:, t * N_EXPERTS:(t + 1) * N_EXPERTS], hT[:, k, t * P:(t + 1) * P],
                                              routw[:, k, :],
                                              start=(k == 0), stop=(k == KT - 1))
                mm.then_inc(v_full, 1)
                b = open_v()
                after(mask_ready)
                chosen = top[:, 0, :, :]
                nc.tensor.matmul(b[:, 0:8], table("before"), chosen[:, 0, :], start=True, stop=True)
                nc.tensor.matmul(b[:, 8:16], table("ones"), chosen[:, 0, :], start=True, stop=False)
                nc.tensor.matmul(b[:, 8:16], table("before"), chosen[:, 1, :], start=False, stop=True)
                nc.tensor.matmul(b[:, 16:24], table("ones"), chosen[:, 0, :], start=True, stop=False)
                nc.tensor.matmul(b[:, 16:24], table("ones"), chosen[:, 1, :], start=False, stop=True).then_inc(v_full, 1)

            def scatter_matrices(part):
                for e in range(0, N_EXPERTS, 2):
                    b = open_v()
                    after(scat_in)
                    for i in range(2):
                        for t in range(TT):
                            mm = nc.tensor.transpose(b[:, i * 256 + t * P:i * 256 + (t + 1) * P],
                                                     XE[:, (e // 2) % 2, i * TT + t, :], ident)
                    mm.then_inc(v_full, 1)

            def experts(part):
                G, U, Y, T, M = bank[0], bank[1], bank[2:4], bank[4:6], bank[6:8]
                s0 = part * N_EXPERTS * EF_SLICES
                e0 = part * N_EXPERTS
                pe.wait_ge(v_done, n_v[0])
                pe.wait_ge(a_done, n_a[0])

                with pe.Fori(0, PAIRS) as i:
                    def gather(ee):
                        e = 2 * i + ee
                        pe.wait_ge(scatter_read, i * 8 + (4 * e0 + 1))
                        for k in range(KT):
                            for t in range(TT):
                                mm = nc.tensor.matmul(M[k // 4][:, (k % 4) * P:(k % 4 + 1) * P], xe_n[:, t, k * P:(k + 1) * P],
                                                      PA[:, t, bass.ds(e, 1), :].rearrange("p e s -> p (e s)"),
                                                      start=(t == 0), stop=(t == TT - 1))
                            if k % 4 == 3:
                                mm.then_inc(gather_full, 1)
                        pe.wait_ge(xe_lo, i * 2 + (e0 + ee + 1))
                        pe.wait_ge(xe_hi, i * 2 + (e0 + ee + 1))

                    def scatter(ee):
                        pe.wait_ge(st_ready, i + (part * PAIRS + 1))
                        pe.wait_ge(y_ready, i * 4 + (2 * e0 + 2 * ee + 2))
                        for t in range(TT):
                            for h in range(2):
                                if t:
                                    pe.wait_ge(scatter_read, i * 8 + (4 * e0 + 1 + 4 * ee + h + 1))
                                nc.tensor.matmul(M[h][:, :], SCAT[:, ee, t * P:(t + 1) * P], YS[:, h * 512:(h + 1) * 512],
                                                 start=True, stop=True).then_inc(scatter_full, 1)

                    used = [0] * RING

                    def weights(n):
                        s = n % RING
                        used[s] += 1
                        pe.wait_ge(slot_loaded[s], i * (16 * PAIR_ITEMS // RING)
                                   + 16 * (before_experts[s] + part * PAIRS * PAIR_ITEMS // RING + used[s]))
                        return s

                    def gate_up(g, n):
                        for which, b, full in ((0, G, gate_full), (1, U, up_full)):
                            s = weights(n + which)
                            if g:
                                pe.wait_ge(up_read if which else gate_read, i * PAIR_SLICES + (s0 + g))
                            for k in range(KT):
                                mm = nc.tensor.matmul(b[:, :], XE[:, g // EF_SLICES, k, :], slot(s)[:, k, :],
                                                      start=(k == 0), stop=(k == KT - 1))
                            mm.then_inc(full, 1)

                    def turn(g):
                        pe.wait_ge(up_read, i * PAIR_SLICES + (s0 + g + 1))
                        if g >= 2:
                            pe.wait_ge(ht_ready, i * PAIR_SLICES + (s0 + g - 1))
                        for j in range(4):
                            mm = nc.tensor.transpose(T[g % 2][:, j * P:(j + 1) * P], HE[:, g % 2, j * P:(j + 1) * P], ident)
                        mm.then_inc(h_turned, 1)

                    def down(g, n):
                        s = weights(n)
                        pe.wait_ge(ht_ready, i * PAIR_SLICES + (s0 + g + 1))
                        for j in range(4):
                            for h in range(2):
                                mm = nc.tensor.matmul(Y[h][:, :], HTE[:, g % 2, j, :],
                                                      slot(s, 4)[:, j, h * 512:(h + 1) * 512],
                                                      start=(g % EF_SLICES == 0 and j == 0),
                                                      stop=(g % EF_SLICES == EF_SLICES - 1 and j == 3))
                        mm.then_inc(down_done, 1)

                    n = 0
                    for g in range(PAIR_SLICES):
                        if g == 0:
                            gather(0)
                        gate_up(g, n)
                        n += 2
                        if g == 5:
                            gather(1)
                        if g == EF_SLICES + 1:
                            scatter(0)
                        if g >= 1:
                            turn(g - 1)
                            down(g - 1, n)
                            n += 1
                    turn(PAIR_SLICES - 1)
                    down(PAIR_SLICES - 1, n)
                    scatter(1)

            after(tables_in, 16)
            for layer in range(DEPTH):
                streams = (0, 1) if layer == 0 else (0,)
                ada_rows()
                after(mod_ready)
                turn_normalized((0, 1))
                modulated_in((0, 1))
                project_in(layer)
                turn_heads(layer)
                turn_qk(layer)
                states()
                retention(layer)
                attention(layer)
                turn_conv(layer)
                turn_mix(layer)
                spread_gate(2, streams)
                project_out(layer)
                turn_normalized(streams)
                modulated_in(streams)
                if layer == 0:
                    dense_ffn()
            routing()
            scatter_matrices(0)
            spread_gate(5, (0,))
            experts(0)
            after(most_ready)
            over = pe.value_load(mosti[0:1, 0:1], min_val=0, max_val=SEQ)
            with pe.If(over > P):
                scatter_matrices(1)
                experts(1)

        @block.sync
        def _(sp):
            sp.dma_start(cload[:, 0, :], io["c"].rearrange("b (p k) -> (b p) k", k=KT)).then_inc(c_in, 16)
            sp.dma_start(cload[:, 1, :], io["c_ctx"].rearrange("(p k) -> p k", k=KT)).then_inc(c_in, 16)
            sp.dma_start(const[:, :], io["shape_tables"]).then_inc(tables_in, 16)
            sp.dma_start(X[:, 0:TT, :], io["x"].rearrange("b (t p) n -> p (b t) n", p=P)).then_inc(x_in, 16)
            sp.dma_start(X[:, TT:NT, :], io["ctx"].rearrange("b (t p) n -> p (b t) n", p=P)).then_inc(x_in, 16)
            holder = [None] * RING
            for n, (src, width, place_, _) in enumerate(items):
                if holder[place_] is not None:
                    sp.wait_ge(*last_use[holder[place_]])
                elif place_ >= MIX_RING:
                    sp.wait_ge(v_full, job[("mixed", 0)])
                holder[place_] = n
                at = place_ * ITEM
                if src == "gate_up":
                    for half, w in enumerate((io["ffn_w_gate"], io["ffn_w_up"])):
                        sp.dma_start(slot(place_)[:, :, half * 256:half * 256 + 256],
                                     cols(w[0], width * 256, (width + 1) * 256)).then_inc(slot_loaded[place_], 16)
                else:
                    k = src.shape[1]
                    sp.dma_start(ring[:, at:at + k * src.shape[2]].rearrange("p (k n) -> p k n", k=k), src)\
                        .then_inc(slot_loaded[place_], 16)

            order = []
            for g in range(PAIR_SLICES):
                order += [("gate", g), ("up", g)] + ([("down", g - 1)] if g else [])
            order.append(("down", PAIR_SLICES - 1))
            full = {"gate": gate_full, "up": up_full, "down": down_done}

            def load_expert(pair, j):
                kind, g = order[j]
                e = pair * 2 + g // EF_SLICES
                s = g % EF_SLICES
                if kind == "down":
                    w = io["moe_w_down"][0]
                    rows = w[bass.ds(e, 1), s * SLICE:(s + 1) * SLICE, :].rearrange("e (k p) n -> p (e k) n", p=P)
                    dst = slot(j % RING, 4)
                else:
                    w = io["moe_w_" + kind][0]
                    rows = w[bass.ds(e, 1), :, s * SLICE:(s + 1) * SLICE].rearrange("e (k p) n -> p (e k) n", p=P)
                    dst = slot(j % RING)
                sp.dma_start(dst, rows).then_inc(slot_loaded[j % RING], 16)

            def wait_used(pair, j, part):
                kind, g = order[j]
                sp.wait_ge(full[kind], pair * PAIR_SLICES + (part * PAIRS * PAIR_SLICES + g + 1))

            def expert_loads(part):
                for j in range(RING):
                    if part == 0:
                        if j < MIX_RING:
                            sp.wait_ge(*last_use[holder[j]])
                        else:
                            sp.wait_ge(v_full, job[("mixed", 1)])
                    else:
                        sp.wait_ge(down_done, PAIRS * PAIR_SLICES)
                    load_expert(0, j)
                with sp.Fori(0, PAIRS - 1) as i:
                    for j in range(PAIR_ITEMS):
                        wait_used(i, j, part)
                        load_expert(i + (j + RING) // PAIR_ITEMS, (j + RING) % PAIR_ITEMS)
                for j in range(PAIR_ITEMS - RING):
                    wait_used(PAIRS - 1, j, part)
                    load_expert(PAIRS - 1, j + RING)

            expert_loads(0)
            sp.wait_ge(most_ready, 1)
            over = sp.value_load(mosti[0:1, 0:1], min_val=0, max_val=SEQ)
            with sp.If(over > P):
                expert_loads(1)
            for t in range(TT):
                sp.wait_ge(out_ready, t + 1)
                sp.dma_start(io["out"][0, t * P:(t + 1) * P, :], X[:, t, :]).then_inc(out_in, 16)
            sp.wait_ge(out_in, 16 * TT)

        @block.scalar
        def _(act):
            after = counter(act)
            step = stepper(act, a_step)
            n_a = [0]

            def take():
                n = n_a[0]
                n_a[0] += 1
                act.wait_ge(a_full, n + 1)
                return AB[n % len(AB)]

            def small_loads(layer):
                for r, name in ((0, "norm1_w"), (KT, "norm2_w"), (2 * KT, "conv_b")):
                    v = io[name][layer].rearrange("(k p) -> k p", p=P)
                    act.dma_start(vrows[r:r + v.shape[0], :], v).then_inc(small_in, 16)
                act.dma_start(convwr[:, :], io["conv_w"][layer]).then_inc(small_in, 16)
                for dst, src in ((qkw[:, 0, :], "q_norm_w"), (qkw[:, 1, :], "k_norm_w"), (sink[:, :], "attn_sink"),
                                 (dlog[:, 0, :], "ret_decay_f"), (dlog[:, 1, :], "ret_decay_b"),
                                 (gnw[:, :], "ret_gn_w"), (lnw[:, :], "conv_ln_w"), (lnb[:, :], "conv_ln_b")):
                    src = io[src][layer]
                    act.dma_start(dst, src.unsqueeze(0).broadcast_to([P, src.shape[0]])).then_inc(small_in, 16)
                b = io["ada_b"][layer]
                act.dma_start(row, b.unsqueeze(0).broadcast_to([2, b.shape[0]])).then_inc(bias_in, 16)

            def squares(tiles):
                for t in tiles:
                    nc.scalar.activation(xn[:, t, :], X[:, t, :], ACT.Square, accum_out=ssq[:, t:t + 1]).then_inc(sq_ready, 1)

            def modulate(which, s):
                for kp in range(KT // 2):
                    b = take()
                    for kk in range(2):
                        k = 2 * kp + kk
                        ins = nc.scalar.activation(hT[:, k, s * SEQ:(s + 1) * SEQ], b[:, kk * SEQ:(kk + 1) * SEQ], ACT.Identity,
                                                   bias=ada[:, 3 * which * KT + k, s:s + 1], scale=scl[:, which, k, s:s + 1])
                    ins.then_inc(a_done, 1)

            def copy_out(out, src):
                nc.scalar.activation(out, src, ACT.Copy).then_inc(a_done, 1)

            def gate_rows(streams):
                for s in streams:
                    for half in range(2):
                        copy_out(GB[:, s, half * 512:(half + 1) * 512], take()[:, :])

            def attention(layer, base):
                its = [(t, r, g) for t in tiles_of(layer) for r in range(4) for g in range(2)]
                for n in range(len(its) + 2):
                    if n < len(its):
                        t, r, g = its[n]
                        head, turn = g * 4 + r, (n // 8) % 2
                        k0 = 0 if t < TT else SEQ
                        after(negm_ready)
                        nc.scalar.activation(SC[:, n % 4, k0:], SC[:, n % 4, k0:], ACT.Exp, bias=negm[:, turn, head:head + 1],
                                             scale=HEAD_DIM ** -0.5, accum_out=rsum[:, turn, head:head + 1]).then_inc(exp_ready, 1)
                        if n % 8 == 7:
                            after(sarg_ready)
                            nc.scalar.activation(esink[:, turn, :], esink[:, turn, :], ACT.Exp).then_inc(esink_ready, 1)
                    if n >= 2:
                        m = n - 2
                        k0 = 0 if its[m][0] < TT else SEQ
                        b = take()
                        if m >= 2:
                            act.wait_ge(att_done, base + m - 1)
                        copy_out(PT[:, m % 2, k0:], b[:, k0:])

            def experts(part):
                G, T, M = bank[0], bank[4:6], bank[6]
                s0, e0 = part * N_EXPERTS * EF_SLICES, part * N_EXPERTS
                with act.Fori(0, PAIRS) as i:
                    def gathered(ee):
                        act.wait_ge(gather_full, i * 4 + (2 * (e0 + ee) + 1))
                        for k in range(4):
                            ins = nc.scalar.activation(XE[:, ee, k, :], M[:, k * P:(k + 1) * P], ACT.Identity,
                                                       bias=ada[:, 3 * KT + k, 0:1], scale=scl[:, 1, k, 0:1])
                        ins.then_inc(xe_lo, 1)

                    def turned(g):
                        act.wait_ge(h_turned, i * PAIR_SLICES + (s0 + g + 1))
                        if g >= 2:
                            act.wait_ge(down_done, i * PAIR_SLICES + (s0 + g - 1))
                        nc.scalar.activation(HTE[:, g % 2, :, :].rearrange("p j n -> p (j n)"), T[g % 2][:, :], ACT.Copy)\
                            .then_inc(ht_ready, 1)

                    for g in range(PAIR_SLICES):
                        if g == 0:
                            gathered(0)
                        act.wait_ge(gate_full, i * PAIR_SLICES + (s0 + g + 1))
                        if g >= 2:
                            act.wait_ge(up_read, i * PAIR_SLICES + (s0 + g - 1))
                        nc.scalar.activation(SGE[:, g % 2, :], G[:, :], ACT.Silu).then_inc(gate_read, 1)
                        if g == 5:
                            gathered(1)
                        if g >= 1:
                            turned(g - 1)
                    turned(PAIR_SLICES - 1)

            act.dma_start(routw[:, :, :], io["router_w"][0].rearrange("(k p) e -> p k e", p=P)).then_inc(router_in, 16)
            att_base = 0
            for layer in range(DEPTH):
                tiles = tiles_of(layer)
                nt = len(tiles)
                if layer == 0:
                    small_loads(0)
                    act.wait_ge(c_in, 32)
                    nc.scalar.activation(cond[:, :, :], cload[:, :, :].rearrange("p s k -> p k s"), ACT.Silu).then_inc(cond_ready, 1)
                    act.wait_ge(x_in, 32)
                else:
                    after(x_ready)
                    small_loads(1)
                squares(range(NT))
                after(dneg_ready)
                step(nc.scalar.activation(dln[:, :, :], dneg[:, :, :], ACT.Exp))
                nc.scalar.activation(dln[:, :, :], dln[:, :, :], ACT.Ln, bias=1.0).then_inc(dln_ready, 1)
                after(mod_ready)
                modulate(0, 1)
                after(dexp_in)
                nc.scalar.activation(decay[:, :, :], decay[:, :, :], ACT.Exp).then_inc(dexp_out, 1)
                nc.scalar.activation(dtok[:, :, :, :, :], dtok[:, :, :, :, :], ACT.Exp).then_inc(dexp_out, 1)
                for a, b_ in IN_SLICES[:-1]:
                    for t in (range(NT) if layer == 0 or b_ <= C_Q else range(TT)):
                        if t % 2:
                            copy_out(proj[:, t, a:b_], take()[:, 0:b_ - a])
                ncol = SEQ * (2 if layer == 0 else 1)
                for ct in range(2):
                    nc.scalar.activation(SC[:, ct, 0:ncol], take()[:, 0:ncol], ACT.Sigmoid).then_inc(a_done, 1)
                act.wait_ge(v_done, job[("in", layer, C_RQ, tiles[-1] - 1)] + 1)
                act.wait_ge(a_done, job[("in", layer, C_RQ, tiles[-1])] + 1)
                gates = proj[:, 0:nt, C_RG:C_CONV]
                nc.scalar.activation(gates, gates, ACT.Silu).then_inc(rg_ready, 1)
                for t in tiles:
                    copy_out(AQT[:, :, t, :], take()[:, :].rearrange("p (r n) -> p r n", r=4))
                for s in ((0, 1) if layer == 0 else (0,)):
                    for t in range(TT):
                        copy_out(RO[:, s * TT + t, :], take()[:, 0:256])
                attention(layer, att_base + NT)
                att_base += NT + 8 * nt
                after(ln_ready)
                nc.scalar.activation(gates, CV[:, 0:nt, :], ACT.Silu).then_inc(act_mix, 1)
                for t in tiles:
                    copy_out(mixT[:, 4:8, t * P:(t + 1) * P], take()[:, :].rearrange("p (k n) -> p k n", k=4))
                gate_rows((0, 1) if layer == 0 else (0,))
                after(x_ready)
                squares(tiles)
                if layer == 0:
                    modulate(1, 1)
                    for f in range(FF_TILES):
                        b = take()
                        if f >= 2:
                            act.wait_ge(v_done, job[("up", f - 2)] + 1)
                        nc.scalar.activation(SG[:, f % 2, :], b[:, :], ACT.Silu).then_inc(a_done, 1)
                    gate_rows((0, 1))
            after(lexp_in)
            nc.scalar.activation(best[:, 3, :], best[:, 2, :], ACT.Exp).then_inc(lexp_out, 1)
            gate_rows((0,))
            experts(0)
            after(most_ready)
            over = act.value_load(mosti[0:1, 0:1], min_val=0, max_val=SEQ)
            with act.If(over > P):
                experts(1)

        @block.gpsimd
        def _(pool):
            after = counter(pool)
            step = stepper(pool, p_step)

            def rsqrt(out, mid, src, scale):
                step(nc.gpsimd.tensor_scalar(mid, src, scale, EPS, ALU.mult, ALU.add))
                return nc.gpsimd.tensor_tensor(out, mid, nhalf[:, 0:out.shape[1]], ALU.pow)

            step(nc.gpsimd.memset(nhalf[:, :], -0.5))
            for layer in range(DEPTH):
                nt = len(tiles_of(layer))
                if layer:
                    after(x_ready)
                nc.gpsimd.memset(CB, 0.0).then_inc(pad_ready, 1)
                after(sq_ready, NT)
                rsqrt(rstd[:, :], lnt[:, 0:NT], ssq[:, :], 1.0 / D_MODEL).then_inc(rstd_ready, 1)
                for t in range(NT):
                    lo = 0 if t in tiles_of(layer) else 8
                    after(qss_ready)
                    rsqrt(qrs[:, t, lo:], qst[:, t, lo:], qss[:, t, lo:], 1.0 / HEAD_DIM).then_inc(qrs_ready, 1)
                after(dexp_out, 2)
                pool.wait_ge(v_done, job[("in", layer, 384, 2)] + 1)
                pool.wait_ge(a_done, job[("in", layer, 384, 3)] + 1)
                for t in range(TT):
                    val = proj[:, TT + t, C_RV:C_RV + 256].rearrange("p (h e) -> p h e", h=RET_HEADS)
                    for d in range(2):
                        ins = nc.gpsimd.tensor_tensor(VW[:, t, :, d, :], val,
                                                      dtok[:, 0, t, :, d].unsqueeze(2).broadcast_to([P, RET_HEADS, HEAD_DIM]),
                                                      ALU.mult)
                    ins.then_inc(vw_ready, 1)
                after(ro_var)
                rsqrt(lnr[:, 0:4 * nt], lnt[:, 0:4 * nt], lnv[:, 0:4 * nt], 1.0 / HEAD_DIM).then_inc(ro_rstd, 1)
                after(cv_var)
                rsqrt(lnr[:, 0:nt], lnt[:, 0:nt], bag[:, 0:nt, 1], 1.0).then_inc(cv_rstd, 1)
                after(x_ready)
                after(sq_ready, nt)
                rsqrt(rstd[:, 0:nt], lnt[:, 0:nt], ssq[:, 0:nt], 1.0 / D_MODEL).then_inc(rstd_ready, 1)

        @block.vector
        def _(dve):
            after = counter(dve)
            step = stepper(dve, v_step)
            n_v = [0]
            x_count = [0]

            def take():
                n = n_v[0]
                n_v[0] += 1
                dve.wait_ge(v_full, n + 1)
                return VB[n % len(VB)]

            def emptied():
                dve.wait_ge(v_done, n_v[0])

            def tt(out, a, b, op):
                return nc.vector.tensor_tensor(out, a, b, op)

            def copy_out(out, src):
                nc.vector.tensor_copy(out, src).then_inc(v_done, 1)

            def per_group(v, width):
                return v.unsqueeze(2).broadcast_to([P, v.shape[1], width])

            def ada_columns():
                after(bias_in, 16)
                for s in range(12):
                    part = row[:, s * SLICE:(s + 1) * SLICE]
                    tt(part, take()[0:2, :], part, ALU.add).then_inc(v_done, 1)
                b = take()
                nc.vector.tensor_copy(vcols[:, :], b[:, 96:96 + 2 * KT + 2])
                copy_out(ada[:, :, :], b[:, 0:96].rearrange("p (c s) -> p c s", s=2))
                emptied()
                for which in range(2):
                    c = (1 + 3 * which) * KT
                    ins = nc.vector.scalar_tensor_tensor(scl[:, which, :, :], ada[:, c:c + KT, :], 1.0,
                                                         vcols[:, which * KT:(which + 1) * KT].unsqueeze(2).broadcast_to([P, KT, 2]), ALU.add, ALU.mult)
                ins.then_inc(mod_ready, 1)

            def normalize(which, tiles):
                after(rstd_ready)
                for t in tiles:
                    nc.vector.tensor_scalar(xn[:, t, :], X[:, t, :], rstd[:, t:t + 1], None, ALU.mult).then_inc(xn_ready, 1)
                for kp in range(KT // 2):
                    b = take()
                    for kk in range(2):
                        k = 2 * kp + kk
                        ins = nc.vector.tensor_scalar(hT[:, k, 0:SEQ], b[:, kk * SEQ:(kk + 1) * SEQ], scl[:, which, k, 0:1],
                                                      ada[:, 3 * which * KT + k, 0:1], ALU.mult, ALU.add)
                    ins.then_inc(v_done, 1)

            def decay_arguments():
                after(dln_ready)
                step(tt(dneg[:, :, :], dmin[:, :, :], dln[:, :, :], ALU.subtract))
                for h in range(RET_HEADS):
                    ins = nc.vector.tensor_scalar(decay[:, h, :], ahead, dneg[:, h, 0:1], None, ALU.mult)
                step(ins)
                for h in range(RET_HEADS):
                    nc.vector.scalar_tensor_tensor(decay[:, h, :], behind, dneg[:, h, 1:2], decay[:, h, :], ALU.mult, ALU.add)
                for h in range(RET_HEADS):
                    ins = tt(dtok[:, :, :, h, :].rearrange("p w t d -> p (w t) d"), expo,
                             dneg[:, h, :].unsqueeze(1).broadcast_to([P, 4, 2]), ALU.mult)
                ins.then_inc(dexp_in, 1)

            def head_squares(layer, t):
                if t % 2:
                    dve.wait_ge(a_done, job[("in", layer, 0, t)] + 1)
                lo = 8
                if t in tiles_of(layer):
                    lo = 0
                    q = proj[:, t, C_Q:C_RQ].rearrange("p (g r d) -> p g r d", g=2, d=HEAD_DIM)
                    tt(TMP[:, 0:512].rearrange("p (r g d) -> p g r d", g=2, d=HEAD_DIM), q, q, ALU.mult)
                k = proj[:, t, C_K:C_V]
                step(tt(TMP[:, 512:640], k, k, ALU.mult))
                nc.vector.tensor_reduce(qss[:, t, lo:], TMP[:, 64 * lo:640].rearrange("p (h d) -> p h d", d=HEAD_DIM),
                                        AX.X, ALU.add).then_inc(qss_ready, 1)

            def head_norm(layer, t):
                after(qrs_ready)
                if t in tiles_of(layer):
                    for g in range(2):
                        tt(QK[:, t, g:8:2, :], proj[:, t, C_Q + 256 * g:C_Q + 256 * g + 256].rearrange("p (r d) -> p r d", d=HEAD_DIM),
                           per_group(qrs[:, t, g:8:2], HEAD_DIM), ALU.mult)
                step(tt(QK[:, t, 8:10, :], proj[:, t, C_K:C_V].rearrange("p (h d) -> p h d", d=HEAD_DIM),
                        per_group(qrs[:, t, 8:10], HEAD_DIM), ALU.mult))
                if t in tiles_of(layer):
                    tt(QK[:, t, 0:8, :], QK[:, t, 0:8, :], qkw[:, 0, :].unsqueeze(1).broadcast_to([P, 8, HEAD_DIM]), ALU.mult)
                last = tt(QK[:, t, 8:10, :], QK[:, t, 8:10, :], qkw[:, 1, :].unsqueeze(1).broadcast_to([P, 2, HEAD_DIM]), ALU.mult)
                if t < TT:
                    step(last)
                    a_ = TMP[:, 0:640].rearrange("p (h d) -> p h d", d=HEAD_DIM)
                    b_ = TMP[:, 640:1280].rearrange("p (h a f) -> p h a f", a=2, f=32)
                    tt(a_, QK[:, t, :, :], cos64[:, t, :].unsqueeze(1).broadcast_to([P, 10, HEAD_DIM]), ALU.mult)
                    q4 = QK[:, t, :, :].rearrange("p h (a f) -> p h a f", a=2)
                    for half in range(2):
                        ins = tt(b_[:, :, :, 16 * half:16 * half + 16], q4[:, :, :, 16 - 16 * half:32 - 16 * half],
                                 sin64[:, t, :, half, :].unsqueeze(1).broadcast_to([P, 10, 2, 16]), ALU.mult)
                    step(ins)
                    last = tt(QK[:, t, :, :], a_, TMP[:, 640:1280].rearrange("p (h d) -> p h d", d=HEAD_DIM), ALU.add)
                last.then_inc(qk_ready, 1)
                dve.wait_ge(qk_ready, NT * layer + t + 1)

            def projections(layer):
                for n, (a, b_) in enumerate(IN_SLICES[:-1]):
                    for t in (range(NT) if layer == 0 or b_ <= C_Q else range(TT)):
                        if t % 2 == 0:
                            copy_out(proj[:, t, a:b_], take()[:, 0:b_ - a])
                    if n == 1:
                        emptied()
                        for t in range(TT):
                            head_squares(layer, t)
                            head_norm(layer, t)
                    if n == 2:
                        emptied()
                        for t in range(TT, NT):
                            head_squares(layer, t)
                            head_norm(layer, t)
                after(pad_ready)
                ns = 2 if layer == 0 else 1
                for ct in range(2):
                    b = take()
                    dve.wait_ge(a_done, job[("conv_gate", layer, ct)] + 1)
                    tt(CB[:, ct, 0:ns, CONV_WIDTH // 2:CONV_WIDTH // 2 + SEQ], b[:, 0:ns * SEQ].rearrange("p (s n) -> p s n", s=ns),
                       SC[:, ct, 0:ns * SEQ].rearrange("p (s n) -> p s n", s=ns), ALU.mult).then_inc(v_done, 1)

            def retention(layer, base):
                tiles = tiles_of(layer)
                copy_out(convw[:, :, :], take()[:, 0:64].rearrange("p (c k) -> p c k", c=2)[:, :, 0:CONV_WIDTH])
                for t in tiles:
                    copy_out(RT[:, :, t, :], take()[:, :].rearrange("p (b n) -> p b n", b=4))
                after(dexp_out, 2)
                nc.vector.tensor_scalar(dec[:, :], dec[:, :], HEAD_DIM ** -0.5, None, ALU.mult)
                read = dtok[:, 1, :, :, :]
                step(nc.vector.tensor_scalar(read, read, HEAD_DIM ** -0.5, None, ALU.mult))
                dve.wait_ge(att_done, base)
                nc.vector.tensor_copy(AKT, OB[:, :]).then_inc(att_read, 1)
                b = take()
                step(nc.vector.memset(ST, 0.0))
                nc.vector.tensor_copy(ST[0:64, :, 0:P], b[0:64, :].rearrange("p (c n) -> p c n", c=2)[:, :, 0:P])
                copy_out(ST[64:128, :, P:2 * P], b[64:128, :].rearrange("p (c n) -> p c n", c=2)[:, :, P:2 * P])
                for s in ((0, 1) if layer == 0 else (0,)):
                    if s:
                        dve.wait_ge(a_full, job[("inner", layer, 0)] + 2)
                    for h in range(RET_HEADS):
                        tt(AD[:, h, :], take()[:, :], decay[:, h, :], ALU.mult).then_inc(v_done, 1)
                dve.wait_ge(a_done, job[("inner", layer, 0)] + 2)
                cross = RW.rearrange("p t c -> p (t c)").rearrange("p (t g n) -> p t g n", t=TT, g=8)
                for t in range(TT):
                    tt(cross[:, t, :, :], take()[:, :].rearrange("p (g n) -> p g n", g=8),
                       per_group(dtok[:, 1, t, :, :].rearrange("p h d -> p (h d)"), HEAD_DIM), ALU.mult).then_inc(v_done, 1)
                emptied()
                for d in range(2):
                    for t in range(TT):
                        out = RO[:, t, :].rearrange("p (h n) -> p h n", h=RET_HEADS)
                        ins = tt(out, out, cross[:, t, d:8:2, :], ALU.add)
                    step(ins)

            def readout(layer):
                nt = len(tiles_of(layer))
                if layer == 0:
                    dve.wait_ge(a_done, job[("inner", layer, 1)] + 2)
                o = RO[:, 0:nt, :].rearrange("p t (h n) -> p (t h) n", h=RET_HEADS)
                w = RW[:, 0:nt, :].rearrange("p t (h n) -> p (t h) n", h=RET_HEADS)
                g = 4 * nt
                step(nc.vector.tensor_reduce(lnm[:, 0:g], o, AX.X, ALU.add))
                step(nc.vector.tensor_scalar(lnm[:, 0:g], lnm[:, 0:g], -1.0 / HEAD_DIM, None, ALU.mult))
                step(tt(o, o, per_group(lnm[:, 0:g], HEAD_DIM), ALU.add))
                step(tt(w, o, o, ALU.mult))
                nc.vector.tensor_reduce(lnv[:, 0:g], w, AX.X, ALU.add).then_inc(ro_var, 1)
                after(ro_rstd)
                step(tt(o, o, per_group(lnr[:, 0:g], HEAD_DIM), ALU.mult))
                r = RO[:, 0:nt, :]
                step(tt(r, r, gnw[:, :].unsqueeze(1).broadcast_to([P, nt, 256]), ALU.mult))
                after(rg_ready)
                step(tt(proj[:, 0:nt, C_RQ:C_RG], r, proj[:, 0:nt, C_RG:C_CONV], ALU.mult))

            def attention(layer, base):
                its = [(t, r, g) for t in tiles_of(layer) for r in range(4) for g in range(2)]
                ns = 2 if layer == 0 else 1
                per = -(-TAPS // len(its))

                def tap(c):
                    ct, k = c % 2, c // 2
                    src = CB[:, ct, 0:ns, k:k + SEQ]
                    acc = CA[:, ct, 0:ns, :]
                    if k == 0:
                        ins = nc.vector.tensor_scalar(acc, src, convw[:, ct, 0:1], vcols[:, 2 * KT + ct:2 * KT + ct + 1], ALU.mult, ALU.add)
                    else:
                        dve.wait_ge(tap_done, tap_base + c - 1)
                        ins = nc.vector.scalar_tensor_tensor(acc, src, convw[:, ct, k:k + 1], acc, ALU.mult, ALU.add)
                    ins.then_inc(tap_done, 1)

                tap_base = layer * TAPS
                for n in range(len(its) + 3):
                    if n < len(its):
                        t, r, g = its[n]
                        head, turn = g * 4 + r, (n // 8) % 2
                        k0 = 0 if t < TT else SEQ
                        b = take()
                        if n >= 4:
                            dve.wait_ge(a_full, job[("probs", layer, n - 4)] + 1)
                        nc.vector.tensor_tensor_reduce(SC[:, n % 4, k0:], b[:, k0:], mask[:, t % TT, k0:], 1.0, 3 * BIG_NEG,
                                                       ALU.add, ALU.max, mx[:, turn, head:head + 1]).then_inc(v_done, 1)
                        emptied()
                        nc.vector.tensor_scalar(negm[:, turn, head:head + 1], mx[:, turn, head:head + 1], -(HEAD_DIM ** -0.5),
                                                nsink[:, head:head + 1], ALU.mult, ALU.min).then_inc(negm_ready, 1)
                        if n % 8 == 7:
                            dve.wait_ge(negm_ready, layer_negm + n + 1)
                            tt(esink[:, turn, :], negm[:, turn, :], sink[:, :], ALU.add).then_inc(sarg_ready, 1)
                        for c in range(n * per, min((n + 1) * per, TAPS)):
                            tap(c)
                    if n == 3:
                        readout(layer)
                    if n >= 10 and (n - 10) % 8 == 0:
                        tile = (n - 10) // 8
                        turn = tile % 2
                        after(esink_ready)
                        step(tt(rsum[:, turn, :], rsum[:, turn, :], esink[:, turn, :], ALU.add))
                        step(nc.vector.reciprocal(rsum[:, turn, :], rsum[:, turn, :]))
                        dve.wait_ge(att_done, base + 8 * (tile + 1))
                        tt(proj[:, tile, C_Q:C_RQ].rearrange("p (h d) -> p h d", d=HEAD_DIM), OB[:, :].rearrange("p (h d) -> p h d", d=HEAD_DIM),
                           per_group(rsum[:, turn, :], HEAD_DIM), ALU.mult).then_inc(att_read, 1)

            def conv_norm(layer):
                nt = len(tiles_of(layer))
                for t in range(nt):
                    copy_out(CV[:, t, :], take()[:, 0:256])
                emptied()
                for t in range(nt):
                    ins = nc.vector.bn_stats(bst[:, t, :], CV[:, t, :])
                step(ins)
                for t in range(nt):
                    ins = nc.vector.bn_aggr(bag[:, t, :], bst[:, t, :])
                ins.then_inc(cv_var, 1)
                after(cv_rstd)
                for t in range(nt):
                    ins = nc.vector.tensor_scalar(CV[:, t, :], CV[:, t, :], bag[:, t, 0:1], lnr[:, t:t + 1], ALU.subtract, ALU.mult)
                step(ins)
                c = CV[:, 0:nt, :]
                step(tt(c, c, lnw[:, :].unsqueeze(1).broadcast_to([P, nt, 256]), ALU.mult))
                tt(c, c, lnb[:, :].unsqueeze(1).broadcast_to([P, nt, 256]), ALU.add).then_inc(ln_ready, 1)

            def add_gated(half, t, last):
                s = t // TT
                y = YG[:, t % 2, :]
                x = X[:, t, half * 512:(half + 1) * 512]
                tt(y, take()[:, :], GB[:, s, half * 512:(half + 1) * 512], ALU.mult).then_inc(v_done, 1)
                emptied()
                ins = tt(x, x, y, ALU.add)
                if last:
                    ins.then_inc(x_ready, 1)
                    x_count[0] += 1
                    dve.wait_ge(x_ready, x_count[0])

            def route():
                L, first, second, chosen = top[:, 1, :, :], top[:, 2, :, :], top[:, 3, :, :], top[:, 0, :, :]
                tmp, comb = top[:, 4, :, :], top[:, 5, :, :]
                idx = table("experts").unsqueeze(1).broadcast_to([P, TT, N_EXPERTS])
                copy_out(L, take()[:, 0:16].rearrange("p (t e) -> p t e", t=TT))
                emptied()

                def pick(value, mask_, at):
                    step(nc.vector.tensor_reduce(value, L, AX.X, ALU.max))
                    step(tt(tmp, L, per_group(value, N_EXPERTS), ALU.is_equal))
                    step(nc.vector.tensor_scalar(tmp, tmp, -64.0, 64.0, ALU.mult, ALU.add))
                    step(tt(tmp, tmp, idx, ALU.add))
                    step(nc.vector.tensor_reduce(at, tmp, AX.X, ALU.min))
                    return tt(mask_, idx, per_group(at, N_EXPERTS), ALU.is_equal)

                step(pick(best[:, 0, :], first, best[:, 4, :]))
                step(nc.vector.scalar_tensor_tensor(L, first, BIG_NEG, L, ALU.mult, ALU.add))
                step(pick(best[:, 1, :], second, best[:, 5, :]))
                tt(chosen, first, second, ALU.add).then_inc(mask_ready, 1)
                tt(best[:, 2, :], best[:, 1, :], best[:, 0, :], ALU.subtract).then_inc(lexp_in, 1)
                after(lexp_out)
                step(nc.vector.tensor_scalar(best[:, 6, :], best[:, 3, :], 1.0, None, ALU.add))
                step(nc.vector.reciprocal(best[:, 6, :], best[:, 6, :]))
                step(tt(best[:, 7, :], best[:, 6, :], best[:, 3, :], ALU.mult))
                step(tt(tmp, first, per_group(best[:, 6, :], N_EXPERTS), ALU.mult))
                step(tt(comb, second, per_group(best[:, 7, :], N_EXPERTS), ALU.mult))
                step(tt(comb, comb, tmp, ALU.add))
                b = take()
                nc.vector.tensor_reduce(most[:, 0:1], b[:, 16:24], AX.X, ALU.max)
                copy_out(top[:, 6, :, :], b[:, 0:16].rearrange("p (t e) -> p t e", t=TT))
                emptied()
                nc.vector.tensor_copy(mosti[:, :], most[:, 0:1]).then_inc(most_ready, 1)

            def place_tokens(part):
                rank, chosen, comb = top[:, 6, :, :], top[:, 0, :, :], top[:, 5, :, :]
                if part:
                    nc.vector.tensor_scalar(rank, rank, -float(P), None, ALU.add).then_inc(rank_moved, 1)
                    dve.wait_ge(rank_moved, 1)

                def weighted(e):
                    for i in range(2):
                        for t in range(TT):
                            ins = nc.vector.tensor_scalar(XE[:, (e // 2) % 2, i * TT + t, :], table("slots"),
                                                          rank[:, t, e + i:e + i + 1], comb[:, t, e + i:e + i + 1],
                                                          ALU.is_equal, ALU.mult)
                    ins.then_inc(scat_in, 1)

                weighted(0)
                for e in range(0, N_EXPERTS, 2):
                    if e + 2 < N_EXPERTS:
                        weighted(e + 2)
                    for i in range(2):
                        for t in range(TT):
                            nc.vector.tensor_scalar(PA[:, t, e + i, :], table("slots"), rank[:, t, e + i:e + i + 1],
                                                    chosen[:, t, e + i:e + i + 1], ALU.is_equal, ALU.mult)
                    copy_out(SA[:, e:e + 2, :], take()[:, :].rearrange("p (e n) -> p e n", e=2))
                emptied()

            def experts(part):
                U, Y, M = bank[1], bank[2:4], bank[6:8]
                s0, e0 = part * N_EXPERTS * EF_SLICES, part * N_EXPERTS
                with dve.Fori(0, PAIRS) as i:
                    def gathered(ee):
                        dve.wait_ge(gather_full, i * 4 + (2 * (e0 + ee) + 2))
                        for k in range(4, KT):
                            ins = nc.vector.tensor_scalar(XE[:, ee, k, :], M[1][:, (k - 4) * P:(k - 3) * P], scl[:, 1, k, 0:1],
                                                          ada[:, 3 * KT + k, 0:1], ALU.mult, ALU.add)
                        ins.then_inc(xe_hi, 1)

                    def expert_out(ee):
                        dve.wait_ge(down_done, i * PAIR_SLICES + (s0 + EF_SLICES * (ee + 1)))
                        for h in range(2):
                            nc.vector.tensor_copy(YS[:, h * 512:(h + 1) * 512], Y[h][:, :]).then_inc(y_ready, 1)

                    def add_scattered(ee):
                        for t in range(TT):
                            for h in range(2):
                                n = 4 * (e0 + ee) + 2 * t + h
                                dve.wait_ge(scatter_full, i * 8 + (n + 1))
                                acc = ACC[:, t, h * 512:(h + 1) * 512]
                                tt(acc, M[h][:, :], acc, ALU.add).then_inc(scatter_read, 1)

                    for ee in range(2):
                        ins = nc.vector.tensor_copy(SCAT[:, ee, :], SA[:, bass.ds(i * 2 + ee, 1), :].rearrange("p e n -> p (e n)"))
                    ins.then_inc(st_ready, 1)
                    for g in range(PAIR_SLICES):
                        if g == 0:
                            gathered(0)
                        dve.wait_ge(up_full, i * PAIR_SLICES + (s0 + g + 1))
                        dve.wait_ge(gate_read, i * PAIR_SLICES + (s0 + g + 1))
                        if g >= 2:
                            dve.wait_ge(h_turned, i * PAIR_SLICES + (s0 + g - 1))
                        tt(HE[:, g % 2, :], U[:, :], SGE[:, g % 2, :], ALU.mult).then_inc(up_read, 1)
                        if g == 5:
                            gathered(1)
                        if g == EF_SLICES:
                            expert_out(0)
                        if g == EF_SLICES + 1:
                            add_scattered(0)
                    expert_out(1)
                    add_scattered(1)

            dve.wait_ge(tables_in, 16)
            att_base = 0
            for layer in range(DEPTH):
                tiles = tiles_of(layer)
                layer_negm = 0 if layer == 0 else 8 * NT
                after(small_in, 16 * N_SMALL)
                nc.vector.tensor_scalar(nsink[:, :], sink[:, :], -1.0, None, ALU.mult)
                logit = dlog[:, :, :].rearrange("p d h -> p h d")
                nc.vector.tensor_scalar(dmin[:, :, :], logit, 0.0, None, ALU.min)
                nc.vector.scalar_tensor_tensor(dneg[:, :, :], logit, -1.0, logit, ALU.mult, ALU.min)\
                    .then_inc(dneg_ready, 1)
                ada_columns()
                normalize(0, range(NT))
                decay_arguments()
                projections(layer)
                retention(layer, att_base + NT)
                attention(layer, att_base + NT)
                att_base += NT + 8 * len(tiles)
                conv_norm(layer)
                for t in tiles:
                    copy_out(mixT[:, 0:4, t * P:(t + 1) * P], take()[:, :].rearrange("p (k n) -> p k n", k=4))
                for half in range(2):
                    for t in tiles:
                        add_gated(half, t, half == 1 and t == tiles[-1])
                normalize(1, tiles)
                if layer == 0:
                    for f in range(FF_TILES):
                        b = take()
                        dve.wait_ge(a_done, job[("gate", f)] + 1)
                        tt(HFF[:, f, :], b[:, :], SG[:, f % 2, :], ALU.mult).then_inc(v_done, 1)
                    for half in range(2):
                        for t in tiles:
                            add_gated(half, t, half == 1 and t == tiles[-1])
            route()
            place_tokens(0)
            nc.vector.memset(ACC, 0.0).then_inc(scatter_read, 1)
            experts(0)
            dve.wait_ge(most_ready, 1)
            over = dve.value_load(mosti[0:1, 0:1], min_val=0, max_val=SEQ)
            with dve.If(over > P):
                place_tokens(1)
                experts(1)
            for t in range(TT):
                step(tt(ACC[:, t, :], ACC[:, t, :], GB[:, 0, :], ALU.mult))
                tt(X[:, t, :], X[:, t, :], ACC[:, t, :], ALU.add).then_inc(out_ready, 1)


_INS = ['x', 'c', 'ctx', 'c_ctx', 'ada_w', 'ada_b', 'norm1_w', 'norm2_w', 'w_in', 'w_out', 'q_norm_w', 'k_norm_w',
        'attn_sink', 'ret_decay_f', 'ret_decay_b', 'ret_gn_w', 'conv_w', 'conv_b', 'conv_ln_w', 'conv_ln_b',
        'ffn_w_gate', 'ffn_w_up', 'ffn_w_down', 'router_w', 'moe_w_gate', 'moe_w_up', 'moe_w_down']


def kernel(**inputs):
    import numpy as _np
    import concourse.bacc as _bacc
    from concourse import mybir as _mybir
    from concourse.bass_utils import run_bass_kernel_spmd as _run

    nc = _bacc.Bacc("TRN2", target_bir_lowering=False, num_devices=1)
    arrays, io = {}, {}
    tables, place = shape_constants()
    for name in _INS + ['shape_tables']:
        a = tables if name == 'shape_tables' else _np.ascontiguousarray(inputs[name])
        arrays[f"in_{name}_dram"] = a
        io[name] = nc.dram_tensor(f"in_{name}_dram", a.shape, _mybir.dt.from_np(a.dtype), kind="ExternalInput").ap()
    io["out"] = nc.dram_tensor("out_0_dram", (1, SEQ, D_MODEL), _mybir.dt.float32, kind="ExternalOutput").ap()
    build(nc, io, place)
    r = _run(nc, [arrays], core_ids=[0])
    return r.results[0]["out_0_dram"]
```

```python
from contextlib import ExitStack

import concourse.bass as bass
from concourse import mybir

ALU = mybir.AluOpType
ACT = mybir.ActivationFunctionType
AX = mybir.AxisListType
F32 = mybir.dt.float32
F32R = mybir.dt.float32r
I32 = mybir.dt.int32

P = 128
D_MODEL, SEQ, CTX_LEN, DEPTH = 1024, 256, 256, 2
HEAD_DIM, Q_HEADS, KV_HEADS, RET_HEADS = 64, 8, 2, 4
CONV_CH, CONV_WIDTH = 256, 31
D_FF, N_EXPERTS, D_FF_EXPERT = 2816, 8, 3584
GRID_W, ROPE_BASE, WINDOW = 64, 10000.0, 128
EPS = 1e-6

KT = D_MODEL // P
TT = SEQ // P
NT = 2 * TT
C_K, C_V, C_RK, C_RV, C_Q, C_RQ, C_RG, C_CONV, IN_COLS = 0, 128, 256, 512, 768, 1280, 1536, 1792, 2304
PCOLS = C_CONV
SLICE = 512
ITEM = KT * SLICE // 2
RAW = 4
PARTS = 4
FF_TILES = D_FF // P
EF_SLICES = D_FF_EXPERT // SLICE
PAIRS = N_EXPERTS // 2
PAIR_SLICES = 2 * EF_SLICES
PAIR_ITEMS = 6 * PAIR_SLICES
HALF_FF = FF_TILES // 2
CREDIT = 2
TAPS = 2 * CONV_WIDTH
BIG_NEG = -1.0e30
N_SMALL = 12


def shape_constants():
    import numpy as np

    part = np.arange(P)
    out = {}
    out["identity"] = np.eye(P)
    mask = np.zeros((P, TT, 2 * SEQ))
    for t in range(TT):
        far = np.abs((t * P + part)[:, None] - np.arange(SEQ)[None, :]) > WINDOW
        mask[:, t, :SEQ][far] = BIG_NEG
    out["mask"] = mask.reshape(P, -1)
    freqs = (ROPE_BASE ** (-np.arange(16, dtype=np.float32) / np.float32(16))).astype(np.float32)
    pos = np.arange(SEQ)
    ang = np.stack([(pos // GRID_W).astype(np.float32)[:, None] * freqs,
                    (pos % GRID_W).astype(np.float32)[:, None] * freqs], axis=1)
    cos, sin = np.cos(ang), np.sin(ang)
    c64 = np.stack([cos, cos], axis=2).reshape(TT, P, 64)
    s64 = np.stack([-sin, sin], axis=2).reshape(TT, P, 64)
    out["cos"] = c64.transpose(1, 0, 2).reshape(P, -1)
    out["sin"] = s64.transpose(1, 0, 2).reshape(P, -1)
    j = (np.arange(TT) * P)[None, :, None] + part[:, None, None]
    i = np.arange(SEQ)[None, None, :]
    out["ahead"] = np.maximum(i - j, 0).reshape(P, -1)
    out["behind"] = np.maximum(j - i, 0).reshape(P, -1)
    tok = (np.arange(TT) * P)[None, :] + part[:, None]
    e = np.stack([np.stack([SEQ - 1 - tok, tok], -1), np.stack([tok + 1, SEQ - tok], -1)], 1)
    out["exponents"] = e.reshape(P, -1)
    out["before"] = (part[:, None] < part[None, :]) * 1.0
    out["ones"] = np.ones((P, P))
    fold = np.zeros((P, 2))
    for r in range(4):
        fold[r, r % 2] = 1.0
    out["fold"] = fold
    out["slots"] = np.tile(np.arange(P), (P, 1))
    out["experts"] = np.tile(np.arange(N_EXPERTS), (P, 1))
    out["mask"] = out.pop("mask")
    at, places = 0, {}
    for name, a in out.items():
        places[name] = (at, a.shape[1])
        at += a.shape[1]
    return np.concatenate([a.astype(np.float32) for a in out.values()], axis=1), places


def build(nc, io, place):
    ctx = ExitStack()
    with ctx:
        def sb(name, shape, dt=F32):
            return ctx.enter_context(nc.sbuf_tensor(name, shape, dt))

        def sem(name):
            return ctx.enter_context(nc.semaphore(name))

        def phase(*tensors):
            guards = [nc.sbuf_tensor(name, [P, n], dt) for name, n, dt in tensors]
            handles = [g.__enter__() for g in guards]
            for g in reversed(guards):
                g.__exit__(None, None, None)
            return handles

        X = sb("X", [P, NT, D_MODEL])
        nconst = place["mask"][0]
        const = sb("const", [P, nconst])
        ada = sb("ada", [P, 48, 2])
        scl = sb("scl", [P, 2, KT, 2])
        cload = sb("cload", [P, 2, KT])
        condf = sb("condf", [P, KT, 2])
        cond = sb("cond", [P, KT, 4], F32R)
        vrows = sb("vrows", [2 * KT + 2, P])
        vcols = sb("vcols", [P, 2 * KT + 2])
        convwr = sb("convwr", [CONV_WIDTH, CONV_CH])
        convw = sb("convw", [P, 2, CONV_WIDTH])
        routw = sb("routw", [P, KT, N_EXPERTS])
        qkw = sb("qkw", [P, 2, HEAD_DIM])
        sink = sb("sink", [P, Q_HEADS])
        nsink = sb("nsink", [P, Q_HEADS])
        dlog = sb("dlog", [P, 2, RET_HEADS])
        dneg = sb("dneg", [P, RET_HEADS, 2])
        dmin = sb("dmin", [P, RET_HEADS, 2])
        dln = sb("dln", [P, RET_HEADS, 2])
        dtok = sb("dtok", [P, 2, TT, RET_HEADS, 2])
        gnw = sb("gnw", [P, 256])
        lnw = sb("lnw", [P, 256])
        lnb = sb("lnb", [P, 256])
        ssq = sb("ssq", [P, NT])
        rstd = sb("rstd", [P, NT])
        qss = sb("qss", [P, NT, 10])
        qrs = sb("qrs", [P, NT, 10])
        nhalf = sb("nhalf", [P, 16])
        mx = sb("mx", [P, 2, Q_HEADS])
        negm = sb("negm", [P, 2, Q_HEADS])
        rsum = sb("rsum", [P, 2, Q_HEADS])
        esink = sb("esink", [P, 2, Q_HEADS])
        lnm = sb("lnm", [P, 16])
        lnv = sb("lnv", [P, 16])
        lnr = sb("lnr", [P, 16])
        bst = sb("bst", [P, NT, 6])
        bag = sb("bag", [P, NT, 2])
        lnt = sb("lnt", [P, 16])
        qst = sb("qst", [P, NT, 10])
        top = sb("top", [P, 7, TT, N_EXPERTS])
        best = sb("best", [P, 8, TT])
        most = sb("most", [P, 2])
        mosti = sb("mosti", [P, 1], I32)

        bank = [ctx.enter_context(nc.psum_tensor(f"bank{i}", [P, 512], F32)) for i in range(8)]
        VB, AB, OB = bank[0:4], bank[4:7], bank[7]

        def table(name):
            a, n = place[name]
            return const[:, a:a + n]

        ident = table("identity")
        cos64 = table("cos").rearrange("p (t k) -> p t k", t=TT)
        sin64 = table("sin").rearrange("p (t a h f) -> p t a h f", t=TT, a=2, h=2)
        ahead, behind = table("ahead"), table("behind")
        expo = table("exponents").rearrange("p (w d) -> p w d", d=2)

        KB = 256
        raw_t, parts_t, _, row_t = phase(("raw", 32 * KB, F32), ("parts", 64 * KB, F32R), ("gap_row", 32 * KB, F32),
                                         ("row", 24 * KB, F32))
        CBW = SEQ + CONV_WIDTH - 1
        (_, AD_t, CB_t, AKT, _, decay_t, SC_t, gb, PT_t, VW_t, hTr_t, proj_t, QK_t, RO_t, ST_t, mask_t) = phase(
            ("gap_ad", 16 * KB, F32), ("AD", 8 * KB, F32), ("CB", 4 * CBW + 4 + 4, F32), ("AKT", 2 * KB, F32),
            ("gap_decay", (64 - 24 - 2) * KB - (4 * CBW + 8), F32), ("decay", 8 * KB, F32), ("SC", 8 * KB, F32), ("gb", 8 * KB, F32),
            ("PT", 4 * KB, F32), ("VW", 4 * KB, F32), ("hTr", 32 * KB, F32R), ("proj", 28 * KB, F32),
            ("QK", 10 * KB, F32), ("RO", 4 * KB, F32), ("ST", 2 * KB, F32), ("mask", 4 * KB, F32))
        _, heads_t, _, hTf_t, _, xn_t = phase(
            ("gap_heads", 96 * KB, F32), ("heads", 16 * KB, F32), ("gap_hTf", 16 * KB, F32), ("hTf", 16 * KB, F32),
            ("gap_xn", 12 * KB, F32), ("xn", 16 * KB, F32))
        _, SG_t, YG_t, _, HFr_t, HF_t = phase(
            ("gap_sg", 88 * KB, F32), ("SG", 4 * KB, F32), ("YG", 4 * KB, F32), ("gap_hfr", 32 * KB, F32),
            ("HFr", 44 * KB, F32R), ("HF", 4 * KB, F32))
        _, XEr_t, HTr_t, SA_t, ACC_t, PA_t, XF_t, HE_t, YS, _, SCAT_t, SGE_t, GBX = phase(
            ("gap_e", 96 * KB, F32), ("XEr", 16 * KB, F32R), ("HTr", 8 * KB, F32R), ("SA", 8 * KB, F32),
            ("ACC", 8 * KB, F32), ("PA", 8 * KB, F32), ("XF", 4 * KB, F32), ("HE", 4 * KB, F32), ("YS", 4 * KB, F32),
            ("gap_e2", 8 * KB, F32), ("SCAT", 2 * KB, F32), ("SGE", 4 * KB, F32), ("GBX", 4 * KB, F32))

        raw = raw_t[:, :].rearrange("p (s n) -> p s n", s=RAW)
        parts = parts_t[:, :].rearrange("p (s two n) -> p s two n", s=PARTS, two=2)
        parts_f = parts_t[:, :].bitcast(F32).rearrange("p (s two n) -> p s two n", s=PARTS, two=2)
        row = row_t[0:4, 0:6 * D_MODEL]
        AD = AD_t[:, :].rearrange("p (h k) -> p h k", h=RET_HEADS)
        CB = CB_t[:, 0:4 * CBW].rearrange("p (c s n) -> p c s n", c=2, s=2)
        AKT = AKT[:, :]
        dec = decay_t[:, :]
        decay = dec.rearrange("p (h k) -> p h k", h=RET_HEADS)
        SC = SC_t[:, :].rearrange("p (b k) -> p b k", b=4)
        CA = gb[:, 0:1024].rearrange("p (c s n) -> p c s n", c=2, s=2)
        RW = gb[:, 1024:2048].rearrange("p (t c) -> p t c", t=NT)
        GB = gb[:, :].rearrange("p (s n) -> p s n", s=2)
        PT = PT_t[:, :].rearrange("p (b k) -> p b k", b=2)
        VW = VW_t[:, :].rearrange("p (t h d e) -> p t h d e", t=TT, h=RET_HEADS, d=2)
        hTr = hTr_t[:, :].rearrange("p (two k c) -> p two k c", two=2, k=KT)
        hTr_f = hTr_t[:, :].bitcast(F32).rearrange("p (two k c) -> p two k c", two=2, k=KT)
        proj = proj_t[:, :].rearrange("p (t c) -> p t c", t=NT)
        QK = QK_t[:, :].rearrange("p (t h d) -> p t h d", t=NT, d=HEAD_DIM)
        RO = RO_t[:, :].rearrange("p (t c) -> p t c", t=NT)
        ST = ST_t[:, :].rearrange("p (c n) -> p c n", c=2)
        mask = mask_t[:, :].rearrange("p (t k) -> p t k", t=TT)
        TMP = AD_t[:, 0:1280]
        AQT = heads_t[:, 0:2048].rearrange("p (r t n) -> p r t n", r=4, t=NT)
        RT = heads_t[:, 2048:4096].rearrange("p (b t n) -> p b t n", b=4, t=NT)
        CV = AD_t[:, 0:1024].rearrange("p (t c) -> p t c", t=NT)
        hTf = hTf_t[:, :].rearrange("p (k c) -> p k c", k=KT)
        xn = xn_t[:, :].rearrange("p (t c) -> p t c", t=NT)
        SG = SG_t[:, :].rearrange("p (b n) -> p b n", b=2)
        YG = YG_t[:, :].rearrange("p (b n) -> p b n", b=2)
        HF = HF_t[:, :].rearrange("p (b n) -> p b n", b=2)
        HFr = HFr_t[:, :].rearrange("p (two f n) -> p two f n", two=2, f=HALF_FF)
        HFr_f = HFr_t[:, :].bitcast(F32).rearrange("p (two f n) -> p two f n", two=2, f=HALF_FF)
        XEr = XEr_t[:, :].rearrange("p (b two k s) -> p b two k s", b=2, two=2, k=KT)
        XEr_f = XEr_t[:, :].bitcast(F32).rearrange("p (b two k s) -> p b two k s", b=2, two=2, k=KT)
        HTr = HTr_t[:, :].rearrange("p (b two n) -> p b two n", b=2, two=2)
        HTr_f = HTr_t[:, :].bitcast(F32).rearrange("p (b two n) -> p b two n", b=2, two=2)
        SA = SA_t[:, :].rearrange("p (e n) -> p e n", e=N_EXPERTS)
        ACC = ACC_t[:, :].rearrange("p (t c) -> p t c", t=TT)
        PA = PA_t[:, :].rearrange("p (t e s) -> p t e s", t=TT, e=N_EXPERTS)
        XF = XF_t[:, :].rearrange("p (k s) -> p k s", k=KT)
        WR = XF_t[:, :].rearrange("p (b i s) -> p b i s", b=2, i=4)
        HE = HE_t[:, :].rearrange("p (b n) -> p b n", b=2)
        SCAT = SCAT_t[:, :].rearrange("p (b n) -> p b n", b=2)
        SGE = SGE_t[:, :].rearrange("p (b n) -> p b n", b=2)

        raw_loaded = [sem(f"raw_loaded{i}") for i in range(RAW)]
        hi_ready, lo_ready = sem("weights_high_ready"), sem("weights_low_ready")
        slot_used = sem("parts_used")
        cond_hi, cond_f = sem("cond_high_ready"), sem("cond_silu_ready")
        row_clear = sem("row_cleared")
        h_hi, h_lo = sem("h_high_ready"), sem("h_low_ready")
        mix_hi = sem("mix_high_ready")
        ff_hi, ff_lo = sem("ffn_high_ready"), sem("ffn_low_ready")
        xe_high, xe_ready = sem("gathered_parts_high"), sem("gathered_parts_ready")
        ht_hi = sem("hidden_transposed_high")
        gate_half, up_half, down_half = sem("gate_half"), sem("up_half"), sem("down_half")
        v_full, v_done = sem("vector_bank_full"), sem("vector_bank_evacuated")
        a_full, a_done = sem("scalar_bank_full"), sem("scalar_bank_evacuated")
        tables_in, x_in, c_in = sem("tables_in"), sem("x_in"), sem("c_in")
        mask_in = sem("mask_in")
        small_in, bias_in, router_in = sem("small_in"), sem("bias_in"), sem("router_in")
        cond_ready = sem("cond_ready")
        mod_ready = sem("modulation_ready")
        sq_ready, rstd_ready, xn_ready = sem("squares_ready"), sem("rstd_ready"), sem("normalized_ready")
        x_ready = sem("residual_ready")
        dneg_ready, dln_ready = sem("decay_arg_ready"), sem("decay_ln_ready")
        dexp_in, dexp_out = sem("decay_exponents_ready"), sem("decay_exp_ready")
        qss_ready, qrs_ready, qk_ready = sem("qk_squares_ready"), sem("qk_rstd_ready"), sem("qk_ready")
        vw_ready = sem("weighted_values_ready")
        pad_ready = sem("conv_pad_ready")
        negm_ready, exp_ready = sem("negmax_ready"), sem("exp_ready")
        sarg_ready, esink_ready = sem("sink_arg_ready"), sem("sink_exp_ready")
        att_done, att_read = sem("attention_products"), sem("attention_evacuated")
        ro_var, ro_rstd = sem("retention_variance_ready"), sem("retention_rstd_ready")
        cv_var, cv_rstd = sem("conv_variance_ready"), sem("conv_rstd_ready")
        ln_ready, rg_ready = sem("conv_norm_ready"), sem("retention_gate_ready")
        act_mix = sem("conv_silu_ready")
        out_ready = sem("output_ready")
        lexp_in, lexp_out = sem("gate_arg_ready"), sem("gate_exp_ready")
        mask_ready = sem("top2_masks_ready")
        scat_in = sem("scatter_rows_ready")
        most_ready = sem("most_tokens_ready")
        gate_full, gate_read = sem("gate_full"), sem("gate_silu_done")
        up_full, up_read = sem("up_full"), sem("up_multiplied")
        h_turned, ht_ready = sem("hidden_transposed"), sem("hidden_transposed_ready")
        down_done, y_ready = sem("down_done"), sem("expert_out_ready")
        gather_full, xe_lo, xe_hi = sem("gather_full"), sem("gathered_low_ready"), sem("gathered_high_ready")
        st_ready = sem("scatter_matrix_ready")
        scatter_full, scatter_read = sem("scatter_full"), sem("scatter_added")
        out_in = sem("out_stored")
        tap_done = sem("conv_tap_done")
        rank_moved = sem("rank_moved")
        v_step, a_step, p_step = sem("vector_step"), sem("scalar_step"), sem("gpsimd_step")

        block = ctx.enter_context(nc.Block())

        def counter(eng):
            seen = {}

            def after(s, n=1):
                seen[s] = seen.get(s, 0) + n
                eng.wait_ge(s, seen[s])
            return after

        def stepper(eng, s):
            n = [0]

            def step(ins):
                n[0] += 1
                ins.then_inc(s, 1)
                eng.wait_ge(s, n[0])
            return step

        def tiles_of(layer):
            return range(NT) if layer == 0 else range(TT)

        def cols(w, a, b, k0=0, k1=KT):
            return w[k0 * P:k1 * P, a:b].rearrange("(k p) n -> p k n", p=P)

        IN_SLICES = [(C_Q, C_RQ), (0, 384), (384, 768), (C_RQ, C_CONV), (C_CONV, IN_COLS)]
        HALVES = ((0, KT // 2), (KT // 2, KT))
        items = []
        first = {}
        ff_split = [(0, 4), (4, 8), (8, HALF_FF)]
        for layer in range(DEPTH):
            first["ada", layer] = len(items)
            n = 0
            for s in range(12):
                w = io["ada_w"][layer][:, s * SLICE:(s + 1) * SLICE].rearrange("(p k) n -> p k n", k=KT)
                for k0, k1 in HALVES:
                    items.append(([w[:, k0:k1, :]], k1 - k0, SLICE, n % RAW, (n + layer) % 3))
                    n += 1
            first["in", layer] = len(items)
            n = 0
            for a, b in IN_SLICES:
                for k0, k1 in HALVES:
                    items.append(([cols(io["w_in"][layer], a, b, k0, k1)], k1 - k0, b - a, n % 2, (n + layer) % 2))
                    n += 1
            first["out", layer] = len(items)
            for h in range(2):
                for k0, k1 in HALVES:
                    items.append(([cols(io["w_out"][layer], h * SLICE, (h + 1) * SLICE, k0, k1)],
                                  k1 - k0, SLICE, n % 2, (n + layer) % 2))
                    n += 1
            if layer == 0:
                first["ffn"] = len(items)
                n = 0
                for p0 in range(0, FF_TILES, HALF_FF):
                    for f in range(p0, p0 + HALF_FF):
                        items.append(([cols(io["ffn_w_gate"][0], f * P, (f + 1) * P), cols(io["ffn_w_up"][0], f * P, (f + 1) * P)],
                                      KT, 2 * P, n % RAW, n % 3))
                        n += 1
                    for h in range(2):
                        for f0, f1 in ff_split:
                            items.append(([io["ffn_w_down"][0][(p0 + f0) * P:(p0 + f1) * P, h * SLICE:(h + 1) * SLICE]
                                           .rearrange("(k p) n -> p k n", p=P)], f1 - f0, SLICE, n % RAW, n % 3))
                            n += 1
                assert n % 3 == 1
        BASE = len(items)
        loads_before = [sum(len(it[0]) for it in items if it[3] == s) for s in range(RAW)]

        order = []
        for g in range(PAIR_SLICES):
            order += [("gate", 0, g), ("gate", 1, g), ("up", 0, g), ("up", 1, g)]
            order += [("down", 0, g - 1), ("down", 1, g - 1)] if g else []
        order += [("down", 0, PAIR_SLICES - 1), ("down", 1, PAIR_SLICES - 1)]
        used_sem = {("gate", 0): gate_half, ("gate", 1): gate_full, ("up", 0): up_half, ("up", 1): up_full,
                    ("down", 0): down_half, ("down", 1): down_done}

        def parts_free(pair, n, part):
            back = n < PARTS
            kind, half, g = order[n - PARTS]
            extra = CREDIT if kind == "down" else 0
            return used_sem[kind, half], pair * PAIR_SLICES + (part * PAIRS * PAIR_SLICES + g + 1 + extra
                                                               - (PAIR_SLICES if back else 0))

        last_use = {}
        job = {}

        @block.tensor
        def _(pe):
            after = counter(pe)
            n_v, n_a, n_i, n_u, n_norm = [0], [0], [0], [0], [0]

            def open_v(name=None):
                n = n_v[0]
                n_v[0] += 1
                if n >= len(VB):
                    pe.wait_ge(v_done, n - len(VB) + 1)
                if name:
                    job[name] = n
                return VB[n % len(VB)]

            def open_a(name=None):
                n = n_a[0]
                n_a[0] += 1
                if n >= len(AB):
                    pe.wait_ge(a_done, n - len(AB) + 1)
                if name:
                    job[name] = n
                return AB[n % len(AB)]

            def next_item():
                n = n_i[0]
                n_i[0] += 1
                _, k, width, _, s = items[n]
                pe.wait_ge(lo_ready, n + 1)
                hi, lo = (parts[:, s, i, 0:k * width].rearrange("p (k n) -> p k n", k=k) for i in range(2))
                return n, hi, lo

            def part_used(n, mm):
                n_u[0] += 1
                mm.then_inc(slot_used, 1)
                last_use[n] = (slot_used, n_u[0])

            def three(out, st, mv, start, stop):
                nc.tensor.matmul(out, st[0], mv[0], start=start, stop=False)
                nc.tensor.matmul(out, st[0], mv[1], start=False, stop=False)
                return nc.tensor.matmul(out, st[1], mv[0], start=False, stop=stop)

            def ada_rows():
                pe.wait_ge(cond_ready, 1)
                for s in range(12):
                    b = open_v()
                    for k0, k1 in HALVES:
                        n, hi, lo = next_item()
                        for k in range(k0, k1):
                            nc.tensor.matmul(b[0:4, :], cond[:, k, :], hi[:, k - k0, :], start=(k == 0), stop=False)
                            mm = nc.tensor.matmul(b[0:4, :], cond[:, k, :], lo[:, k - k0, :], start=False, stop=(k == KT - 1))
                        if k0 == 0:
                            part_used(n, mm)
                    mm.then_inc(v_full, 1)
                    last_use[n] = (v_full, n_v[0])
                pe.wait_ge(v_done, n_v[0])
                b = open_v()
                for c in range(48):
                    nc.tensor.matmul(b[:, 2 * c:2 * c + 2], row[:, c * P:(c + 1) * P], table("fold")[0:4, :],
                                     start=True, stop=True)
                after(small_in, 16 * N_SMALL)
                nc.tensor.transpose(b[:, 96:96 + 2 * KT + 2], vrows[:, :], ident[0:2 * KT + 2, 0:2 * KT + 2])\
                    .then_inc(v_full, 1)

            def turn_normalized(streams, credits=False):
                signals = [down_half, down_done] * CREDIT if credits else []
                for s in streams:
                    after(xn_ready, TT)
                    for kp in range(KT // 2):
                        b = open_v() if s == 0 else open_a()
                        for kk in range(2):
                            for t in range(TT):
                                k = 2 * kp + kk
                                mm = nc.tensor.transpose(b[:, (kk * TT + t) * P:(kk * TT + t + 1) * P],
                                                         xn[:, s * TT + t, k * P:(k + 1) * P], ident)
                                if signals and not (kk and t == TT - 1):
                                    mm.then_inc(signals.pop(), 1)
                        mm.then_inc(v_full if s == 0 else a_full, 1)
                    if s == 0:
                        job[("normalized", n_norm[0])] = n_v[0]
                n_norm[0] += 1

            def modulated_in(streams):
                after(h_lo, len(streams))

            def project_in(layer):
                for a, b_ in IN_SLICES[:-1]:
                    tiles = range(NT) if layer == 0 or b_ <= C_Q else range(TT)
                    outs = [(open_v if t % 2 == 0 else open_a)(("in", layer, a, t)) for t in tiles]
                    for k0, k1 in HALVES:
                        n, hi, lo = next_item()
                        for t in tiles:
                            tok = slice(t * P, (t + 1) * P)
                            for k in range(k0, k1):
                                mm = three(outs[t][:, 0:b_ - a], (hTr[:, 0, k, tok], hTr[:, 1, k, tok]),
                                           (hi[:, k - k0, :], lo[:, k - k0, :]), k == 0, k == KT - 1)
                            if k1 == KT:
                                mm.then_inc(v_full if t % 2 == 0 else a_full, 1)
                        if k0 == 0:
                            part_used(n, mm)
                    last_use[n] = (a_full, n_a[0])
                cols_ = (SEQ + CTX_LEN) if layer == 0 else SEQ
                outs = [(ct, half, open_a(("conv_gate", layer, ct)) if half else open_v()) for ct in range(2) for half in (1, 0)]
                for k0, k1 in HALVES:
                    n, hi, lo = next_item()
                    for ct, half, b in outs:
                        c0 = half * CONV_CH + ct * P
                        for k in range(k0, k1):
                            mm = three(b[:, 0:cols_], (hi[:, k - k0, c0:c0 + P], lo[:, k - k0, c0:c0 + P]),
                                       (hTr[:, 0, k, 0:cols_], hTr[:, 1, k, 0:cols_]), k == 0, k == KT - 1)
                        if k1 == KT:
                            mm.then_inc(a_full if half else v_full, 1)
                    if k0 == 0:
                        part_used(n, mm)
                last_use[n] = (v_full, n_v[0])

            def turn_heads(layer):
                b = open_v()
                for ct in range(2):
                    mm = nc.tensor.transpose(b[:, ct * 32:ct * 32 + CONV_WIDTH],
                                             convwr[:, ct * P:(ct + 1) * P], ident[0:CONV_WIDTH, 0:CONV_WIDTH])
                mm.then_inc(v_full, 1)
                pe.wait_ge(a_done, n_a[0])
                for t in tiles_of(layer):
                    b = open_v()
                    for i, c in enumerate((C_RQ, C_RQ + P, C_RK, C_RK + P)):
                        mm = nc.tensor.transpose(b[:, i * P:(i + 1) * P], proj[:, t, c:c + P], ident)
                    mm.then_inc(v_full, 1)

            def turn_qk(layer):
                bk = OB
                for t in range(NT):
                    if t in tiles_of(layer):
                        b = open_a()
                    after(qk_ready)
                    if t in tiles_of(layer):
                        for r in range(4):
                            mm = nc.tensor.transpose(b[:, r * P:(r + 1) * P],
                                                     QK[:, t, 2 * r:2 * r + 2, :].rearrange("p h d -> p (h d)"), ident)
                        mm.then_inc(a_full, 1)
                    mm = nc.tensor.transpose(bk[:, t * P:(t + 1) * P],
                                             QK[:, t, 8:10, :].rearrange("p h d -> p (h d)"), ident)
                    mm.then_inc(att_done, 1)

            def states():
                b = open_v()
                after(vw_ready, TT)
                for pair in range(2):
                    for t in range(TT):
                        mm = nc.tensor.matmul(b[:, pair * 256:(pair + 1) * 256],
                                              proj[:, TT + t, C_RK + pair * P:C_RK + (pair + 1) * P],
                                              VW[:, t, 2 * pair:2 * pair + 2, :, :].rearrange("p h d e -> p (h d e)"),
                                              start=(t == 0), stop=(t == TT - 1))
                mm.then_inc(v_full, 1)

            def retention(layer):
                def scores(s, h):
                    b = open_v(("decayed", layer, s, h))
                    lo = 64 * (h % 2)
                    for jt in range(TT):
                        mm = nc.tensor.matmul(b[:, jt * SEQ:(jt + 1) * SEQ],
                                              RT[lo:lo + 64, 2 + h // 2, s * TT + jt, :],
                                              RT[lo:lo + 64, h // 2, s * TT:s * TT + TT, :].rearrange("p t n -> p (t n)"),
                                              start=True, stop=True)
                    mm.then_inc(v_full, 1)

                def apply(s, h, outs):
                    pe.wait_ge(v_done, job[("decayed", layer, s, h)] + 1)
                    for it in range(TT):
                        for jt in range(TT):
                            mm = nc.tensor.matmul(outs[it][:, h * 64:(h + 1) * 64],
                                                  AD[:, h, jt * SEQ + it * P:jt * SEQ + (it + 1) * P],
                                                  proj[:, s * TT + jt, C_RV + h * 64:C_RV + (h + 1) * 64],
                                                  start=(jt == 0), stop=(jt == TT - 1))
                        if h == RET_HEADS - 1:
                            mm.then_inc(a_full, 1)

                pe.wait_ge(v_done, n_v[0])
                for s in ((0, 1) if layer == 0 else (0,)):
                    scores(s, 0)
                    outs = [open_a(("inner", layer, s)), open_a()]
                    for h in range(RET_HEADS):
                        if h + 1 < RET_HEADS:
                            scores(s, h + 1)
                        apply(s, h, outs)
                for t in range(TT):
                    b = open_v()
                    for pair in range(2):
                        mm = nc.tensor.matmul(b[:, pair * 256:(pair + 1) * 256], RT[:, pair, t, :], ST[:, pair, :],
                                              start=True, stop=True)
                    mm.then_inc(v_full, 1)

            def attention(layer):
                its = [(t, r, g) for t in tiles_of(layer) for r in range(4) for g in range(2)]
                after(att_read)
                pe.wait_ge(a_done, n_a[0])

                def scores(n):
                    t, r, g = its[n]
                    b = open_v()
                    k0 = 0 if t < TT else SEQ
                    nc.tensor.matmul(b[:, k0:2 * SEQ], AQT[64 * g:64 * g + 64, r, t, :], AKT[64 * g:64 * g + 64, k0:],
                                     start=True, stop=True).then_inc(v_full, 1)

                def turn(n):
                    t, r, g = its[n]
                    b = open_a(("probs", layer, n))
                    after(exp_ready)
                    for kb in range(0 if t < TT else TT, NT):
                        mm = nc.tensor.transpose(b[:, kb * P:(kb + 1) * P], SC[:, n % 4, kb * P:(kb + 1) * P], ident)
                    mm.then_inc(a_full, 1)

                def values(n):
                    t, r, g = its[n]
                    head = g * 4 + r
                    if n % 8 == 0 and n:
                        after(att_read)
                    pe.wait_ge(a_done, job[("probs", layer, n)] + 1)
                    first = 0 if t < TT else TT
                    for kb in range(first, NT):
                        mm = nc.tensor.matmul(OB[:, head * 64:(head + 1) * 64], PT[:, n % 2, kb * P:(kb + 1) * P],
                                              proj[:, kb, C_V + 64 * g:C_V + 64 * g + 64],
                                              start=(kb == first), stop=(kb == NT - 1))
                    mm.then_inc(att_done, 1)

                for n in range(len(its) + 3):
                    if n < len(its):
                        scores(n)
                    if 2 <= n < len(its) + 2:
                        turn(n - 2)
                    if n >= 3:
                        values(n - 3)
                after(att_read)

            def turn_conv(layer):
                pe.wait_ge(tap_done, TAPS * (layer + 1))
                for t in tiles_of(layer):
                    b = open_v()
                    for ct in range(2):
                        mm = nc.tensor.transpose(b[:, ct * P:(ct + 1) * P],
                                                 CA[:, ct, t // TT, (t % TT) * P:(t % TT + 1) * P], ident)
                    mm.then_inc(v_full, 1)

            def turn_mix(layer):
                after(act_mix)
                for t in tiles_of(layer):
                    for half in range(2):
                        b = open_v(("mix", layer, t, half))
                        for i in range(4):
                            c = C_Q + (half * 4 + i) * P
                            mm = nc.tensor.transpose(b[:, i * P:(i + 1) * P], proj[:, t, c:c + P], ident)
                        mm.then_inc(v_full, 1)

            def spread_gate(group, streams):
                for s in streams:
                    for half in range(2):
                        b = open_a()
                        for i in range(4):
                            c = group * KT + half * 4 + i
                            mm = nc.tensor.matmul(b[:, i * P:(i + 1) * P], ada[:, c, s:s + 1].broadcast_to([P, P]), ident,
                                                  start=True, stop=True)
                        mm.then_inc(a_full, 1)

            def project_out(layer):
                pe.wait_ge(v_done, n_v[0])
                pe.wait_ge(a_done, n_a[0])
                for half in range(2):
                    outs = [open_v() for _ in tiles_of(layer)]
                    for k0, k1 in HALVES:
                        n, hi, lo = next_item()
                        for t in tiles_of(layer):
                            tok = slice(t * P, (t + 1) * P)
                            for k in range(k0, k1):
                                mm = three(outs[t][:, :], (hTr[:, 0, k, tok], hTr[:, 1, k, tok]),
                                           (hi[:, k - k0, :], lo[:, k - k0, :]), k == 0, k == KT - 1)
                            if k1 == KT:
                                mm.then_inc(v_full, 1)
                        if k0 == 0:
                            part_used(n, mm)
                    last_use[n] = (v_full, n_v[0])
                job[("mixed", layer)] = n_v[0]

            def dense_ffn():
                for p0 in range(0, FF_TILES, HALF_FF):
                    for f in range(p0, p0 + HALF_FF):
                        n, hi, lo = next_item()
                        for half in range(2):
                            b = open_a(("gate", f)) if half == 0 else open_v(("up", f))
                            c0 = half * P
                            for k in range(KT):
                                mm = three(b[:, :], (hi[:, k, c0:c0 + P], lo[:, k, c0:c0 + P]),
                                           (hTr[:, 0, k, :], hTr[:, 1, k, :]), k == 0, k == KT - 1)
                            mm.then_inc(a_full if half == 0 else v_full, 1)
                        last_use[n] = (v_full, n_v[0])
                    if p0 == 0:
                        spread_gate(5, (0, 1))
                        pe.wait_ge(a_done, n_a[0])
                    after(ff_lo, HALF_FF)
                    for half in range(2):
                        outs = [open_v() for _ in range(NT)]
                        for f0, f1 in ff_split:
                            n, hi, lo = next_item()
                            for f in range(f0, f1):
                                for t in range(NT):
                                    tok = slice(t * P, (t + 1) * P)
                                    mm = three(outs[t][:, :], (HFr[:, 0, f, tok], HFr[:, 1, f, tok]),
                                               (hi[:, f - f0, :], lo[:, f - f0, :]), f == 0, f == HALF_FF - 1)
                                    if f == HALF_FF - 1:
                                        mm.then_inc(v_full, 1)
                            if f1 < HALF_FF:
                                part_used(n, mm)
                            else:
                                last_use[n] = (v_full, n_v[0])

            def routing():
                b = open_v()
                after(router_in, 16)
                pe.wait_ge(v_done, n_v[0] - 1)
                for t in range(TT):
                    for k in range(KT):
                        mm = nc.tensor.matmul(b[:, t * N_EXPERTS:(t + 1) * N_EXPERTS], hTf[:, k, t * P:(t + 1) * P],
                                              routw[:, k, :],
                                              start=(k == 0), stop=(k == KT - 1))
                mm.then_inc(v_full, 1)
                b = open_v()
                after(mask_ready)
                chosen = top[:, 0, :, :]
                nc.tensor.matmul(b[:, 0:8], table("before"), chosen[:, 0, :], start=True, stop=True)
                nc.tensor.matmul(b[:, 8:16], table("ones"), chosen[:, 0, :], start=True, stop=False)
                nc.tensor.matmul(b[:, 8:16], table("before"), chosen[:, 1, :], start=False, stop=True)
                nc.tensor.matmul(b[:, 16:24], table("ones"), chosen[:, 0, :], start=True, stop=False)
                nc.tensor.matmul(b[:, 16:24], table("ones"), chosen[:, 1, :], start=False, stop=True).then_inc(v_full, 1)

            def scatter_matrices(part):
                for e in range(0, N_EXPERTS, 2):
                    b = open_v()
                    after(scat_in)
                    for i in range(2):
                        for t in range(TT):
                            mm = nc.tensor.transpose(b[:, i * 256 + t * P:i * 256 + (t + 1) * P],
                                                     WR[:, (e // 2) % 2, i * TT + t, :], ident)
                    mm.then_inc(v_full, 1)

            def experts(part):
                G, U, Y, T, M = bank[0], bank[1], bank[2:4], bank[4:6], bank[6:8]
                s0 = part * N_EXPERTS * EF_SLICES
                e0 = part * N_EXPERTS
                pe.wait_ge(v_done, n_v[0])
                pe.wait_ge(a_done, n_a[0])

                with pe.Fori(0, PAIRS) as i:
                    def gather(ee):
                        e = 2 * i + ee
                        pe.wait_ge(scatter_read, i * 8 + (4 * e0 + 1))
                        for k in range(KT):
                            for t in range(TT):
                                mm = nc.tensor.matmul(M[k // 4][:, (k % 4) * P:(k % 4 + 1) * P], xn[:, t, k * P:(k + 1) * P],
                                                      PA[:, t, bass.ds(e, 1), :].rearrange("p e s -> p (e s)"),
                                                      start=(t == 0), stop=(t == TT - 1))
                            if k % 4 == 3:
                                mm.then_inc(gather_full, 1)

                    def scatter(ee):
                        pe.wait_ge(st_ready, i + (part * PAIRS + 1))
                        pe.wait_ge(y_ready, i * 4 + (2 * e0 + 2 * ee + 2))
                        for t in range(TT):
                            for h in range(2):
                                if t:
                                    pe.wait_ge(scatter_read, i * 8 + (4 * e0 + 1 + 4 * ee + h + 1))
                                nc.tensor.matmul(M[h][:, :], SCAT[:, ee, t * P:(t + 1) * P], YS[:, h * 512:(h + 1) * 512],
                                                 start=True, stop=True).then_inc(scatter_full, 1)

                    def weights(n):
                        pe.wait_ge(lo_ready, i * PAIR_ITEMS + (BASE + part * PAIRS * PAIR_ITEMS + n + 1))
                        return [parts[:, n % PARTS, j, :].rearrange("p (k n) -> p k n", n=SLICE) for j in range(2)]

                    def gate_or_up(g, n, b, half_used, full):
                        if g:
                            pe.wait_ge(gate_read if b is G else up_read, i * PAIR_SLICES + (s0 + g))
                        for half in range(2):
                            hi, lo = weights(n + half)
                            for kk in range(4):
                                k = 4 * half + kk
                                x = XEr[:, g // EF_SLICES, :, k, :]
                                mm = three(b[:, :], (x[:, 0, :], x[:, 1, :]), (hi[:, kk, :], lo[:, kk, :]), k == 0, k == KT - 1)
                            mm.then_inc(full if half else half_used, 1)

                    def turn(g):
                        pe.wait_ge(up_read, i * PAIR_SLICES + (s0 + g + 1))
                        if g >= 2:
                            pe.wait_ge(ht_ready, i * PAIR_SLICES + (s0 + g - 1))
                        for j in range(4):
                            mm = nc.tensor.transpose(T[g % 2][:, j * P:(j + 1) * P], HE[:, g % 2, j * P:(j + 1) * P], ident)
                        mm.then_inc(h_turned, 1)

                    def down(g, n):
                        pe.wait_ge(ht_ready, i * PAIR_SLICES + (s0 + g + 1))
                        for half in range(2):
                            hi, lo = (v.rearrange("p (j h) n -> p j h n", h=2) for v in weights(n + half))
                            for jj in range(2):
                                j = 2 * half + jj
                                x = HTr[:, g % 2, :, j * P:(j + 1) * P]
                                for h in range(2):
                                    mm = three(Y[h][:, :], (x[:, 0, :], x[:, 1, :]), (hi[:, jj, h, :], lo[:, jj, h, :]),
                                               g % EF_SLICES == 0 and j == 0, g % EF_SLICES == EF_SLICES - 1 and j == 3)
                            mm.then_inc(down_done if half else down_half, 1)

                    n = 0
                    for g in range(PAIR_SLICES):
                        if g == 0:
                            gather(0)
                        if g % EF_SLICES == 0:
                            pe.wait_ge(xe_ready, i * 2 + (e0 + g // EF_SLICES + 1))
                        gate_or_up(g, n, G, gate_half, gate_full)
                        if g >= 1:
                            turn(g - 1)
                        if g == 5:
                            gather(1)
                        gate_or_up(g, n + 2, U, up_half, up_full)
                        n += 4
                        if g == EF_SLICES + 1:
                            scatter(0)
                        if g >= 1:
                            down(g - 1, n)
                            n += 2
                    turn(PAIR_SLICES - 1)
                    down(PAIR_SLICES - 1, n)
                    scatter(1)

            after(tables_in, 16)
            for layer in range(DEPTH):
                streams = (0, 1) if layer == 0 else (0,)
                ada_rows()
                after(mod_ready)
                turn_normalized((0, 1))
                modulated_in((0, 1))
                project_in(layer)
                turn_heads(layer)
                turn_qk(layer)
                states()
                retention(layer)
                attention(layer)
                turn_conv(layer)
                turn_mix(layer)
                spread_gate(2, streams)
                project_out(layer)
                turn_normalized(streams, credits=layer == 1)
                if layer == 0:
                    modulated_in(streams)
                    dense_ffn()
            routing()
            scatter_matrices(0)
            spread_gate(5, (0,))
            experts(0)
            after(most_ready)
            over = pe.value_load(mosti[0:1, 0:1], min_val=0, max_val=SEQ)
            with pe.If(over > P):
                scatter_matrices(1)
                experts(1)

        @block.sync
        def _(sp):
            sp.dma_start(cload[:, 0, :], io["c"].rearrange("b (p k) -> (b p) k", k=KT)).then_inc(c_in, 16)
            sp.dma_start(cload[:, 1, :], io["c_ctx"].rearrange("(p k) -> p k", k=KT)).then_inc(c_in, 16)
            sp.dma_start(const[:, :], io["shape_tables"][:, 0:nconst]).then_inc(tables_in, 16)
            sp.dma_start(X[:, 0:TT, :], io["x"].rearrange("b (t p) n -> p (b t) n", p=P)).then_inc(x_in, 16)
            sp.dma_start(X[:, TT:NT, :], io["ctx"].rearrange("b (t p) n -> p (b t) n", p=P)).then_inc(x_in, 16)
            holder = [None] * RAW
            for n, (srcs, k, width, s, _) in enumerate(items):
                if holder[s] is not None:
                    sp.wait_ge(lo_ready, holder[s] + 1)
                if n in (first["ffn"] + 2, first["ffn"] + 3):
                    sp.wait_ge(v_full, job[("mixed", 0)])
                holder[s] = n
                dst = raw[:, s, 0:k * width].rearrange("p (k n) -> p k n", k=k)
                part_w = width // len(srcs)
                for j, src in enumerate(srcs):
                    sp.dma_start(dst[:, :, j * part_w:(j + 1) * part_w], src).then_inc(raw_loaded[s], 16)

            def expert_loads(part):
                before = BASE + part * PAIRS * PAIR_ITEMS
                sp.wait_ge(lo_ready, before)
                sp.wait_ge(v_full, job[("mixed", 1)])
                with sp.Fori(0, PAIRS) as i:
                    for n, (kind, half, g) in enumerate(order):
                        e = i * 2 + g // EF_SLICES
                        s = g % EF_SLICES
                        sp.wait_ge(lo_ready, i * PAIR_ITEMS + (before + n - RAW + 1))
                        if kind == "down":
                            r0 = s * SLICE + half * 2 * P
                            rows = io["moe_w_down"][0][bass.ds(e, 1), r0:r0 + 2 * P, :].rearrange("e (k p) n -> p (e k) n", p=P)
                            dst = raw[:, n % RAW, :].rearrange("p (k n) -> p k n", k=2)
                        else:
                            r0 = half * 4 * P
                            rows = io["moe_w_" + kind][0][bass.ds(e, 1), r0:r0 + 4 * P, s * SLICE:(s + 1) * SLICE]\
                                .rearrange("e (k p) n -> p (e k) n", p=P)
                            dst = raw[:, n % RAW, :].rearrange("p (k n) -> p k n", k=4)
                        sp.dma_start(dst, rows).then_inc(raw_loaded[n % RAW], 16)

            expert_loads(0)
            sp.wait_ge(most_ready, 1)
            over = sp.value_load(mosti[0:1, 0:1], min_val=0, max_val=SEQ)
            with sp.If(over > P):
                expert_loads(1)
            for t in range(TT):
                sp.wait_ge(out_ready, t + 1)
                sp.dma_start(io["out"][0, t * P:(t + 1) * P, :], X[:, t, :]).then_inc(out_in, 16)
            sp.wait_ge(out_in, 16 * TT)

        @block.scalar
        def _(act):
            after = counter(act)
            step = stepper(act, a_step)
            n_a = [0]

            def take():
                n = n_a[0]
                n_a[0] += 1
                act.wait_ge(a_full, n + 1)
                return AB[n % len(AB)]

            n_hi = [0]
            n_norm = [0]
            holders = [None] * PARTS
            loads = [0] * RAW

            def split_to(stop):
                while n_hi[0] < stop:
                    n = n_hi[0]
                    n_hi[0] += 1
                    srcs, k, width, r, s = items[n]
                    loads[r] += len(srcs)
                    act.wait_ge(raw_loaded[r], 16 * loads[r])
                    if holders[s] is not None:
                        act.wait_ge(*last_use[holders[s]])
                    if n == first["ffn"] + 2:
                        act.wait_ge(v_full, job[("mixed", 0)])
                    holders[s] = n
                    nc.scalar.activation(parts[:, s, 0, 0:k * width], raw[:, r, 0:k * width], ACT.Copy).then_inc(hi_ready, 1)

            def small_loads(layer):
                for r, name in ((0, "norm1_w"), (KT, "norm2_w"), (2 * KT, "conv_b")):
                    v = io[name][layer].rearrange("(k p) -> k p", p=P)
                    act.dma_start(vrows[r:r + v.shape[0], :], v).then_inc(small_in, 16)
                act.dma_start(convwr[:, :], io["conv_w"][layer]).then_inc(small_in, 16)
                for dst, src in ((qkw[:, 0, :], "q_norm_w"), (qkw[:, 1, :], "k_norm_w"), (sink[:, :], "attn_sink"),
                                 (dlog[:, 0, :], "ret_decay_f"), (dlog[:, 1, :], "ret_decay_b"),
                                 (gnw[:, :], "ret_gn_w"), (lnw[:, :], "conv_ln_w"), (lnb[:, :], "conv_ln_b")):
                    src = io[src][layer]
                    act.dma_start(dst, src.unsqueeze(0).broadcast_to([P, src.shape[0]])).then_inc(small_in, 16)
                a, n = place["mask"]
                act.dma_start(mask_t[:, :], io["shape_tables"][:, a:a + n]).then_inc(mask_in, 16)
                b = io["ada_b"][layer]
                act.wait_ge(row_clear, layer + 1)
                act.dma_start(row[0:2, :], b.unsqueeze(0).broadcast_to([2, b.shape[0]])).then_inc(bias_in, 16)

            def squares(tiles):
                for t in tiles:
                    nc.scalar.activation(xn[:, t, :], X[:, t, :], ACT.Square, accum_out=ssq[:, t:t + 1]).then_inc(sq_ready, 1)

            def modulate(which, s):
                for kp in range(KT // 2):
                    b = take()
                    for kk in range(2):
                        k = 2 * kp + kk
                        ins = nc.scalar.activation(hTf[:, k, s * SEQ:(s + 1) * SEQ], b[:, kk * SEQ:(kk + 1) * SEQ], ACT.Identity,
                                                   bias=ada[:, 3 * which * KT + k, s:s + 1], scale=scl[:, which, k, s:s + 1])
                    ins.then_inc(a_done, 1)

            def high_parts(streams):
                for s in streams:
                    if s == 0:
                        act.wait_ge(v_done, job[("normalized", n_norm[0])])
                    else:
                        act.wait_ge(a_done, n_a[0])
                    c = slice(s * SEQ, (s + 1) * SEQ)
                    nc.scalar.activation(hTr[:, 0, :, c], hTf[:, :, c], ACT.Copy).then_inc(h_hi, 1)
                n_norm[0] += 1

            def copy_out(out, src):
                nc.scalar.activation(out, src, ACT.Copy).then_inc(a_done, 1)

            def gate_rows(rows, streams):
                for s in streams:
                    for half in range(2):
                        copy_out(rows[:, s, half * 512:(half + 1) * 512], take()[:, :])

            def attention(layer, base):
                its = [(t, r, g) for t in tiles_of(layer) for r in range(4) for g in range(2)]
                for n in range(len(its) + 2):
                    if n < len(its):
                        t, r, g = its[n]
                        head, turn = g * 4 + r, (n // 8) % 2
                        k0 = 0 if t < TT else SEQ
                        after(negm_ready)
                        nc.scalar.activation(SC[:, n % 4, k0:], SC[:, n % 4, k0:], ACT.Exp, bias=negm[:, turn, head:head + 1],
                                             scale=HEAD_DIM ** -0.5, accum_out=rsum[:, turn, head:head + 1]).then_inc(exp_ready, 1)
                        if n % 8 == 7:
                            after(sarg_ready)
                            nc.scalar.activation(esink[:, turn, :], esink[:, turn, :], ACT.Exp).then_inc(esink_ready, 1)
                    if n >= 2:
                        m = n - 2
                        k0 = 0 if its[m][0] < TT else SEQ
                        b = take()
                        if m >= 2:
                            act.wait_ge(att_done, base + m - 1)
                        copy_out(PT[:, m % 2, k0:], b[:, k0:])

            def experts(part):
                G, T, M = bank[0], bank[4:6], bank[6]
                s0, e0 = part * N_EXPERTS * EF_SLICES, part * N_EXPERTS
                with act.Fori(0, PAIRS) as i:
                    def split(n):
                        r = n % RAW
                        act.wait_ge(raw_loaded[r], i * (16 * PAIR_ITEMS // RAW)
                                    + 16 * (loads_before[r] + part * PAIRS * PAIR_ITEMS // RAW + n // RAW + 1))
                        act.wait_ge(*parts_free(i, n, part))
                        nc.scalar.activation(parts[:, n % PARTS, 0, :], raw[:, r, :], ACT.Copy).then_inc(hi_ready, 1)

                    def gathered(ee):
                        act.wait_ge(gather_full, i * 4 + (2 * (e0 + ee) + 1))
                        for k in range(4):
                            ins = nc.scalar.activation(XF[:, k, :], M[:, k * P:(k + 1) * P], ACT.Identity,
                                                       bias=ada[:, 3 * KT + k, 0:1], scale=scl[:, 1, k, 0:1])
                        ins.then_inc(xe_lo, 1)
                        act.wait_ge(xe_lo, i * 2 + (e0 + ee + 1))
                        act.wait_ge(xe_hi, i * 2 + (e0 + ee + 1))
                        nc.scalar.activation(XEr[:, ee, 0, :, :], XF, ACT.Copy).then_inc(xe_high, 1)

                    def turned(g):
                        act.wait_ge(h_turned, i * PAIR_SLICES + (s0 + g + 1))
                        if g >= 2:
                            act.wait_ge(down_done, i * PAIR_SLICES + (s0 + g - 1 + CREDIT))
                        nc.scalar.activation(HTr[:, g % 2, 0, :], T[g % 2][:, :], ACT.Copy).then_inc(ht_hi, 1)

                    for n in range(PARTS):
                        split(n)
                    n = PARTS
                    for g in range(PAIR_SLICES):
                        if g == 0:
                            gathered(0)
                        split(n)
                        act.wait_ge(gate_full, i * PAIR_SLICES + (s0 + g + 1))
                        if g >= 2:
                            act.wait_ge(up_read, i * PAIR_SLICES + (s0 + g - 1))
                        nc.scalar.activation(SGE[:, g % 2, :], G[:, :], ACT.Silu).then_inc(gate_read, 1)
                        if g >= 1:
                            turned(g - 1)
                        if g == 5:
                            gathered(1)
                        more = 4 if g == 0 or g == PAIR_SLICES - 1 else 6
                        for m in range(n + 1, n + more):
                            split(m)
                        n += more
                    turned(PAIR_SLICES - 1)

            act.dma_start(routw[:, :, :], io["router_w"][0].rearrange("(k p) e -> p k e", p=P)).then_inc(router_in, 16)
            att_base = 0
            for layer in range(DEPTH):
                tiles = tiles_of(layer)
                nt = len(tiles)
                if layer == 0:
                    small_loads(0)
                    act.wait_ge(c_in, 32)
                    nc.scalar.activation(condf[:, :, :], cload[:, :, :].rearrange("p s k -> p k s"), ACT.Silu).then_inc(cond_f, 1)
                    act.wait_ge(cond_f, 1)
                    nc.scalar.activation(cond[:, :, 0:2], condf[:, :, :], ACT.Copy).then_inc(cond_hi, 1)
                    split_to(3)
                    act.wait_ge(x_in, 32)
                else:
                    after(x_ready)
                    small_loads(1)
                squares(range(NT))
                after(dneg_ready)
                step(nc.scalar.activation(dln[:, :, :], dneg[:, :, :], ACT.Exp))
                nc.scalar.activation(dln[:, :, :], dln[:, :, :], ACT.Ln, bias=1.0).then_inc(dln_ready, 1)
                A, W = first["ada", layer], first["in", layer]
                for s in range(12):
                    split_to(min(A + 2 * s + 5, W + 2))
                after(mod_ready)
                modulate(0, 1)
                high_parts((0, 1))
                after(dexp_in)
                nc.scalar.activation(decay, decay, ACT.Exp).then_inc(dexp_out, 1)
                nc.scalar.activation(dtok[:, :, :, :, :], dtok[:, :, :, :, :], ACT.Exp).then_inc(dexp_out, 1)
                for s, (a, b_) in enumerate(IN_SLICES[:-1]):
                    split_to(W + 2 * s + 3)
                    for t in (range(NT) if layer == 0 or b_ <= C_Q else range(TT)):
                        if t % 2:
                            copy_out(proj[:, t, a:b_], take()[:, 0:b_ - a])
                    split_to(W + 2 * s + 4)
                split_to(W + 11)
                ncol = SEQ * (2 if layer == 0 else 1)
                for ct in range(2):
                    nc.scalar.activation(SC[:, ct, 0:ncol], take()[:, 0:ncol], ACT.Sigmoid).then_inc(a_done, 1)
                split_to(W + 12)
                act.wait_ge(v_done, job[("in", layer, C_RQ, tiles[-1] - 1)] + 1)
                act.wait_ge(a_done, job[("in", layer, C_RQ, tiles[-1])] + 1)
                gates = proj[:, 0:nt, C_RG:C_CONV]
                nc.scalar.activation(gates, gates, ACT.Silu).then_inc(rg_ready, 1)
                for t in tiles:
                    copy_out(AQT[:, :, t, :], take()[:, :].rearrange("p (r n) -> p r n", r=4))
                for s in ((0, 1) if layer == 0 else (0,)):
                    for t in range(TT):
                        copy_out(RO[:, s * TT + t, :], take()[:, 0:256])
                attention(layer, att_base + NT)
                att_base += NT + 8 * nt
                after(ln_ready)
                nc.scalar.activation(gates, CV[:, 0:nt, :], ACT.Silu).then_inc(act_mix, 1)
                for t in tiles:
                    for half in range(2):
                        n = job[("mix", layer, t, half)]
                        act.wait_ge(v_full, n + 1)
                        nc.scalar.activation(hTr[:, 0, 4 * half:4 * half + 4, t * P:(t + 1) * P],
                                             VB[n % len(VB)][:, :].rearrange("p (k n) -> p k n", k=4), ACT.Copy).then_inc(mix_hi, 1)
                gate_rows(GB, (0, 1) if layer == 0 else (0,))
                O = first["out", layer]
                split_to(O + 4 if layer else O + 7)
                after(x_ready)
                squares(tiles)
                if layer == 0:
                    modulate(1, 1)
                    high_parts((0, 1))
                    n = first["ffn"] + 3

                    def hidden_high(f):
                        act.wait_ge(v_done, job[("up", f)] + 1)
                        nc.scalar.activation(HFr[:, 0, f % HALF_FF, :], HF[:, f % 2, :], ACT.Copy).then_inc(ff_hi, 1)

                    for p0 in range(0, FF_TILES, HALF_FF):
                        for f in range(p0, p0 + HALF_FF):
                            b = take()
                            if f >= 2:
                                act.wait_ge(v_done, job[("up", f - 2)] + 1)
                            nc.scalar.activation(SG[:, f % 2, :], b[:, :], ACT.Silu).then_inc(a_done, 1)
                            if f > p0:
                                hidden_high(f - 1)
                            n += 1
                            split_to(n)
                        hidden_high(p0 + HALF_FF - 1)
                        if p0 == 0:
                            gate_rows(GB, (0, 1))
                        for _ in range(2 * len(ff_split)):
                            n += 1
                            split_to(n)
            after(lexp_in)
            nc.scalar.activation(best[:, 3, :], best[:, 2, :], ACT.Exp).then_inc(lexp_out, 1)
            gate_rows(GBX[:, :].rearrange("p (s n) -> p s n", s=1), (0,))
            experts(0)
            after(most_ready)
            over = act.value_load(mosti[0:1, 0:1], min_val=0, max_val=SEQ)
            with act.If(over > P):
                experts(1)

        @block.gpsimd
        def _(pool):
            after = counter(pool)
            step = stepper(pool, p_step)

            def rsqrt(out, mid, src, scale):
                step(nc.gpsimd.tensor_scalar(mid, src, scale, EPS, ALU.mult, ALU.add))
                return nc.gpsimd.tensor_tensor(out, mid, nhalf[:, 0:out.shape[1]], ALU.pow)

            step(nc.gpsimd.memset(nhalf[:, :], -0.5))
            for layer in range(DEPTH):
                nt = len(tiles_of(layer))
                if layer:
                    after(x_ready)
                after(sq_ready, NT)
                rsqrt(rstd[:, :], lnt[:, 0:NT], ssq[:, :], 1.0 / D_MODEL).then_inc(rstd_ready, 1)
                pool.wait_ge(lo_ready, first["in", layer])
                nc.gpsimd.memset(CB, 0.0).then_inc(pad_ready, 1)
                for t in range(NT):
                    lo = 0 if t in tiles_of(layer) else 8
                    after(qss_ready)
                    rsqrt(qrs[:, t, lo:], qst[:, t, lo:], qss[:, t, lo:], 1.0 / HEAD_DIM).then_inc(qrs_ready, 1)
                after(dexp_out, 2)
                pool.wait_ge(v_done, job[("in", layer, 384, 2)] + 1)
                pool.wait_ge(a_done, job[("in", layer, 384, 3)] + 1)
                for t in range(TT):
                    val = proj[:, TT + t, C_RV:C_RV + 256].rearrange("p (h e) -> p h e", h=RET_HEADS)
                    for d in range(2):
                        ins = nc.gpsimd.tensor_tensor(VW[:, t, :, d, :], val,
                                                      dtok[:, 0, t, :, d].unsqueeze(2).broadcast_to([P, RET_HEADS, HEAD_DIM]),
                                                      ALU.mult)
                    ins.then_inc(vw_ready, 1)
                after(ro_var)
                rsqrt(lnr[:, 0:4 * nt], lnt[:, 0:4 * nt], lnv[:, 0:4 * nt], 1.0 / HEAD_DIM).then_inc(ro_rstd, 1)
                after(cv_var)
                rsqrt(lnr[:, 0:nt], lnt[:, 0:nt], bag[:, 0:nt, 1], 1.0).then_inc(cv_rstd, 1)
                after(x_ready)
                after(sq_ready, nt)
                rsqrt(rstd[:, 0:nt], lnt[:, 0:nt], ssq[:, 0:nt], 1.0 / D_MODEL).then_inc(rstd_ready, 1)

        @block.vector
        def _(dve):
            after = counter(dve)
            step = stepper(dve, v_step)
            n_v = [0]
            x_count = [0]
            n_lo = [0]

            def split_to(stop):
                while n_lo[0] < stop:
                    n = n_lo[0]
                    n_lo[0] += 1
                    _, k, width, r, s = items[n]
                    dve.wait_ge(hi_ready, n + 1)
                    nc.vector.tensor_tensor(parts[:, s, 1, 0:k * width], raw[:, r, 0:k * width], parts_f[:, s, 0, 0:k * width],
                                            ALU.subtract).then_inc(lo_ready, 1)

            def low_parts(streams):
                for s in streams:
                    after(h_hi)
                    c = slice(s * SEQ, (s + 1) * SEQ)
                    tt(hTr[:, 1, :, c], hTf[:, :, c], hTr_f[:, 0, :, c], ALU.subtract).then_inc(h_lo, 1)

            def take():
                n = n_v[0]
                n_v[0] += 1
                dve.wait_ge(v_full, n + 1)
                return VB[n % len(VB)]

            def emptied():
                dve.wait_ge(v_done, n_v[0])

            def tt(out, a, b, op):
                return nc.vector.tensor_tensor(out, a, b, op)

            def copy_out(out, src):
                nc.vector.tensor_copy(out, src).then_inc(v_done, 1)

            def per_group(v, width):
                return v.unsqueeze(2).broadcast_to([P, v.shape[1], width])

            def ada_columns(layer):
                A, W = first["ada", layer], first["in", layer]
                split_to(A + 3)
                after(bias_in, 16)
                for s in range(12):
                    split_to(min(A + 2 * s + 4, W + 2))
                    part = row[:, s * SLICE:(s + 1) * SLICE]
                    tt(part, take()[0:4, :], part, ALU.add).then_inc(v_done, 1)
                    split_to(min(A + 2 * s + 5, W + 2))
                b = take()
                nc.vector.tensor_copy(vcols[:, :], b[:, 96:96 + 2 * KT + 2])
                copy_out(ada[:, :, :], b[:, 0:96].rearrange("p (c s) -> p c s", s=2))
                emptied()
                for which in range(2):
                    c = (1 + 3 * which) * KT
                    ins = nc.vector.scalar_tensor_tensor(scl[:, which, :, :], ada[:, c:c + KT, :], 1.0,
                                                         vcols[:, which * KT:(which + 1) * KT].unsqueeze(2).broadcast_to([P, KT, 2]), ALU.add, ALU.mult)
                ins.then_inc(mod_ready, 1)

            def normalize(which, tiles):
                after(rstd_ready)
                for t in tiles:
                    nc.vector.tensor_scalar(xn[:, t, :], X[:, t, :], rstd[:, t:t + 1], None, ALU.mult).then_inc(xn_ready, 1)
                for kp in range(KT // 2):
                    b = take()
                    for kk in range(2):
                        k = 2 * kp + kk
                        ins = nc.vector.tensor_scalar(hTf[:, k, 0:SEQ], b[:, kk * SEQ:(kk + 1) * SEQ], scl[:, which, k, 0:1],
                                                      ada[:, 3 * which * KT + k, 0:1], ALU.mult, ALU.add)
                    ins.then_inc(v_done, 1)

            def decay_arguments():
                after(dln_ready)
                step(tt(dneg[:, :, :], dmin[:, :, :], dln[:, :, :], ALU.subtract))
                for h in range(RET_HEADS):
                    ins = nc.vector.tensor_scalar(decay[:, h, :], ahead, dneg[:, h, 0:1], None, ALU.mult)
                step(ins)
                for h in range(RET_HEADS):
                    nc.vector.scalar_tensor_tensor(decay[:, h, :], behind, dneg[:, h, 1:2], decay[:, h, :], ALU.mult, ALU.add)
                for h in range(RET_HEADS):
                    ins = tt(dtok[:, :, :, h, :].rearrange("p w t d -> p (w t) d"), expo,
                             dneg[:, h, :].unsqueeze(1).broadcast_to([P, 4, 2]), ALU.mult)
                ins.then_inc(dexp_in, 1)

            def head_squares(layer, t):
                if t % 2:
                    dve.wait_ge(a_done, job[("in", layer, 0, t)] + 1)
                lo = 8
                if t in tiles_of(layer):
                    lo = 0
                    q = proj[:, t, C_Q:C_RQ].rearrange("p (g r d) -> p g r d", g=2, d=HEAD_DIM)
                    tt(TMP[:, 0:512].rearrange("p (r g d) -> p g r d", g=2, d=HEAD_DIM), q, q, ALU.mult)
                k = proj[:, t, C_K:C_V]
                step(tt(TMP[:, 512:640], k, k, ALU.mult))
                nc.vector.tensor_reduce(qss[:, t, lo:], TMP[:, 64 * lo:640].rearrange("p (h d) -> p h d", d=HEAD_DIM),
                                        AX.X, ALU.add).then_inc(qss_ready, 1)

            def head_norm(layer, t):
                after(qrs_ready)
                if t in tiles_of(layer):
                    for g in range(2):
                        tt(QK[:, t, g:8:2, :], proj[:, t, C_Q + 256 * g:C_Q + 256 * g + 256].rearrange("p (r d) -> p r d", d=HEAD_DIM),
                           per_group(qrs[:, t, g:8:2], HEAD_DIM), ALU.mult)
                step(tt(QK[:, t, 8:10, :], proj[:, t, C_K:C_V].rearrange("p (h d) -> p h d", d=HEAD_DIM),
                        per_group(qrs[:, t, 8:10], HEAD_DIM), ALU.mult))
                if t in tiles_of(layer):
                    tt(QK[:, t, 0:8, :], QK[:, t, 0:8, :], qkw[:, 0, :].unsqueeze(1).broadcast_to([P, 8, HEAD_DIM]), ALU.mult)
                last = tt(QK[:, t, 8:10, :], QK[:, t, 8:10, :], qkw[:, 1, :].unsqueeze(1).broadcast_to([P, 2, HEAD_DIM]), ALU.mult)
                if t < TT:
                    step(last)
                    a_ = TMP[:, 0:640].rearrange("p (h d) -> p h d", d=HEAD_DIM)
                    b_ = TMP[:, 640:1280].rearrange("p (h a f) -> p h a f", a=2, f=32)
                    tt(a_, QK[:, t, :, :], cos64[:, t, :].unsqueeze(1).broadcast_to([P, 10, HEAD_DIM]), ALU.mult)
                    q4 = QK[:, t, :, :].rearrange("p h (a f) -> p h a f", a=2)
                    for half in range(2):
                        ins = tt(b_[:, :, :, 16 * half:16 * half + 16], q4[:, :, :, 16 - 16 * half:32 - 16 * half],
                                 sin64[:, t, :, half, :].unsqueeze(1).broadcast_to([P, 10, 2, 16]), ALU.mult)
                    step(ins)
                    last = tt(QK[:, t, :, :], a_, TMP[:, 640:1280].rearrange("p (h d) -> p h d", d=HEAD_DIM), ALU.add)
                last.then_inc(qk_ready, 1)
                dve.wait_ge(qk_ready, NT * layer + t + 1)

            def projections(layer):
                W = first["in", layer]
                for n, (a, b_) in enumerate(IN_SLICES[:-1]):
                    split_to(W + 2 * n + 3)
                    for t in (range(NT) if layer == 0 or b_ <= C_Q else range(TT)):
                        if t % 2 == 0:
                            copy_out(proj[:, t, a:b_], take()[:, 0:b_ - a])
                    split_to(W + 2 * n + 4)
                    if n == 1:
                        emptied()
                        for t in range(TT):
                            head_squares(layer, t)
                            head_norm(layer, t)
                    if n == 2:
                        emptied()
                        for t in range(TT, NT):
                            head_squares(layer, t)
                            head_norm(layer, t)
                after(pad_ready)
                ns = 2 if layer == 0 else 1
                split_to(W + 11)
                for ct in range(2):
                    b = take()
                    dve.wait_ge(a_done, job[("conv_gate", layer, ct)] + 1)
                    tt(CB[:, ct, 0:ns, CONV_WIDTH // 2:CONV_WIDTH // 2 + SEQ], b[:, 0:ns * SEQ].rearrange("p (s n) -> p s n", s=ns),
                       SC[:, ct, 0:ns * SEQ].rearrange("p (s n) -> p s n", s=ns), ALU.mult).then_inc(v_done, 1)
                split_to(W + 12)

            def retention(layer, base):
                tiles = tiles_of(layer)
                copy_out(convw[:, :, :], take()[:, 0:64].rearrange("p (c k) -> p c k", c=2)[:, :, 0:CONV_WIDTH])
                for t in tiles:
                    copy_out(RT[:, :, t, :], take()[:, :].rearrange("p (b n) -> p b n", b=4))
                after(dexp_out, 2)
                nc.vector.tensor_scalar(dec[:, :], dec[:, :], HEAD_DIM ** -0.5, None, ALU.mult)
                read = dtok[:, 1, :, :, :]
                step(nc.vector.tensor_scalar(read, read, HEAD_DIM ** -0.5, None, ALU.mult))
                dve.wait_ge(att_done, base)
                after(mask_in, 16)
                nc.vector.tensor_copy(AKT, OB[:, :]).then_inc(att_read, 1)
                b = take()
                step(nc.vector.memset(ST, 0.0))
                nc.vector.tensor_copy(ST[0:64, :, 0:P], b[0:64, :].rearrange("p (c n) -> p c n", c=2)[:, :, 0:P])
                copy_out(ST[64:128, :, P:2 * P], b[64:128, :].rearrange("p (c n) -> p c n", c=2)[:, :, P:2 * P])
                for s in ((0, 1) if layer == 0 else (0,)):
                    if s:
                        dve.wait_ge(a_full, job[("inner", layer, 0)] + 2)
                    for h in range(RET_HEADS):
                        tt(AD[:, h, :], take()[:, :], decay[:, h, :], ALU.mult).then_inc(v_done, 1)
                dve.wait_ge(a_done, job[("inner", layer, 0)] + 2)
                cross = RW.rearrange("p t c -> p (t c)").rearrange("p (t g n) -> p t g n", t=TT, g=8)
                for t in range(TT):
                    tt(cross[:, t, :, :], take()[:, :].rearrange("p (g n) -> p g n", g=8),
                       per_group(dtok[:, 1, t, :, :].rearrange("p h d -> p (h d)"), HEAD_DIM), ALU.mult).then_inc(v_done, 1)
                emptied()
                for d in range(2):
                    for t in range(TT):
                        out = RO[:, t, :].rearrange("p (h n) -> p h n", h=RET_HEADS)
                        ins = tt(out, out, cross[:, t, d:8:2, :], ALU.add)
                    step(ins)

            def readout(layer):
                nt = len(tiles_of(layer))
                if layer == 0:
                    dve.wait_ge(a_done, job[("inner", layer, 1)] + 2)
                o = RO[:, 0:nt, :].rearrange("p t (h n) -> p (t h) n", h=RET_HEADS)
                w = RW[:, 0:nt, :].rearrange("p t (h n) -> p (t h) n", h=RET_HEADS)
                g = 4 * nt
                step(nc.vector.tensor_reduce(lnm[:, 0:g], o, AX.X, ALU.add))
                step(nc.vector.tensor_scalar(lnm[:, 0:g], lnm[:, 0:g], -1.0 / HEAD_DIM, None, ALU.mult))
                step(tt(o, o, per_group(lnm[:, 0:g], HEAD_DIM), ALU.add))
                step(tt(w, o, o, ALU.mult))
                nc.vector.tensor_reduce(lnv[:, 0:g], w, AX.X, ALU.add).then_inc(ro_var, 1)
                after(ro_rstd)
                step(tt(o, o, per_group(lnr[:, 0:g], HEAD_DIM), ALU.mult))
                r = RO[:, 0:nt, :]
                step(tt(r, r, gnw[:, :].unsqueeze(1).broadcast_to([P, nt, 256]), ALU.mult))
                after(rg_ready)
                step(tt(proj[:, 0:nt, C_RQ:C_RG], r, proj[:, 0:nt, C_RG:C_CONV], ALU.mult))

            def attention(layer, base):
                its = [(t, r, g) for t in tiles_of(layer) for r in range(4) for g in range(2)]
                ns = 2 if layer == 0 else 1
                per = -(-TAPS // len(its))

                def tap(c):
                    ct, k = c % 2, c // 2
                    src = CB[:, ct, 0:ns, k:k + SEQ]
                    acc = CA[:, ct, 0:ns, :]
                    if k == 0:
                        ins = nc.vector.tensor_scalar(acc, src, convw[:, ct, 0:1], vcols[:, 2 * KT + ct:2 * KT + ct + 1], ALU.mult, ALU.add)
                    else:
                        dve.wait_ge(tap_done, tap_base + c - 1)
                        ins = nc.vector.scalar_tensor_tensor(acc, src, convw[:, ct, k:k + 1], acc, ALU.mult, ALU.add)
                    ins.then_inc(tap_done, 1)

                tap_base = layer * TAPS
                for n in range(len(its) + 3):
                    if n < len(its):
                        t, r, g = its[n]
                        head, turn = g * 4 + r, (n // 8) % 2
                        k0 = 0 if t < TT else SEQ
                        b = take()
                        if n >= 4:
                            dve.wait_ge(a_full, job[("probs", layer, n - 4)] + 1)
                        nc.vector.tensor_tensor_reduce(SC[:, n % 4, k0:], b[:, k0:], mask[:, t % TT, k0:], 1.0, 3 * BIG_NEG,
                                                       ALU.add, ALU.max, mx[:, turn, head:head + 1]).then_inc(v_done, 1)
                        emptied()
                        nc.vector.tensor_scalar(negm[:, turn, head:head + 1], mx[:, turn, head:head + 1], -(HEAD_DIM ** -0.5),
                                                nsink[:, head:head + 1], ALU.mult, ALU.min).then_inc(negm_ready, 1)
                        if n % 8 == 7:
                            dve.wait_ge(negm_ready, layer_negm + n + 1)
                            tt(esink[:, turn, :], negm[:, turn, :], sink[:, :], ALU.add).then_inc(sarg_ready, 1)
                        for c in range(n * per, min((n + 1) * per, TAPS)):
                            tap(c)
                    if n == 3:
                        readout(layer)
                    if n >= 10 and (n - 10) % 8 == 0:
                        tile = (n - 10) // 8
                        turn = tile % 2
                        after(esink_ready)
                        step(tt(rsum[:, turn, :], rsum[:, turn, :], esink[:, turn, :], ALU.add))
                        step(nc.vector.reciprocal(rsum[:, turn, :], rsum[:, turn, :]))
                        dve.wait_ge(att_done, base + 8 * (tile + 1))
                        tt(proj[:, tile, C_Q:C_RQ].rearrange("p (h d) -> p h d", d=HEAD_DIM), OB[:, :].rearrange("p (h d) -> p h d", d=HEAD_DIM),
                           per_group(rsum[:, turn, :], HEAD_DIM), ALU.mult).then_inc(att_read, 1)

            def conv_norm(layer):
                nt = len(tiles_of(layer))
                for t in range(nt):
                    copy_out(CV[:, t, :], take()[:, 0:256])
                emptied()
                for t in range(nt):
                    ins = nc.vector.bn_stats(bst[:, t, :], CV[:, t, :])
                step(ins)
                for t in range(nt):
                    ins = nc.vector.bn_aggr(bag[:, t, :], bst[:, t, :])
                ins.then_inc(cv_var, 1)
                after(cv_rstd)
                for t in range(nt):
                    ins = nc.vector.tensor_scalar(CV[:, t, :], CV[:, t, :], bag[:, t, 0:1], lnr[:, t:t + 1], ALU.subtract, ALU.mult)
                step(ins)
                c = CV[:, 0:nt, :]
                step(tt(c, c, lnw[:, :].unsqueeze(1).broadcast_to([P, nt, 256]), ALU.mult))
                tt(c, c, lnb[:, :].unsqueeze(1).broadcast_to([P, nt, 256]), ALU.add).then_inc(ln_ready, 1)

            def add_gated(half, t, last):
                s = t // TT
                y = YG[:, t % 2, :]
                x = X[:, t, half * 512:(half + 1) * 512]
                tt(y, take()[:, :], GB[:, s, half * 512:(half + 1) * 512], ALU.mult).then_inc(v_done, 1)
                emptied()
                ins = tt(x, x, y, ALU.add)
                if last:
                    ins.then_inc(x_ready, 1)
                    x_count[0] += 1
                    dve.wait_ge(x_ready, x_count[0])

            def route():
                L, first, second, chosen = top[:, 1, :, :], top[:, 2, :, :], top[:, 3, :, :], top[:, 0, :, :]
                tmp, comb = top[:, 4, :, :], top[:, 5, :, :]
                idx = table("experts").unsqueeze(1).broadcast_to([P, TT, N_EXPERTS])
                copy_out(L, take()[:, 0:16].rearrange("p (t e) -> p t e", t=TT))
                emptied()

                def pick(value, mask_, at):
                    step(nc.vector.tensor_reduce(value, L, AX.X, ALU.max))
                    step(tt(tmp, L, per_group(value, N_EXPERTS), ALU.is_equal))
                    step(nc.vector.tensor_scalar(tmp, tmp, -64.0, 64.0, ALU.mult, ALU.add))
                    step(tt(tmp, tmp, idx, ALU.add))
                    step(nc.vector.tensor_reduce(at, tmp, AX.X, ALU.min))
                    return tt(mask_, idx, per_group(at, N_EXPERTS), ALU.is_equal)

                step(pick(best[:, 0, :], first, best[:, 4, :]))
                step(nc.vector.scalar_tensor_tensor(L, first, BIG_NEG, L, ALU.mult, ALU.add))
                step(pick(best[:, 1, :], second, best[:, 5, :]))
                tt(chosen, first, second, ALU.add).then_inc(mask_ready, 1)
                tt(best[:, 2, :], best[:, 1, :], best[:, 0, :], ALU.subtract).then_inc(lexp_in, 1)
                after(lexp_out)
                step(nc.vector.tensor_scalar(best[:, 6, :], best[:, 3, :], 1.0, None, ALU.add))
                step(nc.vector.reciprocal(best[:, 6, :], best[:, 6, :]))
                step(tt(best[:, 7, :], best[:, 6, :], best[:, 3, :], ALU.mult))
                step(tt(tmp, first, per_group(best[:, 6, :], N_EXPERTS), ALU.mult))
                step(tt(comb, second, per_group(best[:, 7, :], N_EXPERTS), ALU.mult))
                step(tt(comb, comb, tmp, ALU.add))
                b = take()
                nc.vector.tensor_reduce(most[:, 0:1], b[:, 16:24], AX.X, ALU.max)
                copy_out(top[:, 6, :, :], b[:, 0:16].rearrange("p (t e) -> p t e", t=TT))
                emptied()
                nc.vector.tensor_copy(mosti[:, :], most[:, 0:1]).then_inc(most_ready, 1)

            def place_tokens(part):
                rank, chosen, comb = top[:, 6, :, :], top[:, 0, :, :], top[:, 5, :, :]
                if part:
                    nc.vector.tensor_scalar(rank, rank, -float(P), None, ALU.add).then_inc(rank_moved, 1)
                    dve.wait_ge(rank_moved, 1)

                def weighted(e):
                    for i in range(2):
                        for t in range(TT):
                            ins = nc.vector.tensor_scalar(WR[:, (e // 2) % 2, i * TT + t, :], table("slots"),
                                                          rank[:, t, e + i:e + i + 1], comb[:, t, e + i:e + i + 1],
                                                          ALU.is_equal, ALU.mult)
                    ins.then_inc(scat_in, 1)

                weighted(0)
                for e in range(0, N_EXPERTS, 2):
                    if e + 2 < N_EXPERTS:
                        weighted(e + 2)
                    for i in range(2):
                        for t in range(TT):
                            nc.vector.tensor_scalar(PA[:, t, e + i, :], table("slots"), rank[:, t, e + i:e + i + 1],
                                                    chosen[:, t, e + i:e + i + 1], ALU.is_equal, ALU.mult)
                    copy_out(SA[:, e:e + 2, :], take()[:, :].rearrange("p (e n) -> p e n", e=2))
                emptied()

            def experts(part):
                U, Y, T, M = bank[1], bank[2:4], bank[4:6], bank[6:8]
                s0, e0 = part * N_EXPERTS * EF_SLICES, part * N_EXPERTS
                with dve.Fori(0, PAIRS) as i:
                    def split(n):
                        dve.wait_ge(hi_ready, i * PAIR_ITEMS + (BASE + part * PAIRS * PAIR_ITEMS + n + 1))
                        tt(parts[:, n % PARTS, 1, :], raw[:, n % RAW, :], parts_f[:, n % PARTS, 0, :], ALU.subtract)\
                            .then_inc(lo_ready, 1)

                    def turned(g):
                        dve.wait_ge(ht_hi, i * PAIR_SLICES + (s0 + g + 1))
                        tt(HTr[:, g % 2, 1, :], T[g % 2][:, :], HTr_f[:, g % 2, 0, :], ALU.subtract).then_inc(ht_ready, 1)

                    def gathered(ee):
                        dve.wait_ge(gather_full, i * 4 + (2 * (e0 + ee) + 2))
                        for k in range(4, KT):
                            ins = nc.vector.tensor_scalar(XF[:, k, :], M[1][:, (k - 4) * P:(k - 3) * P], scl[:, 1, k, 0:1],
                                                          ada[:, 3 * KT + k, 0:1], ALU.mult, ALU.add)
                        ins.then_inc(xe_hi, 1)
                        dve.wait_ge(xe_high, i * 2 + (e0 + ee + 1))
                        tt(XEr[:, ee, 1, :, :], XF, XEr_f[:, ee, 0, :, :], ALU.subtract).then_inc(xe_ready, 1)

                    def expert_out(ee):
                        dve.wait_ge(down_done, i * PAIR_SLICES + (s0 + EF_SLICES * (ee + 1) + CREDIT))
                        for h in range(2):
                            nc.vector.tensor_copy(YS[:, h * 512:(h + 1) * 512], Y[h][:, :]).then_inc(y_ready, 1)

                    def add_scattered(ee):
                        for t in range(TT):
                            for h in range(2):
                                n = 4 * (e0 + ee) + 2 * t + h
                                dve.wait_ge(scatter_full, i * 8 + (n + 1))
                                acc = ACC[:, t, h * 512:(h + 1) * 512]
                                tt(acc, M[h][:, :], acc, ALU.add).then_inc(scatter_read, 1)

                    for ee in range(2):
                        ins = nc.vector.tensor_copy(SCAT[:, ee, :], SA[:, bass.ds(i * 2 + ee, 1), :].rearrange("p e n -> p (e n)"))
                    ins.then_inc(st_ready, 1)
                    for n in range(PARTS):
                        split(n)
                    n = PARTS
                    for g in range(PAIR_SLICES):
                        if g == 0:
                            gathered(0)
                        split(n)
                        if g >= 1:
                            turned(g - 1)
                        if g == 5:
                            gathered(1)
                        split(n + 1)
                        split(n + 2)
                        dve.wait_ge(up_full, i * PAIR_SLICES + (s0 + g + 1))
                        dve.wait_ge(gate_read, i * PAIR_SLICES + (s0 + g + 1))
                        if g >= 2:
                            dve.wait_ge(h_turned, i * PAIR_SLICES + (s0 + g - 1))
                        tt(HE[:, g % 2, :], U[:, :], SGE[:, g % 2, :], ALU.mult).then_inc(up_read, 1)
                        if g == EF_SLICES + 1:
                            add_scattered(0)
                        more = 4 if g == 0 or g == PAIR_SLICES - 1 else 6
                        for m in range(n + 3, n + more):
                            split(m)
                        n += more
                        if g == EF_SLICES:
                            expert_out(0)
                    turned(PAIR_SLICES - 1)
                    expert_out(1)
                    add_scattered(1)

            def clear_rows():
                nc.vector.memset(row, 0.0).then_inc(row_clear, 1)

            clear_rows()
            dve.wait_ge(cond_hi, 1)
            tt(cond[:, :, 2:4], condf[:, :, :], cond[:, :, 0:2].bitcast(F32), ALU.subtract).then_inc(cond_ready, 1)
            dve.wait_ge(tables_in, 16)
            att_base = 0
            for layer in range(DEPTH):
                tiles = tiles_of(layer)
                layer_negm = 0 if layer == 0 else 8 * NT
                if layer:
                    clear_rows()
                after(small_in, 16 * N_SMALL)
                nc.vector.tensor_scalar(nsink[:, :], sink[:, :], -1.0, None, ALU.mult)
                logit = dlog[:, :, :].rearrange("p d h -> p h d")
                nc.vector.tensor_scalar(dmin[:, :, :], logit, 0.0, None, ALU.min)
                nc.vector.scalar_tensor_tensor(dneg[:, :, :], logit, -1.0, logit, ALU.mult, ALU.min)\
                    .then_inc(dneg_ready, 1)
                ada_columns(layer)
                normalize(0, range(NT))
                low_parts((0, 1))
                decay_arguments()
                projections(layer)
                retention(layer, att_base + NT)
                attention(layer, att_base + NT)
                att_base += NT + 8 * len(tiles)
                conv_norm(layer)
                for t in tiles:
                    for half in range(2):
                        k = slice(4 * half, 4 * half + 4)
                        tok = slice(t * P, (t + 1) * P)
                        b = take()
                        after(mix_hi)
                        tt(hTr[:, 1, k, tok], b[:, :].rearrange("p (k n) -> p k n", k=4), hTr_f[:, 0, k, tok], ALU.subtract)\
                            .then_inc(v_done, 1)
                O = first["out", layer]
                for half in range(2):
                    split_to(O + 2 * half + 3 if half == 0 or layer == 0 else O + 4)
                    for t in tiles:
                        add_gated(half, t, half == 1 and t == tiles[-1])
                    if half == 0:
                        split_to(O + 4)
                if layer == 0:
                    split_to(O + 7)
                normalize(1, tiles)
                if layer == 0:
                    low_parts((0, 1))
                    n = first["ffn"] + 3

                    def hidden_low(f):
                        after(ff_hi)
                        tt(HFr[:, 1, f % HALF_FF, :], HF[:, f % 2, :], HFr_f[:, 0, f % HALF_FF, :], ALU.subtract).then_inc(ff_lo, 1)

                    for p0 in range(0, FF_TILES, HALF_FF):
                        for f in range(p0, p0 + HALF_FF):
                            b = take()
                            dve.wait_ge(a_done, job[("gate", f)] + 1)
                            if f >= 2:
                                dve.wait_ge(ff_lo, f - 1)
                            tt(HF[:, f % 2, :], b[:, :], SG[:, f % 2, :], ALU.mult).then_inc(v_done, 1)
                            if f > p0:
                                hidden_low(f - 1)
                            n += 1
                            split_to(n)
                        hidden_low(p0 + HALF_FF - 1)
                        for half in range(2):
                            for j in range(len(ff_split)):
                                if j == len(ff_split) - 1:
                                    for t in tiles:
                                        add_gated(half, t, p0 > 0 and half == 1 and t == tiles[-1])
                                n += 1
                                split_to(n)
            route()
            place_tokens(0)
            nc.vector.memset(ACC_t[:, :], 0.0).then_inc(scatter_read, 1)
            experts(0)
            dve.wait_ge(most_ready, 1)
            over = dve.value_load(mosti[0:1, 0:1], min_val=0, max_val=SEQ)
            with dve.If(over > P):
                place_tokens(1)
                experts(1)
            for t in range(TT):
                step(tt(ACC[:, t, :], ACC[:, t, :], GBX[:, :], ALU.mult))
                tt(X[:, t, :], X[:, t, :], ACC[:, t, :], ALU.add).then_inc(out_ready, 1)


_INS = ['x', 'c', 'ctx', 'c_ctx', 'ada_w', 'ada_b', 'norm1_w', 'norm2_w', 'w_in', 'w_out', 'q_norm_w', 'k_norm_w',
        'attn_sink', 'ret_decay_f', 'ret_decay_b', 'ret_gn_w', 'conv_w', 'conv_b', 'conv_ln_w', 'conv_ln_b',
        'ffn_w_gate', 'ffn_w_up', 'ffn_w_down', 'router_w', 'moe_w_gate', 'moe_w_up', 'moe_w_down']


def kernel(**inputs):
    import numpy as _np
    import concourse.bacc as _bacc
    from concourse import mybir as _mybir
    from concourse.bass_utils import run_bass_kernel_spmd as _run

    nc = _bacc.Bacc("TRN2", target_bir_lowering=False, num_devices=1)
    arrays, io = {}, {}
    tables, place = shape_constants()
    for name in _INS + ['shape_tables']:
        a = tables if name == 'shape_tables' else _np.ascontiguousarray(inputs[name])
        arrays[f"in_{name}_dram"] = a
        io[name] = nc.dram_tensor(f"in_{name}_dram", a.shape, _mybir.dt.from_np(a.dtype), kind="ExternalInput").ap()
    io["out"] = nc.dram_tensor("out_0_dram", (1, SEQ, D_MODEL), _mybir.dt.float32, kind="ExternalOutput").ap()
    build(nc, io, place)
    r = _run(nc, [arrays], core_ids=[0])
    return r.results[0]["out_0_dram"]
```

```python
from contextlib import ExitStack

import concourse.bass as bass
from concourse import mybir

ALU = mybir.AluOpType
ACT = mybir.ActivationFunctionType
AX = mybir.AxisListType
F32 = mybir.dt.float32
F32R = mybir.dt.float32r
I32 = mybir.dt.int32

P = 128
D_MODEL, SEQ, CTX_LEN, DEPTH = 1024, 256, 256, 2
HEAD_DIM, Q_HEADS, KV_HEADS, RET_HEADS = 64, 8, 2, 4
CONV_CH, CONV_WIDTH = 256, 31
D_FF, N_EXPERTS, D_FF_EXPERT = 2816, 8, 3584
GRID_W, ROPE_BASE, WINDOW = 64, 10000.0, 128
EPS = 1e-6

KT = D_MODEL // P
TT = SEQ // P
NT = 2 * TT
C_K, C_V, C_RK, C_RV, C_Q, C_RQ, C_RG, C_CONV, IN_COLS = 0, 128, 256, 512, 768, 1280, 1536, 1792, 2304
PCOLS = C_CONV
SLICE = 512
ITEM = KT * SLICE // 2
RAW = 4
PARTS = 4
FF_TILES = D_FF // P
EF_SLICES = D_FF_EXPERT // SLICE
PAIRS = N_EXPERTS // 2
PAIR_SLICES = 2 * EF_SLICES
PAIR_ITEMS = 6 * PAIR_SLICES
GATHERS = N_EXPERTS + 1
HALF_FF = FF_TILES // 2
ADA_SLICES = 6 * D_MODEL // SLICE
ADA_ROWS = 4 * ADA_SLICES
ADA_ITEMS = 2 * ADA_SLICES
COND_PAD = ADA_ROWS - 4
RO_TAP = (12, 12)
CREDIT = 2
BIG_NEG = -1.0e30
N_SMALL = 12


def shape_constants():
    import numpy as np

    part = np.arange(P)
    out = {}
    out["identity"] = np.eye(P)
    mask = np.zeros((P, TT, 2 * SEQ))
    for t in range(TT):
        far = np.abs((t * P + part)[:, None] - np.arange(SEQ)[None, :]) > WINDOW
        mask[:, t, :SEQ][far] = BIG_NEG
    out["mask"] = mask.reshape(P, -1)
    freqs = (ROPE_BASE ** (-np.arange(16, dtype=np.float32) / np.float32(16))).astype(np.float32)
    pos = np.arange(SEQ)
    ang = np.stack([(pos // GRID_W).astype(np.float32)[:, None] * freqs,
                    (pos % GRID_W).astype(np.float32)[:, None] * freqs], axis=1)
    cos, sin = np.cos(ang), np.sin(ang)
    c64 = np.stack([cos, cos], axis=2).reshape(TT, P, 64)
    s64 = np.stack([-sin, sin], axis=2).reshape(TT, P, 64)
    out["cos"] = c64.transpose(1, 0, 2).reshape(P, -1)
    out["sin"] = s64.transpose(1, 0, 2).reshape(P, -1)
    j = (np.arange(TT) * P)[None, :, None] + part[:, None, None]
    i = np.arange(SEQ)[None, None, :]
    out["ahead"] = np.maximum(i - j, 0).reshape(P, -1)
    out["behind"] = np.maximum(j - i, 0).reshape(P, -1)
    tok = (np.arange(TT) * P)[None, :] + part[:, None]
    e = np.stack([np.stack([SEQ - 1 - tok, tok], -1), np.stack([tok + 1, SEQ - tok], -1)], 1)
    out["exponents"] = e.reshape(P, -1)
    out["before"] = (part[:, None] < part[None, :]) * 1.0
    out["ones"] = np.ones((P, P))
    fold = np.zeros((P, ADA_SLICES, 2))
    for s in range(ADA_SLICES):
        for r in range(4):
            fold[4 * s + r, s, r % 2] = 1.0
        fold[4 * ADA_SLICES + s, s, :] = 1.0
    out["fold"] = fold.reshape(P, -1)
    out["slots"] = np.tile(np.arange(P), (P, 1))
    out["experts"] = np.tile(np.arange(N_EXPERTS), (P, 1))
    out["mask"] = out.pop("mask")
    at, places = 0, {}
    for name, a in out.items():
        places[name] = (at, a.shape[1])
        at += a.shape[1]
    return np.concatenate([a.astype(np.float32) for a in out.values()], axis=1), places


def build(nc, io, place):
    ctx = ExitStack()
    with ctx:
        def sb(name, shape, dt=F32):
            return ctx.enter_context(nc.sbuf_tensor(name, shape, dt))

        def sem(name):
            return ctx.enter_context(nc.semaphore(name))

        def phase(*tensors):
            guards = [nc.sbuf_tensor(name, [P, n], dt) for name, n, dt in tensors]
            handles = [g.__enter__() for g in guards]
            for g in reversed(guards):
                g.__exit__(None, None, None)
            return handles

        X = sb("X", [P, NT, D_MODEL])
        nconst = place["mask"][0]
        const = sb("const", [P, nconst])
        ada = sb("ada", [P, 48, 2])
        scl = sb("scl", [P, 2, KT, 2])
        cload = sb("cload", [P, 2, KT])
        condf = sb("condf", [P, KT, 2])
        vrows = sb("vrows", [2 * KT + 2, P])
        vcols = sb("vcols", [P, 2 * KT + 2])
        convwr = sb("convwr", [CONV_WIDTH, CONV_CH])
        convw = sb("convw", [P, 2, CONV_WIDTH])
        routw = sb("routw", [P, KT, N_EXPERTS])
        qkw = sb("qkw", [P, 2, HEAD_DIM])
        sink = sb("sink", [P, Q_HEADS])
        nsink = sb("nsink", [P, Q_HEADS])
        dlog = sb("dlog", [P, 2, RET_HEADS])
        dneg = sb("dneg", [P, RET_HEADS, 2])
        dmin = sb("dmin", [P, RET_HEADS, 2])
        dln = sb("dln", [P, RET_HEADS, 2])
        dtok = sb("dtok", [P, 2, TT, RET_HEADS, 2])
        gnw = sb("gnw", [P, 256])
        lnw = sb("lnw", [P, 256])
        lnb = sb("lnb", [P, 256])
        ssq = sb("ssq", [P, NT])
        rstd = sb("rstd", [P, NT])
        qss = sb("qss", [P, NT, 10])
        qrs = sb("qrs", [P, NT, 10])
        nhalf = sb("nhalf", [P, 16])
        mx = sb("mx", [P, 2, Q_HEADS])
        negm = sb("negm", [P, 2, Q_HEADS])
        rsum = sb("rsum", [P, 2, Q_HEADS])
        esink = sb("esink", [P, 2, Q_HEADS])
        lnm = sb("lnm", [P, 16])
        lnv = sb("lnv", [P, 16])
        lnr = sb("lnr", [P, 16])
        bst = sb("bst", [P, NT, 6])
        bag = sb("bag", [P, NT, 2])
        lnt = sb("lnt", [P, 16])
        qst = sb("qst", [P, NT, 10])
        top = sb("top", [P, 7, TT, N_EXPERTS])
        best = sb("best", [P, 8, TT])
        most = sb("most", [P, 2])
        mosti = sb("mosti", [P, 1], I32)

        bank = [ctx.enter_context(nc.psum_tensor(f"bank{i}", [P, 512], F32)) for i in range(8)]
        VB, AB, OB = bank[0:4], bank[4:7], bank[7]
        rows_bank = (OB, VB[3])

        def table(name):
            a, n = place[name]
            return const[:, a:a + n]

        ident = table("identity")
        cos64 = table("cos").rearrange("p (t k) -> p t k", t=TT)
        sin64 = table("sin").rearrange("p (t a h f) -> p t a h f", t=TT, a=2, h=2)
        ahead, behind = table("ahead"), table("behind")
        expo = table("exponents").rearrange("p (w d) -> p w d", d=2)

        KB = 256
        raw_t, parts_t = phase(("raw", 32 * KB, F32), ("parts", 64 * KB, F32R))
        cond_t, row_t = [None] * DEPTH, [None] * DEPTH
        for layer, cond_kb, row_kb in ((0, 80, 83), (1, 64, 27)):
            _, cond_t[layer] = phase((f"gap_cond{layer}", cond_kb * KB, F32), (f"cond{layer}", KT * (2 * COND_PAD + 4), F32R))
            _, row_t[layer] = phase((f"gap_row{layer}", row_kb * KB, F32), (f"row{layer}", SLICE, F32))
        CBW = SEQ + CONV_WIDTH - 1
        (_, AD_t, CB_t, AKT, _, decay_t, SC_t, gb, PT_t, VW_t, hTr_t, proj_t, QK_t, RO_t, ST_t, mask_t) = phase(
            ("gap_ad", 16 * KB, F32), ("AD", 8 * KB, F32), ("CB", 4 * CBW + 4 + 4, F32), ("AKT", 2 * KB, F32),
            ("gap_decay", (64 - 24 - 2) * KB - (4 * CBW + 8), F32), ("decay", 8 * KB, F32), ("SC", 8 * KB, F32), ("gb", 8 * KB, F32),
            ("PT", 4 * KB, F32), ("VW", 4 * KB, F32), ("hTr", 32 * KB, F32R), ("proj", 28 * KB, F32),
            ("QK", 10 * KB, F32), ("RO", 4 * KB, F32), ("ST", 2 * KB, F32), ("mask", 4 * KB, F32))
        _, heads_t, _, hTf_t, _, xn_t = phase(
            ("gap_heads", 96 * KB, F32), ("heads", 16 * KB, F32), ("gap_hTf", 16 * KB, F32), ("hTf", 16 * KB, F32),
            ("gap_xn", 12 * KB, F32), ("xn", 16 * KB, F32))
        _, SG_t, YG_t, _, HFr_t, HF_t = phase(
            ("gap_sg", 88 * KB, F32), ("SG", 4 * KB, F32), ("YG", 4 * KB, F32), ("gap_hfr", 32 * KB, F32),
            ("HFr", 44 * KB, F32R), ("HF", 4 * KB, F32))
        _, XEr_t, HTr_t, SA_t, ACC_t, PA_t, XF_t, HE_t, SCAT_t, _, SGE_t, GBX, YS = phase(
            ("gap_e", 96 * KB, F32), ("XEr", 16 * KB, F32R), ("HTr", 8 * KB, F32R), ("SA", 8 * KB, F32),
            ("ACC", 8 * KB, F32), ("PA", 9 * KB, F32), ("XF", 4 * KB, F32), ("HE", 4 * KB, F32),
            ("SCAT", 2 * KB, F32), ("gap_e2", 9 * KB, F32), ("SGE", 4 * KB, F32), ("GBX", 4 * KB, F32), ("YS", 4 * KB, F32))

        raw = raw_t[:, :].rearrange("p (s n) -> p s n", s=RAW)
        parts = parts_t[:, :].rearrange("p (s two n) -> p s two n", s=PARTS, two=2)
        parts_f = parts_t[:, :].bitcast(F32).rearrange("p (s two n) -> p s two n", s=PARTS, two=2)
        row = [t[:, :] for t in row_t]
        cond = [t[:, :].rearrange("p (k c) -> p k c", k=KT) for t in cond_t]
        cond_f32 = [t[:, :].bitcast(F32).rearrange("p (k c) -> p k c", k=KT) for t in cond_t]
        AD = AD_t[:, :].rearrange("p (h k) -> p h k", h=RET_HEADS)
        CB = CB_t[:, 0:4 * CBW].rearrange("p (c s n) -> p c s n", c=2, s=2)
        AKT = AKT[:, :]
        dec = decay_t[:, :]
        decay = dec.rearrange("p (h k) -> p h k", h=RET_HEADS)
        SC = SC_t[:, :].rearrange("p (b k) -> p b k", b=4)
        CA = gb[:, 0:1024].rearrange("p (c s n) -> p c s n", c=2, s=2)
        RW = gb[:, 1024:2048].rearrange("p (t c) -> p t c", t=NT)
        GB = gb[:, :].rearrange("p (s n) -> p s n", s=2)
        PT = PT_t[:, :].rearrange("p (b k) -> p b k", b=2)
        VW = VW_t[:, :].rearrange("p (t h d e) -> p t h d e", t=TT, h=RET_HEADS, d=2)
        hTr = hTr_t[:, :].rearrange("p (two k c) -> p two k c", two=2, k=KT)
        hTr_f = hTr_t[:, :].bitcast(F32).rearrange("p (two k c) -> p two k c", two=2, k=KT)
        proj = proj_t[:, :].rearrange("p (t c) -> p t c", t=NT)
        QK = QK_t[:, :].rearrange("p (t h d) -> p t h d", t=NT, d=HEAD_DIM)
        CP = QK_t[:, 0:4 * SEQ].rearrange("p (b s n) -> p b s n", b=2, s=2)
        RO = RO_t[:, :].rearrange("p (t c) -> p t c", t=NT)
        ST = ST_t[:, :].rearrange("p (c n) -> p c n", c=2)
        mask = mask_t[:, :].rearrange("p (t k) -> p t k", t=TT)
        TMP = AD_t[:, 0:1280]
        AQT = heads_t[:, 0:2048].rearrange("p (r t n) -> p r t n", r=4, t=NT)
        RT = heads_t[:, 2048:4096].rearrange("p (b t n) -> p b t n", b=4, t=NT)
        CV = AD_t[:, 0:1024].rearrange("p (t c) -> p t c", t=NT)
        hTf = hTf_t[:, :].rearrange("p (k c) -> p k c", k=KT)
        xn = xn_t[:, :].rearrange("p (t c) -> p t c", t=NT)
        SG = SG_t[:, :].rearrange("p (b n) -> p b n", b=2)
        YG = YG_t[:, :].rearrange("p (b n) -> p b n", b=2)
        HF = HF_t[:, :].rearrange("p (b n) -> p b n", b=2)
        HFr = HFr_t[:, :].rearrange("p (two f n) -> p two f n", two=2, f=HALF_FF)
        HFr_f = HFr_t[:, :].bitcast(F32).rearrange("p (two f n) -> p two f n", two=2, f=HALF_FF)
        XEr = XEr_t[:, :].rearrange("p (b two k s) -> p b two k s", b=2, two=2, k=KT)
        XEr_f = XEr_t[:, :].bitcast(F32).rearrange("p (b two k s) -> p b two k s", b=2, two=2, k=KT)
        HTr = HTr_t[:, :].rearrange("p (b two n) -> p b two n", b=2, two=2)
        HTr_f = HTr_t[:, :].bitcast(F32).rearrange("p (b two n) -> p b two n", b=2, two=2)
        SA = SA_t[:, :].rearrange("p (e n) -> p e n", e=N_EXPERTS)
        ACC = ACC_t[:, :].rearrange("p (t c) -> p t c", t=TT)
        PA = PA_t[:, :].rearrange("p (t e s) -> p t e s", t=TT, e=GATHERS)
        XF = XF_t[:, :].rearrange("p (k s) -> p k s", k=KT)
        WR = XF_t[:, :].rearrange("p (b i s) -> p b i s", b=2, i=4)
        HE = HE_t[:, :].rearrange("p (b n) -> p b n", b=2)
        SCAT = SCAT_t[:, :].rearrange("p (b n) -> p b n", b=2)
        SGE = SGE_t[:, :].rearrange("p (b n) -> p b n", b=2)

        raw_loaded = [sem(f"raw_loaded{i}") for i in range(RAW)]
        hi_ready, lo_ready = sem("weights_high_ready"), sem("weights_low_ready")
        slot_used = sem("parts_used")
        cond_hi, cond_f = sem("cond_high_ready"), sem("cond_silu_ready")
        cond_clear = sem("cond_cleared")
        rows_full, rows_out, cols_full = sem("modulation_rows_full"), sem("modulation_rows_ready"), sem("modulation_columns_full")
        h_hi, h_lo = sem("h_high_ready"), sem("h_low_ready")
        mix_hi = sem("mix_high_ready")
        ff_hi, ff_lo = sem("ffn_high_ready"), sem("ffn_low_ready")
        xe_high, xe_ready = sem("gathered_parts_high"), sem("gathered_parts_ready")
        ht_hi = sem("hidden_transposed_high")
        gate_half, up_half, down_half = sem("gate_half"), sem("up_half"), sem("down_half")
        v_full, v_done = sem("vector_bank_full"), sem("vector_bank_evacuated")
        a_full, a_done = sem("scalar_bank_full"), sem("scalar_bank_evacuated")
        tables_in, x_in, c_in = sem("tables_in"), sem("x_in"), sem("c_in")
        mask_in = sem("mask_in")
        small_in, bias_in, router_in = sem("small_in"), sem("bias_in"), sem("router_in")
        cond_ready = sem("cond_ready")
        mod_ready = sem("modulation_ready")
        sq_ready, rstd_ready, xn_ready = sem("squares_ready"), sem("rstd_ready"), sem("normalized_ready")
        x_ready = sem("residual_ready")
        dneg_ready, dln_ready = sem("decay_arg_ready"), sem("decay_ln_ready")
        dexp_in, dexp_out = sem("decay_exponents_ready"), sem("decay_exp_ready")
        qss_ready, qrs_ready, qk_ready = sem("qk_squares_ready"), sem("qk_rstd_ready"), sem("qk_ready")
        vw_ready = sem("weighted_values_ready")
        pad_ready = sem("conv_pad_ready")
        negm_ready, exp_ready = sem("negmax_ready"), sem("exp_ready")
        sarg_ready, esink_ready = sem("sink_arg_ready"), sem("sink_exp_ready")
        att_done, att_read = sem("attention_products"), sem("attention_evacuated")
        ro_var, ro_rstd = sem("retention_variance_ready"), sem("retention_rstd_ready")
        cv_var, cv_rstd = sem("conv_variance_ready"), sem("conv_rstd_ready")
        ln_ready, rg_ready = sem("conv_norm_ready"), sem("retention_gate_ready")
        act_mix = sem("conv_silu_ready")
        out_ready = sem("output_ready")
        lexp_in, lexp_out = sem("gate_arg_ready"), sem("gate_exp_ready")
        mask_ready = sem("top2_masks_ready")
        scat_in = sem("scatter_rows_ready")
        most_ready = sem("most_tokens_ready")
        gate_full, gate_read = sem("gate_full"), sem("gate_silu_done")
        up_full, up_read = sem("up_full"), sem("up_multiplied")
        h_turned, ht_ready = sem("hidden_transposed"), sem("hidden_transposed_ready")
        down_done, y_ready = sem("down_done"), sem("expert_out_ready")
        gather_full, xe_lo, xe_hi = sem("gather_full"), sem("gathered_low_ready"), sem("gathered_high_ready")
        st_ready = sem("scatter_matrix_ready")
        scatter_full, scatter_read = sem("scatter_full"), sem("scatter_added")
        out_in = sem("out_stored")
        tap_done, pool_tap = sem("conv_tap_done"), sem("conv_tap_done_by_gpsimd")
        rank_moved = sem("rank_moved")
        v_step, a_step, p_step = sem("vector_step"), sem("scalar_step"), sem("gpsimd_step")

        block = ctx.enter_context(nc.Block())

        def counter(eng):
            seen = {}

            def after(s, n=1):
                seen[s] = seen.get(s, 0) + n
                eng.wait_ge(s, seen[s])
            return after

        def stepper(eng, s):
            n = [0]

            def step(ins):
                n[0] += 1
                ins.then_inc(s, 1)
                eng.wait_ge(s, n[0])
            return step

        def tiles_of(layer):
            return range(NT) if layer == 0 else range(TT)

        def cols(w, a, b, k0=0, k1=KT):
            return w[k0 * P:k1 * P, a:b].rearrange("(k p) n -> p k n", p=P)

        IN_SLICES = [(C_Q, C_RQ), (0, 384), (384, 768), (C_RQ, C_CONV), (C_CONV, IN_COLS)]
        HALVES = ((0, KT // 2), (KT // 2, KT))
        items = []
        first = {}
        ff_split = [(0, 4), (4, 8), (8, HALF_FF)]

        def ada_item(layer, h, r, s):
            w = io["ada_w"][layer][:, (h // 2) * SLICE:(h // 2 + 1) * SLICE].rearrange("(p k) n -> p k n", k=KT)
            k0, k1 = HALVES[h % 2]
            items.append(([w[:, k0:k1, :]], k1 - k0, SLICE, r, s))

        for layer in range(DEPTH):
            if layer == 0:
                for h in range(ADA_ITEMS):
                    ada_item(0, h, h % RAW, h % 3)
            first["in", layer] = len(items)
            n = 0
            for a, b in IN_SLICES:
                for k0, k1 in HALVES:
                    items.append(([cols(io["w_in"][layer], a, b, k0, k1)], k1 - k0, b - a, n % 2, (n + layer) % 2))
                    n += 1
            if layer == 0:
                first["ada", 1] = len(items)
                for h in range(ADA_ITEMS):
                    ada_item(1, h, h % 2, h % 2)
            first["out", layer] = len(items)
            for h in range(2):
                for k0, k1 in HALVES:
                    items.append(([cols(io["w_out"][layer], h * SLICE, (h + 1) * SLICE, k0, k1)],
                                  k1 - k0, SLICE, n % 2, (n + layer) % 2))
                    n += 1
            if layer == 0:
                first["ffn"] = len(items)
                n = 0
                for p0 in range(0, FF_TILES, HALF_FF):
                    for f in range(p0, p0 + HALF_FF):
                        items.append(([cols(io["ffn_w_gate"][0], f * P, (f + 1) * P), cols(io["ffn_w_up"][0], f * P, (f + 1) * P)],
                                      KT, 2 * P, n % 3, n % 3))
                        n += 1
                    for h in range(2):
                        for f0, f1 in ff_split:
                            items.append(([io["ffn_w_down"][0][(p0 + f0) * P:(p0 + f1) * P, h * SLICE:(h + 1) * SLICE]
                                           .rearrange("(k p) n -> p k n", p=P)], f1 - f0, SLICE, n % 3, n % 3))
                            n += 1
                assert n % 3 == 1
        BASE = len(items)
        loads_before = [sum(len(it[0]) for it in items if it[3] == s) for s in range(RAW)]

        order = []
        for g in range(PAIR_SLICES):
            order += [("gate", 0, g), ("gate", 1, g), ("up", 0, g), ("up", 1, g)]
            order += [("down", 0, g - 1), ("down", 1, g - 1)] if g else []
        order += [("down", 0, PAIR_SLICES - 1), ("down", 1, PAIR_SLICES - 1)]
        used_sem = {("gate", 0): gate_half, ("gate", 1): gate_full, ("up", 0): up_half, ("up", 1): up_full,
                    ("down", 0): down_half, ("down", 1): down_done}

        def parts_free(pair, n, part):
            back = n < PARTS
            kind, half, g = order[n - PARTS]
            extra = CREDIT if kind == "down" else 0
            return used_sem[kind, half], pair * PAIR_SLICES + (part * PAIRS * PAIR_SLICES + g + 1 + extra
                                                               - (PAIR_SLICES if back else 0))

        v_bank = []
        last_use = {}
        job = {}

        @block.tensor
        def _(pe):
            after = counter(pe)
            n_v, n_a, n_i, n_u, n_norm = [0], [0], [0], [0], [0]
            ring_v, turn_v, user_v = [len(VB)], [-1], {}

            def open_v(name=None):
                n = n_v[0]
                n_v[0] += 1
                turn_v[0] = (turn_v[0] + 1) % ring_v[0]
                b = VB[turn_v[0]]
                if turn_v[0] in user_v:
                    pe.wait_ge(v_done, user_v[turn_v[0]] + 1)
                user_v[turn_v[0]] = n
                v_bank.append(b)
                if name:
                    job[name] = n
                return b

            def open_a(name=None):
                n = n_a[0]
                n_a[0] += 1
                if n >= len(AB):
                    pe.wait_ge(a_done, n - len(AB) + 1)
                if name:
                    job[name] = n
                return AB[n % len(AB)]

            def next_item():
                n = n_i[0]
                n_i[0] += 1
                _, k, width, _, s = items[n]
                pe.wait_ge(lo_ready, n + 1)
                hi, lo = (parts[:, s, i, 0:k * width].rearrange("p (k n) -> p k n", k=k) for i in range(2))
                return n, hi, lo

            def part_used(n, mm):
                n_u[0] += 1
                mm.then_inc(slot_used, 1)
                last_use[n] = (slot_used, n_u[0])

            def three(out, st, mv, start, stop):
                nc.tensor.matmul(out, st[0], mv[0], start=start, stop=False)
                nc.tensor.matmul(out, st[0], mv[1], start=False, stop=False)
                return nc.tensor.matmul(out, st[1], mv[0], start=False, stop=stop)

            n_h = [0]

            def ada_product():
                layer, h = divmod(n_h[0], ADA_ITEMS)
                n_h[0] += 1
                s, (k0, k1) = h // 2, HALVES[h % 2]
                n, hi, lo = next_item()
                b = rows_bank[layer]
                for k in range(k0, k1):
                    st = cond[layer][:, k, COND_PAD - 4 * s:COND_PAD - 4 * s + ADA_ROWS]
                    nc.tensor.matmul(b[0:ADA_ROWS, :], st, hi[:, k - k0, :], start=(h == 0 and k == 0), stop=False)
                    mm = nc.tensor.matmul(b[0:ADA_ROWS, :], st, lo[:, k - k0, :], start=False,
                                          stop=(h == ADA_ITEMS - 1 and k == KT - 1))
                if h < ADA_ITEMS - 1:
                    part_used(n, mm)
                else:
                    mm.then_inc(rows_full, 1)
                    last_use[n] = (rows_full, layer + 1)

            def ada_columns(layer):
                after(bias_in, 16)
                after(small_in, 16 * N_SMALL)
                if layer == 0:
                    after(rows_out)
                for j in range(SLICE // P):
                    nc.tensor.matmul(OB[:, 24 * j:24 * j + 24], row[layer][0:ADA_ROWS + ADA_SLICES, j * P:(j + 1) * P],
                                     table("fold")[0:ADA_ROWS + ADA_SLICES, :], start=True, stop=True)
                nc.tensor.transpose(OB[:, 96:96 + 2 * KT + 2], vrows[:, :], ident[0:2 * KT + 2, 0:2 * KT + 2])\
                    .then_inc(cols_full, 1)

            def turn_normalized(streams, first_chunk=0, last_chunk=KT, credits=False):
                signals = [down_half, down_done] * CREDIT if credits else []
                if first_chunk == 0:
                    after(xn_ready, TT * len(streams))
                for kp, s in [(kp, s) for kp in range(KT // 2) for s in streams][first_chunk:last_chunk]:
                    b = open_v(("normalized", n_norm[0], kp, s)) if s == 0 else open_a(("normalized", n_norm[0], kp, s))
                    for kk in range(2):
                        for t in range(TT):
                            k = 2 * kp + kk
                            mm = nc.tensor.transpose(b[:, (kk * TT + t) * P:(kk * TT + t + 1) * P],
                                                     xn[:, s * TT + t, k * P:(k + 1) * P], ident)
                            if signals and not (kk and t == TT - 1):
                                mm.then_inc(signals.pop(), 1)
                    mm.then_inc(v_full if s == 0 else a_full, 1)
                if last_chunk >= len(streams) * KT // 2:
                    n_norm[0] += 1

            def project_in(layer):
                for a, b_ in IN_SLICES[:-1]:
                    tiles = range(NT) if layer == 0 or b_ <= C_Q else range(TT)
                    outs = [(open_v if t % 2 == 0 else open_a)(("in", layer, a, t)) for t in tiles]
                    for k0, k1 in HALVES:
                        n, hi, lo = next_item()
                        if a == C_Q:
                            after(h_lo, KT // 2)
                        for t in tiles:
                            tok = slice(t * P, (t + 1) * P)
                            for k in range(k0, k1):
                                mm = three(outs[t][:, 0:b_ - a], (hTr[:, 0, k, tok], hTr[:, 1, k, tok]),
                                           (hi[:, k - k0, :], lo[:, k - k0, :]), k == 0, k == KT - 1)
                            if k1 == KT:
                                mm.then_inc(v_full if t % 2 == 0 else a_full, 1)
                        if k0 == 0:
                            part_used(n, mm)
                    last_use[n] = (a_full, n_a[0])
                cols_ = (SEQ + CTX_LEN) if layer == 0 else SEQ
                outs = [(ct, half, open_a(("conv_gate", layer, ct)) if half else open_v(("conv_value", layer, ct))) for ct in range(2) for half in (1, 0)]
                for k0, k1 in HALVES:
                    n, hi, lo = next_item()
                    for ct, half, b in outs:
                        c0 = half * CONV_CH + ct * P
                        for k in range(k0, k1):
                            mm = three(b[:, 0:cols_], (hi[:, k - k0, c0:c0 + P], lo[:, k - k0, c0:c0 + P]),
                                       (hTr[:, 0, k, 0:cols_], hTr[:, 1, k, 0:cols_]), k == 0, k == KT - 1)
                        if k1 == KT:
                            mm.then_inc(a_full if half else v_full, 1)
                    if k0 == 0:
                        part_used(n, mm)
                last_use[n] = (v_full, n_v[0])

            def turn_heads(layer):
                b = open_v(("taps", layer))
                for ct in range(2):
                    mm = nc.tensor.transpose(b[:, ct * 32:ct * 32 + CONV_WIDTH],
                                             convwr[:, ct * P:(ct + 1) * P], ident[0:CONV_WIDTH, 0:CONV_WIDTH])
                mm.then_inc(v_full, 1)
                pe.wait_ge(a_done, n_a[0])
                for t in tiles_of(layer):
                    b = open_v()
                    for i, c in enumerate((C_RQ, C_RQ + P, C_RK, C_RK + P)):
                        mm = nc.tensor.transpose(b[:, i * P:(i + 1) * P], proj[:, t, c:c + P], ident)
                    mm.then_inc(v_full, 1)

            def turn_qk(layer):
                bk = OB
                for t in range(NT):
                    if t in tiles_of(layer):
                        b = open_a()
                    after(qk_ready)
                    if t in tiles_of(layer):
                        for r in range(4):
                            mm = nc.tensor.transpose(b[:, r * P:(r + 1) * P],
                                                     QK[:, t, 2 * r:2 * r + 2, :].rearrange("p h d -> p (h d)"), ident)
                        mm.then_inc(a_full, 1)
                    mm = nc.tensor.transpose(bk[:, t * P:(t + 1) * P],
                                             QK[:, t, 8:10, :].rearrange("p h d -> p (h d)"), ident)
                    mm.then_inc(att_done, 1)

            def states():
                b = open_v()
                after(vw_ready, TT)
                for pair in range(2):
                    for t in range(TT):
                        mm = nc.tensor.matmul(b[:, pair * 256:(pair + 1) * 256],
                                              proj[:, TT + t, C_RK + pair * P:C_RK + (pair + 1) * P],
                                              VW[:, t, 2 * pair:2 * pair + 2, :, :].rearrange("p h d e -> p (h d e)"),
                                              start=(t == 0), stop=(t == TT - 1))
                mm.then_inc(v_full, 1)

            def retention(layer):
                def scores(s, h):
                    b = open_v(("decayed", layer, s, h))
                    lo = 64 * (h % 2)
                    for jt in range(TT):
                        mm = nc.tensor.matmul(b[:, jt * SEQ:(jt + 1) * SEQ],
                                              RT[lo:lo + 64, 2 + h // 2, s * TT + jt, :],
                                              RT[lo:lo + 64, h // 2, s * TT:s * TT + TT, :].rearrange("p t n -> p (t n)"),
                                              start=True, stop=True)
                    mm.then_inc(v_full, 1)

                def apply(s, h, outs):
                    pe.wait_ge(v_done, job[("decayed", layer, s, h)] + 1)
                    for it in range(TT):
                        for jt in range(TT):
                            mm = nc.tensor.matmul(outs[it][:, h * 64:(h + 1) * 64],
                                                  AD[:, h, jt * SEQ + it * P:jt * SEQ + (it + 1) * P],
                                                  proj[:, s * TT + jt, C_RV + h * 64:C_RV + (h + 1) * 64],
                                                  start=(jt == 0), stop=(jt == TT - 1))
                        if h == RET_HEADS - 1:
                            mm.then_inc(a_full, 1)

                pe.wait_ge(v_done, n_v[0])
                for s in ((0, 1) if layer == 0 else (0,)):
                    scores(s, 0)
                    outs = [open_a(("inner", layer, s)), open_a()]
                    for h in range(RET_HEADS):
                        if h + 1 < RET_HEADS:
                            scores(s, h + 1)
                        apply(s, h, outs)
                for t in range(TT):
                    b = open_v()
                    for pair in range(2):
                        mm = nc.tensor.matmul(b[:, pair * 256:(pair + 1) * 256], RT[:, pair, t, :], ST[:, pair, :],
                                              start=True, stop=True)
                    mm.then_inc(v_full, 1)

            def attention(layer):
                its = [(t, r, g) for t in tiles_of(layer) for r in range(4) for g in range(2)]
                after(att_read)
                pe.wait_ge(a_done, n_a[0])

                def scores(n):
                    t, r, g = its[n]
                    b = open_v()
                    k0 = 0 if t < TT else SEQ
                    nc.tensor.matmul(b[:, k0:2 * SEQ], AQT[64 * g:64 * g + 64, r, t, :], AKT[64 * g:64 * g + 64, k0:],
                                     start=True, stop=True).then_inc(v_full, 1)

                def turn(n):
                    t, r, g = its[n]
                    b = open_a(("probs", layer, n))
                    after(exp_ready)
                    for kb in range(0 if t < TT else TT, NT):
                        mm = nc.tensor.transpose(b[:, kb * P:(kb + 1) * P], SC[:, n % 4, kb * P:(kb + 1) * P], ident)
                    mm.then_inc(a_full, 1)

                def values(n):
                    t, r, g = its[n]
                    head = g * 4 + r
                    if n % 8 == 0 and n:
                        after(att_read)
                    pe.wait_ge(a_done, job[("probs", layer, n)] + 1)
                    first = 0 if t < TT else TT
                    for kb in range(first, NT):
                        mm = nc.tensor.matmul(OB[:, head * 64:(head + 1) * 64], PT[:, n % 2, kb * P:(kb + 1) * P],
                                              proj[:, kb, C_V + 64 * g:C_V + 64 * g + 64],
                                              start=(kb == first), stop=(kb == NT - 1))
                    mm.then_inc(att_done, 1)

                if layer == 0:
                    ring_v[0], turn_v[0] = 3, turn_v[0] % 3
                    after(cond_ready)
                    pe.wait_ge(v_done, user_v[3] + 1)
                for n in range(len(its) + 3):
                    if n < len(its):
                        scores(n)
                    if 2 <= n < len(its) + 2:
                        turn(n - 2)
                    if n >= 3:
                        values(n - 3)
                    if layer == 0 and 2 <= n < ADA_ITEMS + 2:
                        ada_product()
                after(att_read)
                if layer == 0:
                    after(rows_out)
                    ring_v[0] = len(VB)

            def turn_conv(layer):
                pe.wait_ge(tap_done, CONV_WIDTH * (layer + 1))
                pe.wait_ge(pool_tap, CONV_WIDTH * (layer + 1))
                for t in tiles_of(layer):
                    b = open_v()
                    for ct in range(2):
                        mm = nc.tensor.transpose(b[:, ct * P:(ct + 1) * P],
                                                 CA[:, ct, t // TT, (t % TT) * P:(t % TT + 1) * P], ident)
                    mm.then_inc(v_full, 1)

            def turn_mix(layer):
                after(act_mix)
                for t in tiles_of(layer):
                    for half in range(2):
                        b = open_v(("mix", layer, t, half))
                        for i in range(4):
                            c = C_Q + (half * 4 + i) * P
                            mm = nc.tensor.transpose(b[:, i * P:(i + 1) * P], proj[:, t, c:c + P], ident)
                        mm.then_inc(v_full, 1)

            def spread_gate(group, streams):
                for s in streams:
                    for half in range(2):
                        b = open_a()
                        for i in range(4):
                            c = group * KT + half * 4 + i
                            mm = nc.tensor.matmul(b[:, i * P:(i + 1) * P], ada[:, c, s:s + 1].broadcast_to([P, P]), ident,
                                                  start=True, stop=True)
                        mm.then_inc(a_full, 1)

            def project_out(layer):
                pe.wait_ge(v_done, n_v[0])
                pe.wait_ge(a_done, n_a[0])
                for half in range(2):
                    outs = [open_v() for _ in tiles_of(layer)]
                    for k0, k1 in HALVES:
                        n, hi, lo = next_item()
                        for t in tiles_of(layer):
                            tok = slice(t * P, (t + 1) * P)
                            for k in range(k0, k1):
                                mm = three(outs[t][:, :], (hTr[:, 0, k, tok], hTr[:, 1, k, tok]),
                                           (hi[:, k - k0, :], lo[:, k - k0, :]), k == 0, k == KT - 1)
                            if k1 == KT:
                                mm.then_inc(v_full, 1)
                        if k0 == 0:
                            part_used(n, mm)
                    last_use[n] = (v_full, n_v[0])
                job[("mixed", layer)] = n_v[0]

            def dense_ffn():
                for p0 in range(0, FF_TILES, HALF_FF):
                    for f in range(p0, p0 + HALF_FF):
                        n, hi, lo = next_item()
                        for half in range(2):
                            b = open_a(("gate", f)) if half == 0 else open_v(("up", f))
                            c0 = half * P
                            for k in range(KT):
                                if f == 0 and half == 0 and k % (KT // 2) == 0:
                                    after(h_lo, KT // 2)
                                mm = three(b[:, :], (hi[:, k, c0:c0 + P], lo[:, k, c0:c0 + P]),
                                           (hTr[:, 0, k, :], hTr[:, 1, k, :]), k == 0, k == KT - 1)
                            mm.then_inc(a_full if half == 0 else v_full, 1)
                        last_use[n] = (v_full, n_v[0])
                    if p0 == 0:
                        spread_gate(5, (0, 1))
                        pe.wait_ge(a_done, n_a[0])
                    after(ff_lo, HALF_FF)
                    if p0:
                        ada_columns(1)
                    for half in range(2):
                        outs = [open_v() for _ in range(NT)]
                        for f0, f1 in ff_split:
                            n, hi, lo = next_item()
                            for f in range(f0, f1):
                                for t in range(NT):
                                    tok = slice(t * P, (t + 1) * P)
                                    mm = three(outs[t][:, :], (HFr[:, 0, f, tok], HFr[:, 1, f, tok]),
                                               (hi[:, f - f0, :], lo[:, f - f0, :]), f == 0, f == HALF_FF - 1)
                                    if f == HALF_FF - 1:
                                        mm.then_inc(v_full, 1)
                            if f1 < HALF_FF:
                                part_used(n, mm)
                            else:
                                last_use[n] = (v_full, n_v[0])

            def routing():
                b = open_v()
                after(router_in, 16)
                pe.wait_ge(v_done, n_v[0] - 1)
                for t in range(TT):
                    for k in range(KT):
                        mm = nc.tensor.matmul(b[:, t * N_EXPERTS:(t + 1) * N_EXPERTS], hTf[:, k, t * P:(t + 1) * P],
                                              routw[:, k, :],
                                              start=(k == 0), stop=(k == KT - 1))
                mm.then_inc(v_full, 1)
                b = open_v()
                after(mask_ready)
                chosen = top[:, 0, :, :]
                nc.tensor.matmul(b[:, 0:8], table("before"), chosen[:, 0, :], start=True, stop=True)
                nc.tensor.matmul(b[:, 8:16], table("ones"), chosen[:, 0, :], start=True, stop=False)
                nc.tensor.matmul(b[:, 8:16], table("before"), chosen[:, 1, :], start=False, stop=True)
                nc.tensor.matmul(b[:, 16:24], table("ones"), chosen[:, 0, :], start=True, stop=False)
                nc.tensor.matmul(b[:, 16:24], table("ones"), chosen[:, 1, :], start=False, stop=True).then_inc(v_full, 1)

            def scatter_matrices(part):
                for e in range(0, N_EXPERTS, 2):
                    b = open_v()
                    after(scat_in)
                    for i in range(2):
                        for t in range(TT):
                            mm = nc.tensor.transpose(b[:, i * 256 + t * P:i * 256 + (t + 1) * P],
                                                     WR[:, (e // 2) % 2, i * TT + t, :], ident)
                    mm.then_inc(v_full, 1)

            def experts(part):
                G, U, Y, T, M = bank[0], bank[1], bank[2:4], bank[4:6], bank[6:8]
                s0 = part * N_EXPERTS * EF_SLICES
                e0, j0 = part * N_EXPERTS, part * GATHERS

                def gather(i, j):
                    pe.wait_ge(scatter_read, i * 8 + (4 * e0 + 1 + 4 * max(j - 1, 0)))
                    for k in range(KT):
                        for t in range(TT):
                            mm = nc.tensor.matmul(M[k // 4][:, (k % 4) * P:(k % 4 + 1) * P], xn[:, t, k * P:(k + 1) * P],
                                                  PA[:, t, bass.ds(i * 2 + j, 1), :].rearrange("p e s -> p (e s)"),
                                                  start=(t == 0), stop=(t == TT - 1))
                        if k % 4 == 3:
                            mm.then_inc(gather_full, 1)

                def scatter(i, ee):
                    pe.wait_ge(st_ready, i * 2 + (e0 + ee + 1))
                    pe.wait_ge(y_ready, i * 4 + (2 * (e0 + ee) + 2))
                    for t in range(TT):
                        for h in range(2):
                            if t:
                                pe.wait_ge(scatter_read, i * 8 + (4 * (e0 + ee) + 1 + h + 1))
                            nc.tensor.matmul(M[h][:, :], SCAT[:, ee % 2, t * P:(t + 1) * P], YS[:, h * 512:(h + 1) * 512],
                                             start=True, stop=True).then_inc(scatter_full, 1)

                def pair(i, opening):
                    def weights(n):
                        pe.wait_ge(lo_ready, i * PAIR_ITEMS + (BASE + part * PAIRS * PAIR_ITEMS + n + 1))
                        return [parts[:, n % PARTS, j, :].rearrange("p (k n) -> p k n", n=SLICE) for j in range(2)]

                    def gate_or_up(g, n, b, half_used, full):
                        if g or not opening:
                            pe.wait_ge(gate_read if b is G else up_read, i * PAIR_SLICES + (s0 + g))
                        for half in range(2):
                            hi, lo = weights(n + half)
                            for kk in range(4):
                                k = 4 * half + kk
                                x = XEr[:, g // EF_SLICES, :, k, :]
                                mm = three(b[:, :], (x[:, 0, :], x[:, 1, :]), (hi[:, kk, :], lo[:, kk, :]), k == 0, k == KT - 1)
                            mm.then_inc(full if half else half_used, 1)

                    def turn(g):
                        pe.wait_ge(up_read, i * PAIR_SLICES + (s0 + g + 1))
                        if g >= 2 or not opening:
                            pe.wait_ge(ht_ready, i * PAIR_SLICES + (s0 + g - 1))
                        for j in range(4):
                            mm = nc.tensor.transpose(T[g % 2][:, j * P:(j + 1) * P], HE[:, g % 2, j * P:(j + 1) * P], ident)
                        mm.then_inc(h_turned, 1)

                    def down(g, n):
                        pe.wait_ge(ht_ready, i * PAIR_SLICES + (s0 + g + 1))
                        for half in range(2):
                            hi, lo = (v.rearrange("p (j h) n -> p j h n", h=2) for v in weights(n + half))
                            for jj in range(2):
                                j = 2 * half + jj
                                x = HTr[:, g % 2, :, j * P:(j + 1) * P]
                                for h in range(2):
                                    mm = three(Y[h][:, :], (x[:, 0, :], x[:, 1, :]), (hi[:, jj, h, :], lo[:, jj, h, :]),
                                               g % EF_SLICES == 0 and j == 0, g % EF_SLICES == EF_SLICES - 1 and j == 3)
                            mm.then_inc(down_done if half else down_half, 1)

                    n = 0
                    for g in range(PAIR_SLICES):
                        if g % EF_SLICES == 0:
                            pe.wait_ge(xe_ready, i * 2 + (j0 + g // EF_SLICES + 1))
                        gate_or_up(g, n, G, gate_half, gate_full)
                        if g >= 1:
                            turn(g - 1)
                        if g == 5:
                            gather(i, 1)
                        gate_or_up(g, n + 2, U, up_half, up_full)
                        n += 4
                        if g == 1 and not opening:
                            scatter(i, -1)
                        if g == EF_SLICES + 1:
                            scatter(i, 0)
                        if g >= 1:
                            down(g - 1, n)
                            n += 2
                    turn(PAIR_SLICES - 1)
                    gather(i, 2)
                    down(PAIR_SLICES - 1, n)

                pe.wait_ge(v_done, n_v[0])
                pe.wait_ge(a_done, n_a[0])
                gather(0, 0)
                pair(0, True)
                with pe.Fori(1, PAIRS) as i:
                    pair(i, False)
                pe.wait_ge(xe_ready, j0 + GATHERS)
                scatter(PAIRS, -1)

            after(tables_in, 16)
            for layer in range(DEPTH):
                streams = (0, 1) if layer == 0 else (0,)
                if layer == 0:
                    after(cond_ready)
                    for _ in range(ADA_ITEMS - 4):
                        ada_product()
                    turn_normalized((0, 1), 0, KT - 1)
                    for _ in range(4):
                        ada_product()
                    ada_columns(0)
                    turn_normalized((0, 1), KT - 1, KT)
                else:
                    turn_normalized((0, 1))
                project_in(layer)
                turn_heads(layer)
                turn_qk(layer)
                states()
                retention(layer)
                attention(layer)
                turn_conv(layer)
                turn_mix(layer)
                after(mod_ready)
                spread_gate(2, streams)
                project_out(layer)
                turn_normalized(streams, credits=layer == 1)
                if layer == 0:
                    dense_ffn()
            routing()
            scatter_matrices(0)
            spread_gate(5, (0,))
            experts(0)
            after(most_ready)
            over = pe.value_load(mosti[0:1, 0:1], min_val=0, max_val=SEQ)
            with pe.If(over > P):
                scatter_matrices(1)
                experts(1)

        @block.sync
        def _(sp):
            sp.dma_start(cload[:, 0, :], io["c"].rearrange("b (p k) -> (b p) k", k=KT)).then_inc(c_in, 16)
            sp.dma_start(cload[:, 1, :], io["c_ctx"].rearrange("(p k) -> p k", k=KT)).then_inc(c_in, 16)
            sp.dma_start(const[:, :], io["shape_tables"][:, 0:nconst]).then_inc(tables_in, 16)
            sp.dma_start(X[:, 0:TT, :], io["x"].rearrange("b (t p) n -> p (b t) n", p=P)).then_inc(x_in, 16)
            sp.dma_start(X[:, TT:NT, :], io["ctx"].rearrange("b (t p) n -> p (b t) n", p=P)).then_inc(x_in, 16)
            holder = [None] * RAW
            for n, (srcs, k, width, s, _) in enumerate(items):
                if holder[s] is not None:
                    sp.wait_ge(lo_ready, holder[s] + 1)
                if n == first["ffn"] + 2:
                    sp.wait_ge(v_full, job[("mixed", 0)])
                holder[s] = n
                dst = raw[:, s, 0:k * width].rearrange("p (k n) -> p k n", k=k)
                part_w = width // len(srcs)
                for j, src in enumerate(srcs):
                    sp.dma_start(dst[:, :, j * part_w:(j + 1) * part_w], src).then_inc(raw_loaded[s], 16)

            def expert_loads(part):
                before = BASE + part * PAIRS * PAIR_ITEMS
                sp.wait_ge(lo_ready, before)
                sp.wait_ge(v_full, job[("mixed", 1)])
                with sp.Fori(0, PAIRS) as i:
                    for n, (kind, half, g) in enumerate(order):
                        e = i * 2 + g // EF_SLICES
                        s = g % EF_SLICES
                        sp.wait_ge(lo_ready, i * PAIR_ITEMS + (before + n - RAW + 1))
                        if kind == "down":
                            r0 = s * SLICE + half * 2 * P
                            rows = io["moe_w_down"][0][bass.ds(e, 1), r0:r0 + 2 * P, :].rearrange("e (k p) n -> p (e k) n", p=P)
                            dst = raw[:, n % RAW, :].rearrange("p (k n) -> p k n", k=2)
                        else:
                            r0 = half * 4 * P
                            rows = io["moe_w_" + kind][0][bass.ds(e, 1), r0:r0 + 4 * P, s * SLICE:(s + 1) * SLICE]\
                                .rearrange("e (k p) n -> p (e k) n", p=P)
                            dst = raw[:, n % RAW, :].rearrange("p (k n) -> p k n", k=4)
                        sp.dma_start(dst, rows).then_inc(raw_loaded[n % RAW], 16)

            expert_loads(0)
            sp.wait_ge(most_ready, 1)
            over = sp.value_load(mosti[0:1, 0:1], min_val=0, max_val=SEQ)
            with sp.If(over > P):
                expert_loads(1)
            for t in range(TT):
                sp.wait_ge(out_ready, t + 1)
                sp.dma_start(io["out"][0, t * P:(t + 1) * P, :], X[:, t, :]).then_inc(out_in, 16)
            sp.wait_ge(out_in, 16 * TT)

        @block.scalar
        def _(act):
            after = counter(act)
            step = stepper(act, a_step)
            n_a = [0]

            def take():
                n = n_a[0]
                n_a[0] += 1
                act.wait_ge(a_full, n + 1)
                return AB[n % len(AB)]

            n_hi = [0]
            n_norm = [0]
            holders = [None] * PARTS
            loads = [0] * RAW

            def split_to(stop):
                while n_hi[0] < stop:
                    n = n_hi[0]
                    n_hi[0] += 1
                    srcs, k, width, r, s = items[n]
                    loads[r] += len(srcs)
                    act.wait_ge(raw_loaded[r], 16 * loads[r])
                    if holders[s] is not None:
                        act.wait_ge(*last_use[holders[s]])
                    if n == first["ffn"] + 2:
                        act.wait_ge(v_full, job[("mixed", 0)])
                    holders[s] = n
                    nc.scalar.activation(parts[:, s, 0, 0:k * width], raw[:, r, 0:k * width], ACT.Copy).then_inc(hi_ready, 1)

            def small_loads(layer):
                b = io["ada_b"][layer]
                act.dma_start(row[layer][ADA_ROWS:ADA_ROWS + ADA_SLICES, :], b.rearrange("(s n) -> s n", n=SLICE)).then_inc(bias_in, 16)
                for r, name in ((0, "norm1_w"), (KT, "norm2_w"), (2 * KT, "conv_b")):
                    v = io[name][layer].rearrange("(k p) -> k p", p=P)
                    act.dma_start(vrows[r:r + v.shape[0], :], v).then_inc(small_in, 16)
                act.dma_start(convwr[:, :], io["conv_w"][layer]).then_inc(small_in, 16)
                for dst, src in ((qkw[:, 0, :], "q_norm_w"), (qkw[:, 1, :], "k_norm_w"), (sink[:, :], "attn_sink"),
                                 (dlog[:, 0, :], "ret_decay_f"), (dlog[:, 1, :], "ret_decay_b"),
                                 (gnw[:, :], "ret_gn_w"), (lnw[:, :], "conv_ln_w"), (lnb[:, :], "conv_ln_b")):
                    src = io[src][layer]
                    act.dma_start(dst, src.unsqueeze(0).broadcast_to([P, src.shape[0]])).then_inc(small_in, 16)

            def mask_load():
                a, n = place["mask"]
                act.dma_start(mask_t[:, :], io["shape_tables"][:, a:a + n]).then_inc(mask_in, 16)

            def cond_high(layer):
                after(cond_clear)
                nc.scalar.activation(cond[layer][:, :, COND_PAD:COND_PAD + 2], condf[:, :, :], ACT.Copy).then_inc(cond_hi, 1)

            def squares(tiles, x_in_tiles=True):
                for t in tiles:
                    if x_in_tiles:
                        after(x_ready)
                    nc.scalar.activation(xn[:, t, :], X[:, t, :], ACT.Square, accum_out=ssq[:, t:t + 1]).then_inc(sq_ready, 1)

            def modulate(which):
                for kp in range(KT // 2):
                    b = take()
                    for kk in range(2):
                        k = 2 * kp + kk
                        ins = nc.scalar.activation(hTf[:, k, SEQ:2 * SEQ], b[:, kk * SEQ:(kk + 1) * SEQ], ACT.Identity,
                                                   bias=ada[:, 3 * which * KT + k, 1:2], scale=scl[:, which, k, 1:2])
                    ins.then_inc(a_done, 1)
                    for s, done in ((0, v_done), (1, a_done)):
                        act.wait_ge(done, job[("normalized", n_norm[0], kp, s)] + 1)
                        k, c = slice(2 * kp, 2 * kp + 2), slice(s * SEQ, (s + 1) * SEQ)
                        nc.scalar.activation(hTr[:, 0, k, c], hTf[:, k, c], ACT.Copy).then_inc(h_hi, 1)
                n_norm[0] += 1

            def copy_out(out, src):
                nc.scalar.activation(out, src, ACT.Copy).then_inc(a_done, 1)

            def gate_rows(rows, streams):
                for s in streams:
                    for half in range(2):
                        copy_out(rows[:, s, half * 512:(half + 1) * 512], take()[:, :])

            def attention(layer, base):
                its = [(t, r, g) for t in tiles_of(layer) for r in range(4) for g in range(2)]
                if layer == 0:
                    cond_high(1)
                for n in range(len(its) + 2):
                    if n < len(its):
                        t, r, g = its[n]
                        head, turn = g * 4 + r, (n // 8) % 2
                        k0 = 0 if t < TT else SEQ
                        after(negm_ready)
                        nc.scalar.activation(SC[:, n % 4, k0:], SC[:, n % 4, k0:], ACT.Exp, bias=negm[:, turn, head:head + 1],
                                             scale=HEAD_DIM ** -0.5, accum_out=rsum[:, turn, head:head + 1]).then_inc(exp_ready, 1)
                        if n % 8 == 7:
                            after(sarg_ready)
                            nc.scalar.activation(esink[:, turn, :], esink[:, turn, :], ACT.Exp).then_inc(esink_ready, 1)
                    if n >= 2:
                        m = n - 2
                        k0 = 0 if its[m][0] < TT else SEQ
                        b = take()
                        if m >= 2:
                            act.wait_ge(att_done, base + m - 1)
                        copy_out(PT[:, m % 2, k0:], b[:, k0:])
                    if layer == 0 and n < ADA_ITEMS:
                        split_to(first["ada", 1] + n + 1)
                    if n == len(its) - 4:
                        split_to(first["out", layer] + 2)

            def split_expert(i, n, part):
                r = n % RAW
                act.wait_ge(raw_loaded[r], i * (16 * PAIR_ITEMS // RAW)
                            + 16 * (loads_before[r] + part * PAIRS * PAIR_ITEMS // RAW + n // RAW + 1))
                act.wait_ge(*parts_free(i, n, part))
                nc.scalar.activation(parts[:, n % PARTS, 0, :], raw[:, r, :], ACT.Copy).then_inc(hi_ready, 1)

            def experts(part):
                G, T, M = bank[0], bank[4:6], bank[6]
                s0, j0 = part * N_EXPERTS * EF_SLICES, part * GATHERS

                def gathered(i, j):
                    act.wait_ge(gather_full, i * 4 + (2 * (j0 + j) + 1))
                    for k in range(4):
                        ins = nc.scalar.activation(XF[:, k, :], M[:, k * P:(k + 1) * P], ACT.Identity,
                                                   bias=ada[:, 3 * KT + k, 0:1], scale=scl[:, 1, k, 0:1])
                    ins.then_inc(xe_lo, 1)
                    act.wait_ge(xe_lo, i * 2 + (j0 + j + 1))
                    act.wait_ge(xe_hi, i * 2 + (j0 + j + 1))
                    nc.scalar.activation(XEr[:, j % 2, 0, :, :], XF, ACT.Copy).then_inc(xe_high, 1)

                def pair(i, opening):
                    def turned(g):
                        act.wait_ge(h_turned, i * PAIR_SLICES + (s0 + g + 1))
                        if g >= 2 or not opening:
                            act.wait_ge(down_done, i * PAIR_SLICES + (s0 + g - 1 + CREDIT))
                        nc.scalar.activation(HTr[:, g % 2, 0, :], T[g % 2][:, :], ACT.Copy).then_inc(ht_hi, 1)

                    if not opening:
                        for n in range(PARTS):
                            split_expert(i, n, part)
                    n = PARTS
                    for g in range(PAIR_SLICES):
                        split_expert(i, n, part)
                        act.wait_ge(gate_full, i * PAIR_SLICES + (s0 + g + 1))
                        if g >= 2 or not opening:
                            act.wait_ge(up_read, i * PAIR_SLICES + (s0 + g - 1))
                        nc.scalar.activation(SGE[:, g % 2, :], G[:, :], ACT.Silu).then_inc(gate_read, 1)
                        if g >= 1:
                            turned(g - 1)
                        if g == 5:
                            gathered(i, 1)
                        more = 4 if g == 0 or g == PAIR_SLICES - 1 else 6
                        for m in range(n + 1, n + more):
                            split_expert(i, m, part)
                        n += more
                    turned(PAIR_SLICES - 1)
                    gathered(i, 2)

                gathered(0, 0)
                pair(0, True)
                with act.Fori(1, PAIRS) as i:
                    pair(i, False)

            act.dma_start(routw[:, :, :], io["router_w"][0].rearrange("(k p) e -> p k e", p=P)).then_inc(router_in, 16)
            att_base = 0
            for layer in range(DEPTH):
                tiles = tiles_of(layer)
                nt = len(tiles)
                if layer == 0:
                    small_loads(0)
                    act.wait_ge(c_in, 32)
                    nc.scalar.activation(condf[:, :, :], cload[:, :, :].rearrange("p s k -> p k s"), ACT.Silu).then_inc(cond_f, 1)
                    act.wait_ge(cond_f, 1)
                    cond_high(0)
                    split_to(3)
                    mask_load()
                    act.wait_ge(x_in, 32)
                squares(range(NT), x_in_tiles=layer > 0)
                if layer:
                    mask_load()
                after(dneg_ready)
                step(nc.scalar.activation(dln[:, :, :], dneg[:, :, :], ACT.Exp))
                nc.scalar.activation(dln[:, :, :], dln[:, :, :], ACT.Ln, bias=1.0).then_inc(dln_ready, 1)
                W = first["in", layer]
                split_to(W + 2)
                after(mod_ready)
                modulate(0)
                after(dexp_in)
                nc.scalar.activation(decay, decay, ACT.Exp).then_inc(dexp_out, 1)
                nc.scalar.activation(dtok[:, :, :, :, :], dtok[:, :, :, :, :], ACT.Exp).then_inc(dexp_out, 1)
                for s, (a, b_) in enumerate(IN_SLICES[:-1]):
                    split_to(W + 2 * s + 3)
                    for t in (range(NT) if layer == 0 or b_ <= C_Q else range(TT)):
                        if t % 2:
                            copy_out(proj[:, t, a:b_], take()[:, 0:b_ - a])
                    split_to(W + 2 * s + 4)
                split_to(W + 10)
                ncol = SEQ * (2 if layer == 0 else 1)
                for ct in range(2):
                    nc.scalar.activation(SC[:, ct, 0:ncol], take()[:, 0:ncol], ACT.Sigmoid).then_inc(a_done, 1)
                act.wait_ge(v_done, job[("in", layer, C_RQ, tiles[-1] - 1)] + 1)
                act.wait_ge(a_done, job[("in", layer, C_RQ, tiles[-1])] + 1)
                gates = proj[:, 0:nt, C_RG:C_CONV]
                nc.scalar.activation(gates, gates, ACT.Silu).then_inc(rg_ready, 1)
                for t in tiles:
                    copy_out(AQT[:, :, t, :], take()[:, :].rearrange("p (r n) -> p r n", r=4))
                for s in ((0, 1) if layer == 0 else (0,)):
                    for t in range(TT):
                        copy_out(RO[:, s * TT + t, :], take()[:, 0:256])
                attention(layer, att_base + NT)
                att_base += NT + 8 * nt
                after(ln_ready)
                nc.scalar.activation(gates, CV[:, 0:nt, :], ACT.Silu).then_inc(act_mix, 1)
                for t in tiles:
                    for half in range(2):
                        n = job[("mix", layer, t, half)]
                        act.wait_ge(v_full, n + 1)
                        nc.scalar.activation(hTr[:, 0, 4 * half:4 * half + 4, t * P:(t + 1) * P],
                                             v_bank[n][:, :].rearrange("p (k n) -> p k n", k=4), ACT.Copy).then_inc(mix_hi, 1)
                gate_rows(GB, (0, 1) if layer == 0 else (0,))
                O = first["out", layer]
                split_to(O + 4 if layer else O + 7)
                squares(tiles)
                if layer == 0:
                    small_loads(1)
                    modulate(1)
                    n = first["ffn"] + 3

                    def hidden_high(f):
                        act.wait_ge(v_done, job[("up", f)] + 1)
                        nc.scalar.activation(HFr[:, 0, f % HALF_FF, :], HF[:, f % 2, :], ACT.Copy).then_inc(ff_hi, 1)

                    for p0 in range(0, FF_TILES, HALF_FF):
                        for f in range(p0, p0 + HALF_FF):
                            b = take()
                            if f >= 2:
                                act.wait_ge(v_done, job[("up", f - 2)] + 1)
                            nc.scalar.activation(SG[:, f % 2, :], b[:, :], ACT.Silu).then_inc(a_done, 1)
                            if f > p0:
                                hidden_high(f - 1)
                            n += 1
                            split_to(n)
                        hidden_high(p0 + HALF_FF - 1)
                        if p0 == 0:
                            gate_rows(GB, (0, 1))
                        n += 2 * len(ff_split)
                        split_to(min(n, first["in", 1] + 2))
            for n in range(PARTS):
                split_expert(0, n, 0)
            after(lexp_in)
            nc.scalar.activation(best[:, 3, :], best[:, 2, :], ACT.Exp).then_inc(lexp_out, 1)
            gate_rows(GBX[:, :].rearrange("p (s n) -> p s n", s=1), (0,))
            experts(0)
            after(most_ready)
            over = act.value_load(mosti[0:1, 0:1], min_val=0, max_val=SEQ)
            with act.If(over > P):
                for n in range(PARTS):
                    split_expert(0, n, 1)
                experts(1)

        @block.gpsimd
        def _(pool):
            after = counter(pool)
            step = stepper(pool, p_step)

            def rsqrt(out, mid, src, scale):
                step(nc.gpsimd.tensor_scalar(mid, src, scale, EPS, ALU.mult, ALU.add))
                return nc.gpsimd.tensor_tensor(out, mid, nhalf[:, 0:out.shape[1]], ALU.pow)

            def root_squares(nt):
                for t in range(nt):
                    after(sq_ready)
                    rsqrt(rstd[:, t:t + 1], lnt[:, t:t + 1], ssq[:, t:t + 1], 1.0 / D_MODEL).then_inc(rstd_ready, 1)

            step(nc.gpsimd.memset(nhalf[:, :], -0.5))
            for layer in range(DEPTH):
                nt = len(tiles_of(layer))
                root_squares(NT)
                pool.wait_ge(mod_ready, layer + 1)
                pool.wait_ge(lo_ready, first["in", layer])
                nc.gpsimd.memset(CB, 0.0).then_inc(pad_ready, 1)
                for t in range(NT):
                    lo = 0 if t in tiles_of(layer) else 8
                    after(qss_ready)
                    rsqrt(qrs[:, t, lo:], qst[:, t, lo:], qss[:, t, lo:], 1.0 / HEAD_DIM).then_inc(qrs_ready, 1)
                after(dexp_out, 2)
                pool.wait_ge(v_done, job[("in", layer, 384, 2)] + 1)
                pool.wait_ge(a_done, job[("in", layer, 384, 3)] + 1)
                for t in range(TT):
                    val = proj[:, TT + t, C_RV:C_RV + 256].rearrange("p (h e) -> p h e", h=RET_HEADS)
                    for d in range(2):
                        ins = nc.gpsimd.tensor_tensor(VW[:, t, :, d, :], val,
                                                      dtok[:, 0, t, :, d].unsqueeze(2).broadcast_to([P, RET_HEADS, HEAD_DIM]),
                                                      ALU.mult)
                    ins.then_inc(vw_ready, 1)
                pool.wait_ge(v_done, job[("conv_value", layer, 1)] + 1)
                pool.wait_ge(v_done, job[("taps", layer)] + 1)
                ns = nt // TT
                pool.wait_ge(att_read, 1 + layer * (NT + 1))
                for k in range(CONV_WIDTH):
                    src, acc = CB[:, 1, 0:ns, k:k + SEQ], CA[:, 1, 0:ns, :]
                    if k == 0:
                        nc.gpsimd.tensor_scalar(acc, src, convw[:, 1, 0:1], vcols[:, 2 * KT + 1:2 * KT + 2], ALU.mult, ALU.add)\
                            .then_inc(pool_tap, 1)
                        continue
                    n = layer * CONV_WIDTH + k
                    if k >= 3:
                        pool.wait_ge(pool_tap, n - 1)
                    prod = CP[:, k % 2, 0:ns, :]
                    step(nc.gpsimd.tensor_scalar(prod, src, convw[:, 1, k:k + 1], None, ALU.mult))
                    pool.wait_ge(pool_tap, n)
                    nc.gpsimd.tensor_tensor(acc, acc, prod, ALU.add).then_inc(pool_tap, 1)
                    if k == RO_TAP[layer]:
                        after(ro_var)
                        rsqrt(lnr[:, 0:4 * nt], lnt[:, 0:4 * nt], lnv[:, 0:4 * nt], 1.0 / HEAD_DIM).then_inc(ro_rstd, 1)
                after(cv_var)
                rsqrt(lnr[:, 0:nt], lnt[:, 0:nt], bag[:, 0:nt, 1], 1.0).then_inc(cv_rstd, 1)
                root_squares(nt)

        @block.vector
        def _(dve):
            after = counter(dve)
            step = stepper(dve, v_step)
            n_v = [0]
            x_count = [0]
            n_lo = [0]

            def split_to(stop):
                while n_lo[0] < stop:
                    n = n_lo[0]
                    n_lo[0] += 1
                    _, k, width, r, s = items[n]
                    dve.wait_ge(hi_ready, n + 1)
                    nc.vector.tensor_tensor(parts[:, s, 1, 0:k * width], raw[:, r, 0:k * width], parts_f[:, s, 0, 0:k * width],
                                            ALU.subtract).then_inc(lo_ready, 1)

            def take():
                n = n_v[0]
                n_v[0] += 1
                dve.wait_ge(v_full, n + 1)
                return v_bank[n]

            def emptied():
                dve.wait_ge(v_done, n_v[0])

            def tt(out, a, b, op):
                return nc.vector.tensor_tensor(out, a, b, op)

            def copy_out(out, src):
                nc.vector.tensor_copy(out, src).then_inc(v_done, 1)

            def per_group(v, width):
                return v.unsqueeze(2).broadcast_to([P, v.shape[1], width])

            def cond_low(layer):
                c = COND_PAD
                zeros = ident[:, 0:2 * c + 4].unsqueeze(1).broadcast_to([P, KT, 2 * c + 4])
                nc.vector.tensor_scalar(cond[layer][:, :, :], zeros, 0.0, None, ALU.mult).then_inc(cond_clear, 1)
                after(cond_hi)
                tt(cond[layer][:, :, c + 2:c + 4], condf[:, :, :], cond_f32[layer][:, :, c:c + 2], ALU.subtract).then_inc(cond_ready, 1)

            def ada_rows(layer):
                after(rows_full)
                nc.vector.tensor_copy(row[layer][0:ADA_ROWS, :], rows_bank[layer][0:ADA_ROWS, :]).then_inc(rows_out, 1)

            def ada_columns(layer):
                if layer == 0:
                    ada_rows(0)
                after(cols_full)
                nc.vector.tensor_copy(vcols[:, :], OB[:, 96:96 + 2 * KT + 2])
                step(nc.vector.tensor_copy(ada[:, :, :].rearrange("p (s j) r -> p j s r", s=ADA_SLICES),
                                           OB[:, 0:96].rearrange("p (j s r) -> p j s r", s=ADA_SLICES, r=2)))
                for which in range(2):
                    c = (1 + 3 * which) * KT
                    ins = nc.vector.scalar_tensor_tensor(scl[:, which, :, :], ada[:, c:c + KT, :], 1.0,
                                                         vcols[:, which * KT:(which + 1) * KT].unsqueeze(2).broadcast_to([P, KT, 2]), ALU.add, ALU.mult)
                ins.then_inc(mod_ready, 1)
                dve.wait_ge(mod_ready, layer + 1)

            def scale_tokens(tiles):
                for t in tiles:
                    after(rstd_ready)
                    nc.vector.tensor_scalar(xn[:, t, :], X[:, t, :], rstd[:, t:t + 1], None, ALU.mult).then_inc(xn_ready, 1)

            def modulate(which, streams):
                def low(kp):
                    for s in streams:
                        after(h_hi)
                        k, c = slice(2 * kp, 2 * kp + 2), slice(s * SEQ, (s + 1) * SEQ)
                        tt(hTr[:, 1, k, c], hTf[:, k, c], hTr_f[:, 0, k, c], ALU.subtract).then_inc(h_lo, 1)

                for kp in range(KT // 2):
                    b = take()
                    for kk in range(2):
                        k = 2 * kp + kk
                        ins = nc.vector.tensor_scalar(hTf[:, k, 0:SEQ], b[:, kk * SEQ:(kk + 1) * SEQ], scl[:, which, k, 0:1],
                                                      ada[:, 3 * which * KT + k, 0:1], ALU.mult, ALU.add)
                    ins.then_inc(v_done, 1)
                    if streams and kp:
                        low(kp - 1)
                if streams:
                    low(KT // 2 - 1)

            def decay_arguments():
                after(dln_ready)
                step(tt(dneg[:, :, :], dmin[:, :, :], dln[:, :, :], ALU.subtract))
                for h in range(RET_HEADS):
                    ins = nc.vector.tensor_scalar(decay[:, h, :], ahead, dneg[:, h, 0:1], None, ALU.mult)
                step(ins)
                for h in range(RET_HEADS):
                    nc.vector.scalar_tensor_tensor(decay[:, h, :], behind, dneg[:, h, 1:2], decay[:, h, :], ALU.mult, ALU.add)
                for h in range(RET_HEADS):
                    ins = tt(dtok[:, :, :, h, :].rearrange("p w t d -> p (w t) d"), expo,
                             dneg[:, h, :].unsqueeze(1).broadcast_to([P, 4, 2]), ALU.mult)
                ins.then_inc(dexp_in, 1)

            def head_squares(layer, t):
                if t % 2:
                    dve.wait_ge(a_done, job[("in", layer, 0, t)] + 1)
                lo = 8
                if t in tiles_of(layer):
                    lo = 0
                    q = proj[:, t, C_Q:C_RQ].rearrange("p (g r d) -> p g r d", g=2, d=HEAD_DIM)
                    tt(TMP[:, 0:512].rearrange("p (r g d) -> p g r d", g=2, d=HEAD_DIM), q, q, ALU.mult)
                k = proj[:, t, C_K:C_V]
                step(tt(TMP[:, 512:640], k, k, ALU.mult))
                nc.vector.tensor_reduce(qss[:, t, lo:], TMP[:, 64 * lo:640].rearrange("p (h d) -> p h d", d=HEAD_DIM),
                                        AX.X, ALU.add).then_inc(qss_ready, 1)

            def head_norm(layer, t):
                after(qrs_ready)
                if t in tiles_of(layer):
                    for g in range(2):
                        tt(QK[:, t, g:8:2, :], proj[:, t, C_Q + 256 * g:C_Q + 256 * g + 256].rearrange("p (r d) -> p r d", d=HEAD_DIM),
                           per_group(qrs[:, t, g:8:2], HEAD_DIM), ALU.mult)
                step(tt(QK[:, t, 8:10, :], proj[:, t, C_K:C_V].rearrange("p (h d) -> p h d", d=HEAD_DIM),
                        per_group(qrs[:, t, 8:10], HEAD_DIM), ALU.mult))
                if t in tiles_of(layer):
                    tt(QK[:, t, 0:8, :], QK[:, t, 0:8, :], qkw[:, 0, :].unsqueeze(1).broadcast_to([P, 8, HEAD_DIM]), ALU.mult)
                last = tt(QK[:, t, 8:10, :], QK[:, t, 8:10, :], qkw[:, 1, :].unsqueeze(1).broadcast_to([P, 2, HEAD_DIM]), ALU.mult)
                if t < TT:
                    step(last)
                    a_ = TMP[:, 0:640].rearrange("p (h d) -> p h d", d=HEAD_DIM)
                    b_ = TMP[:, 640:1280].rearrange("p (h a f) -> p h a f", a=2, f=32)
                    tt(a_, QK[:, t, :, :], cos64[:, t, :].unsqueeze(1).broadcast_to([P, 10, HEAD_DIM]), ALU.mult)
                    q4 = QK[:, t, :, :].rearrange("p h (a f) -> p h a f", a=2)
                    for half in range(2):
                        ins = tt(b_[:, :, :, 16 * half:16 * half + 16], q4[:, :, :, 16 - 16 * half:32 - 16 * half],
                                 sin64[:, t, :, half, :].unsqueeze(1).broadcast_to([P, 10, 2, 16]), ALU.mult)
                    step(ins)
                    last = tt(QK[:, t, :, :], a_, TMP[:, 640:1280].rearrange("p (h d) -> p h d", d=HEAD_DIM), ALU.add)
                last.then_inc(qk_ready, 1)
                dve.wait_ge(qk_ready, NT * layer + t + 1)

            def projections(layer):
                W = first["in", layer]
                for n, (a, b_) in enumerate(IN_SLICES[:-1]):
                    split_to(W + 2 * n + 3)
                    for t in (range(NT) if layer == 0 or b_ <= C_Q else range(TT)):
                        if t % 2 == 0:
                            copy_out(proj[:, t, a:b_], take()[:, 0:b_ - a])
                    split_to(W + 2 * n + 4)
                    if n == 1:
                        emptied()
                        for t in range(TT):
                            head_squares(layer, t)
                            head_norm(layer, t)
                    if n == 2:
                        emptied()
                        for t in range(TT, NT):
                            head_squares(layer, t)
                            head_norm(layer, t)
                after(pad_ready)
                ns = 2 if layer == 0 else 1
                split_to(W + 10)
                for ct in range(2):
                    b = take()
                    dve.wait_ge(a_done, job[("conv_gate", layer, ct)] + 1)
                    tt(CB[:, ct, 0:ns, CONV_WIDTH // 2:CONV_WIDTH // 2 + SEQ], b[:, 0:ns * SEQ].rearrange("p (s n) -> p s n", s=ns),
                       SC[:, ct, 0:ns * SEQ].rearrange("p (s n) -> p s n", s=ns), ALU.mult).then_inc(v_done, 1)

            def retention(layer, base):
                tiles = tiles_of(layer)
                copy_out(convw[:, :, :], take()[:, 0:64].rearrange("p (c k) -> p c k", c=2)[:, :, 0:CONV_WIDTH])
                for t in tiles:
                    copy_out(RT[:, :, t, :], take()[:, :].rearrange("p (b n) -> p b n", b=4))
                after(dexp_out, 2)
                nc.vector.tensor_scalar(dec[:, :], dec[:, :], HEAD_DIM ** -0.5, None, ALU.mult)
                read = dtok[:, 1, :, :, :]
                step(nc.vector.tensor_scalar(read, read, HEAD_DIM ** -0.5, None, ALU.mult))
                dve.wait_ge(att_done, base)
                after(mask_in, 16)
                nc.vector.tensor_copy(AKT, OB[:, :]).then_inc(att_read, 1)
                b = take()
                step(nc.vector.memset(ST, 0.0))
                nc.vector.tensor_copy(ST[0:64, :, 0:P], b[0:64, :].rearrange("p (c n) -> p c n", c=2)[:, :, 0:P])
                copy_out(ST[64:128, :, P:2 * P], b[64:128, :].rearrange("p (c n) -> p c n", c=2)[:, :, P:2 * P])
                for s in ((0, 1) if layer == 0 else (0,)):
                    if s:
                        dve.wait_ge(a_full, job[("inner", layer, 0)] + 2)
                    for h in range(RET_HEADS):
                        tt(AD[:, h, :], take()[:, :], decay[:, h, :], ALU.mult).then_inc(v_done, 1)
                dve.wait_ge(a_done, job[("inner", layer, 0)] + 2)
                cross = RW.rearrange("p t c -> p (t c)").rearrange("p (t g n) -> p t g n", t=TT, g=8)
                for t in range(TT):
                    tt(cross[:, t, :, :], take()[:, :].rearrange("p (g n) -> p g n", g=8),
                       per_group(dtok[:, 1, t, :, :].rearrange("p h d -> p (h d)"), HEAD_DIM), ALU.mult).then_inc(v_done, 1)
                emptied()
                for d in range(2):
                    for t in range(TT):
                        out = RO[:, t, :].rearrange("p (h n) -> p h n", h=RET_HEADS)
                        ins = tt(out, out, cross[:, t, d:8:2, :], ALU.add)
                    step(ins)

            def readout(layer):
                nt = len(tiles_of(layer))
                if layer == 0:
                    dve.wait_ge(a_done, job[("inner", layer, 1)] + 2)
                o = RO[:, 0:nt, :].rearrange("p t (h n) -> p (t h) n", h=RET_HEADS)
                w = RW[:, 0:nt, :].rearrange("p t (h n) -> p (t h) n", h=RET_HEADS)
                g = 4 * nt
                step(nc.vector.tensor_reduce(lnm[:, 0:g], o, AX.X, ALU.add))
                step(nc.vector.tensor_scalar(lnm[:, 0:g], lnm[:, 0:g], -1.0 / HEAD_DIM, None, ALU.mult))
                yield
                step(tt(o, o, per_group(lnm[:, 0:g], HEAD_DIM), ALU.add))
                yield
                step(tt(w, o, o, ALU.mult))
                yield
                nc.vector.tensor_reduce(lnv[:, 0:g], w, AX.X, ALU.add).then_inc(ro_var, 1)
                yield
                yield
                after(ro_rstd)
                step(tt(o, o, per_group(lnr[:, 0:g], HEAD_DIM), ALU.mult))
                yield
                r = RO[:, 0:nt, :]
                step(tt(r, r, gnw[:, :].unsqueeze(1).broadcast_to([P, nt, 256]), ALU.mult))
                yield
                after(rg_ready)
                step(tt(proj[:, 0:nt, C_RQ:C_RG], r, proj[:, 0:nt, C_RG:C_CONV], ALU.mult))

            def attention(layer, base):
                its = [(t, r, g) for t in tiles_of(layer) for r in range(4) for g in range(2)]
                ns = 2 if layer == 0 else 1
                per = -(-CONV_WIDTH // len(its))
                rest = readout(layer)

                def tap(k):
                    src, acc = CB[:, 0, 0:ns, k:k + SEQ], CA[:, 0, 0:ns, :]
                    if k == 0:
                        ins = nc.vector.tensor_scalar(acc, src, convw[:, 0, 0:1], vcols[:, 2 * KT:2 * KT + 1], ALU.mult, ALU.add)
                    else:
                        dve.wait_ge(tap_done, layer * CONV_WIDTH + k)
                        ins = nc.vector.scalar_tensor_tensor(acc, src, convw[:, 0, k:k + 1], acc, ALU.mult, ALU.add)
                    ins.then_inc(tap_done, 1)

                if layer == 0:
                    cond_low(1)
                for n in range(len(its) + 3):
                    if n < len(its):
                        t, r, g = its[n]
                        head, turn = g * 4 + r, (n // 8) % 2
                        k0 = 0 if t < TT else SEQ
                        b = take()
                        if n >= 4:
                            dve.wait_ge(a_full, job[("probs", layer, n - 4)] + 1)
                        nc.vector.tensor_tensor_reduce(SC[:, n % 4, k0:], b[:, k0:], mask[:, t % TT, k0:], 1.0, 3 * BIG_NEG,
                                                       ALU.add, ALU.max, mx[:, turn, head:head + 1]).then_inc(v_done, 1)
                        emptied()
                        nc.vector.tensor_scalar(negm[:, turn, head:head + 1], mx[:, turn, head:head + 1], -(HEAD_DIM ** -0.5),
                                                nsink[:, head:head + 1], ALU.mult, ALU.min).then_inc(negm_ready, 1)
                        if n % 8 == 7:
                            dve.wait_ge(negm_ready, layer_negm + n + 1)
                            tt(esink[:, turn, :], negm[:, turn, :], sink[:, :], ALU.add).then_inc(sarg_ready, 1)
                        for c in range(n * per, min((n + 1) * per, CONV_WIDTH)):
                            tap(c)
                    if n >= 2:
                        next(rest, None)
                    if layer == 0 and 0 < n <= ADA_ITEMS:
                        split_to(first["ada", 1] + n)
                    if n == len(its) - 4:
                        split_to(first["out", layer] + 2)
                    if n >= 10 and (n - 10) % 8 == 0:
                        tile = (n - 10) // 8
                        turn = tile % 2
                        after(esink_ready)
                        step(tt(rsum[:, turn, :], rsum[:, turn, :], esink[:, turn, :], ALU.add))
                        step(nc.vector.reciprocal(rsum[:, turn, :], rsum[:, turn, :]))
                        dve.wait_ge(att_done, base + 8 * (tile + 1))
                        tt(proj[:, tile, C_Q:C_RQ].rearrange("p (h d) -> p h d", d=HEAD_DIM), OB[:, :].rearrange("p (h d) -> p h d", d=HEAD_DIM),
                           per_group(rsum[:, turn, :], HEAD_DIM), ALU.mult).then_inc(att_read, 1)

            def conv_norm(layer):
                nt = len(tiles_of(layer))
                if layer == 0:
                    dve.wait_ge(tap_done, CONV_WIDTH)
                    dve.wait_ge(pool_tap, CONV_WIDTH)
                    ada_rows(1)
                for t in range(nt):
                    copy_out(CV[:, t, :], take()[:, 0:256])
                emptied()
                for t in range(nt):
                    ins = nc.vector.bn_stats(bst[:, t, :], CV[:, t, :])
                step(ins)
                for t in range(nt):
                    ins = nc.vector.bn_aggr(bag[:, t, :], bst[:, t, :])
                ins.then_inc(cv_var, 1)
                after(cv_rstd)
                for t in range(nt):
                    ins = nc.vector.tensor_scalar(CV[:, t, :], CV[:, t, :], bag[:, t, 0:1], lnr[:, t:t + 1], ALU.subtract, ALU.mult)
                step(ins)
                c = CV[:, 0:nt, :]
                step(tt(c, c, lnw[:, :].unsqueeze(1).broadcast_to([P, nt, 256]), ALU.mult))
                tt(c, c, lnb[:, :].unsqueeze(1).broadcast_to([P, nt, 256]), ALU.add).then_inc(ln_ready, 1)

            def add_gated(half, t, last):
                s = t // TT
                y = YG[:, t % 2, :]
                x = X[:, t, half * 512:(half + 1) * 512]
                tt(y, take()[:, :], GB[:, s, half * 512:(half + 1) * 512], ALU.mult).then_inc(v_done, 1)
                emptied()
                ins = tt(x, x, y, ALU.add)
                if last:
                    ins.then_inc(x_ready, 1)
                    x_count[0] += 1

            def route():
                L, first, second, chosen = top[:, 1, :, :], top[:, 2, :, :], top[:, 3, :, :], top[:, 0, :, :]
                tmp, comb = top[:, 4, :, :], top[:, 5, :, :]
                idx = table("experts").unsqueeze(1).broadcast_to([P, TT, N_EXPERTS])
                copy_out(L, take()[:, 0:16].rearrange("p (t e) -> p t e", t=TT))
                emptied()

                def pick(value, mask_, at):
                    step(nc.vector.tensor_reduce(value, L, AX.X, ALU.max))
                    step(tt(tmp, L, per_group(value, N_EXPERTS), ALU.is_equal))
                    step(nc.vector.tensor_scalar(tmp, tmp, -64.0, 64.0, ALU.mult, ALU.add))
                    step(tt(tmp, tmp, idx, ALU.add))
                    step(nc.vector.tensor_reduce(at, tmp, AX.X, ALU.min))
                    return tt(mask_, idx, per_group(at, N_EXPERTS), ALU.is_equal)

                step(pick(best[:, 0, :], first, best[:, 4, :]))
                step(nc.vector.scalar_tensor_tensor(L, first, BIG_NEG, L, ALU.mult, ALU.add))
                step(pick(best[:, 1, :], second, best[:, 5, :]))
                tt(chosen, first, second, ALU.add).then_inc(mask_ready, 1)
                tt(best[:, 2, :], best[:, 1, :], best[:, 0, :], ALU.subtract).then_inc(lexp_in, 1)
                after(lexp_out)
                step(nc.vector.tensor_scalar(best[:, 6, :], best[:, 3, :], 1.0, None, ALU.add))
                step(nc.vector.reciprocal(best[:, 6, :], best[:, 6, :]))
                step(tt(best[:, 7, :], best[:, 6, :], best[:, 3, :], ALU.mult))
                step(tt(tmp, first, per_group(best[:, 6, :], N_EXPERTS), ALU.mult))
                step(tt(comb, second, per_group(best[:, 7, :], N_EXPERTS), ALU.mult))
                step(tt(comb, comb, tmp, ALU.add))
                b = take()
                nc.vector.tensor_reduce(most[:, 0:1], b[:, 16:24], AX.X, ALU.max)
                copy_out(top[:, 6, :, :], b[:, 0:16].rearrange("p (t e) -> p t e", t=TT))
                emptied()
                nc.vector.tensor_copy(mosti[:, :], most[:, 0:1]).then_inc(most_ready, 1)

            def place_tokens(part):
                rank, chosen, comb = top[:, 6, :, :], top[:, 0, :, :], top[:, 5, :, :]
                if part:
                    nc.vector.tensor_scalar(rank, rank, -float(P), None, ALU.add).then_inc(rank_moved, 1)
                    dve.wait_ge(rank_moved, 1)

                def weighted(e):
                    for i in range(2):
                        for t in range(TT):
                            ins = nc.vector.tensor_scalar(WR[:, (e // 2) % 2, i * TT + t, :], table("slots"),
                                                          rank[:, t, e + i:e + i + 1], comb[:, t, e + i:e + i + 1],
                                                          ALU.is_equal, ALU.mult)
                    ins.then_inc(scat_in, 1)

                if not part:
                    nc.vector.memset(PA[:, :, N_EXPERTS, :], 0.0)
                weighted(0)
                for e in range(0, N_EXPERTS, 2):
                    if e + 2 < N_EXPERTS:
                        weighted(e + 2)
                    for i in range(2):
                        for t in range(TT):
                            nc.vector.tensor_scalar(PA[:, t, e + i, :], table("slots"), rank[:, t, e + i:e + i + 1],
                                                    chosen[:, t, e + i:e + i + 1], ALU.is_equal, ALU.mult)
                    copy_out(SA[:, e:e + 2, :], take()[:, :].rearrange("p (e n) -> p e n", e=2))
                emptied()

            def split_expert(i, n, part):
                dve.wait_ge(hi_ready, i * PAIR_ITEMS + (BASE + part * PAIRS * PAIR_ITEMS + n + 1))
                tt(parts[:, n % PARTS, 1, :], raw[:, n % RAW, :], parts_f[:, n % PARTS, 0, :], ALU.subtract).then_inc(lo_ready, 1)

            def experts(part):
                U, Y, T, M = bank[1], bank[2:4], bank[4:6], bank[6:8]
                s0, e0, j0 = part * N_EXPERTS * EF_SLICES, part * N_EXPERTS, part * GATHERS

                def gathered(i, j):
                    dve.wait_ge(gather_full, i * 4 + (2 * (j0 + j) + 2))
                    for k in range(4, KT):
                        ins = nc.vector.tensor_scalar(XF[:, k, :], M[1][:, (k - 4) * P:(k - 3) * P], scl[:, 1, k, 0:1],
                                                      ada[:, 3 * KT + k, 0:1], ALU.mult, ALU.add)
                    ins.then_inc(xe_hi, 1)
                    dve.wait_ge(xe_high, i * 2 + (j0 + j + 1))
                    tt(XEr[:, j % 2, 1, :, :], XF, XEr_f[:, j % 2, 0, :, :], ALU.subtract).then_inc(xe_ready, 1)

                def scatter_row(i, ee):
                    nc.vector.tensor_copy(SCAT[:, ee, :], SA[:, bass.ds(i * 2 + ee, 1), :].rearrange("p e n -> p (e n)"))\
                        .then_inc(st_ready, 1)

                def expert_out(i, ee):
                    dve.wait_ge(down_done, i * PAIR_SLICES + (s0 + EF_SLICES * (ee + 1) + CREDIT))
                    for h in range(2):
                        nc.vector.tensor_copy(YS[:, h * 512:(h + 1) * 512], Y[h][:, :]).then_inc(y_ready, 1)

                def add_scattered(i, ee):
                    for t in range(TT):
                        for h in range(2):
                            n = 4 * (e0 + ee) + 2 * t + h
                            dve.wait_ge(scatter_full, i * 8 + (n + 1))
                            acc = ACC[:, t, h * 512:(h + 1) * 512]
                            tt(acc, M[h][:, :], acc, ALU.add).then_inc(scatter_read, 1)

                def pair(i, opening):
                    def turned(g):
                        dve.wait_ge(ht_hi, i * PAIR_SLICES + (s0 + g + 1))
                        tt(HTr[:, g % 2, 1, :], T[g % 2][:, :], HTr_f[:, g % 2, 0, :], ALU.subtract).then_inc(ht_ready, 1)

                    if not opening:
                        split_expert(i, 0, part)
                        split_expert(i, 1, part)
                        expert_out(i, -1)
                        split_expert(i, 2, part)
                        split_expert(i, 3, part)
                    scatter_row(i, 0)
                    n = PARTS
                    for g in range(PAIR_SLICES):
                        split_expert(i, n, part)
                        if g >= 1:
                            turned(g - 1)
                        if g == 5:
                            gathered(i, 1)
                        split_expert(i, n + 1, part)
                        split_expert(i, n + 2, part)
                        dve.wait_ge(up_full, i * PAIR_SLICES + (s0 + g + 1))
                        dve.wait_ge(gate_read, i * PAIR_SLICES + (s0 + g + 1))
                        if g >= 2 or not opening:
                            dve.wait_ge(h_turned, i * PAIR_SLICES + (s0 + g - 1))
                        tt(HE[:, g % 2, :], U[:, :], SGE[:, g % 2, :], ALU.mult).then_inc(up_read, 1)
                        if g == 1 and not opening:
                            add_scattered(i, -1)
                        if g == 3:
                            scatter_row(i, 1)
                        if g == EF_SLICES + 1:
                            add_scattered(i, 0)
                        more = 4 if g == 0 or g == PAIR_SLICES - 1 else 6
                        for m in range(n + 3, n + more):
                            split_expert(i, m, part)
                        n += more
                        if g == EF_SLICES:
                            expert_out(i, 0)
                    turned(PAIR_SLICES - 1)
                    gathered(i, 2)

                gathered(0, 0)
                pair(0, True)
                with dve.Fori(1, PAIRS) as i:
                    pair(i, False)
                expert_out(PAIRS, -1)
                add_scattered(PAIRS, -1)

            dve.wait_ge(tables_in, 16)
            cond_low(0)
            att_base = 0
            for layer in range(DEPTH):
                tiles = tiles_of(layer)
                layer_negm = 0 if layer == 0 else 8 * NT
                if layer == 0:
                    split_to(3)
                    after(small_in, 16 * N_SMALL)
                nc.vector.tensor_scalar(nsink[:, :], sink[:, :], -1.0, None, ALU.mult)
                logit = dlog[:, :, :].rearrange("p d h -> p h d")
                nc.vector.tensor_scalar(dmin[:, :, :], logit, 0.0, None, ALU.min)
                nc.vector.scalar_tensor_tensor(dneg[:, :, :], logit, -1.0, logit, ALU.mult, ALU.min)\
                    .then_inc(dneg_ready, 1)
                if layer == 0:
                    split_to(ADA_ITEMS - 6)
                scale_tokens(range(NT))
                split_to(first["in", layer] + 2)
                if layer == 0:
                    ada_columns(0)
                modulate(0, (0, 1))
                decay_arguments()
                projections(layer)
                retention(layer, att_base + NT)
                attention(layer, att_base + NT)
                att_base += NT + 8 * len(tiles)
                conv_norm(layer)
                for t in tiles:
                    for half in range(2):
                        k = slice(4 * half, 4 * half + 4)
                        tok = slice(t * P, (t + 1) * P)
                        b = take()
                        after(mix_hi)
                        tt(hTr[:, 1, k, tok], b[:, :].rearrange("p (k n) -> p k n", k=4), hTr_f[:, 0, k, tok], ALU.subtract)\
                            .then_inc(v_done, 1)
                O = first["out", layer]
                for half in range(2):
                    split_to(O + 2 * half + 3 if half == 0 or layer == 0 else O + 4)
                    for t in tiles:
                        add_gated(half, t, half == 1)
                    if half == 0:
                        split_to(O + 4)
                if layer == 0:
                    split_to(O + 7)
                dve.wait_ge(x_ready, x_count[0])
                scale_tokens(tiles)
                modulate(1, (0, 1) if layer == 0 else ())
                if layer == 0:
                    n = first["ffn"] + 3

                    def hidden_low(f):
                        after(ff_hi)
                        tt(HFr[:, 1, f % HALF_FF, :], HF[:, f % 2, :], HFr_f[:, 0, f % HALF_FF, :], ALU.subtract).then_inc(ff_lo, 1)

                    for p0 in range(0, FF_TILES, HALF_FF):
                        for f in range(p0, p0 + HALF_FF):
                            b = take()
                            dve.wait_ge(a_done, job[("gate", f)] + 1)
                            if f >= 2:
                                dve.wait_ge(ff_lo, f - 1)
                            tt(HF[:, f % 2, :], b[:, :], SG[:, f % 2, :], ALU.mult).then_inc(v_done, 1)
                            if f > p0:
                                hidden_low(f - 1)
                            n += 1
                            split_to(n)
                        hidden_low(p0 + HALF_FF - 1)
                        if p0:
                            after(small_in, 16 * N_SMALL)
                            ada_columns(1)
                        for half in range(2):
                            for j in range(len(ff_split)):
                                if j == len(ff_split) - 1:
                                    for t in tiles:
                                        add_gated(half, t, p0 > 0 and half == 1)
                                n += 1
                                split_to(min(n, first["in", 1] + 2))
                    dve.wait_ge(x_ready, x_count[0])
            for n in range(PARTS):
                split_expert(0, n, 0)
            route()
            place_tokens(0)
            nc.vector.memset(ACC_t[:, :], 0.0).then_inc(scatter_read, 1)
            experts(0)
            dve.wait_ge(most_ready, 1)
            over = dve.value_load(mosti[0:1, 0:1], min_val=0, max_val=SEQ)
            with dve.If(over > P):
                place_tokens(1)
                for n in range(PARTS):
                    split_expert(0, n, 1)
                experts(1)
            for t in range(TT):
                step(tt(ACC[:, t, :], ACC[:, t, :], GBX[:, :], ALU.mult))
                tt(X[:, t, :], X[:, t, :], ACC[:, t, :], ALU.add).then_inc(out_ready, 1)


_INS = ['x', 'c', 'ctx', 'c_ctx', 'ada_w', 'ada_b', 'norm1_w', 'norm2_w', 'w_in', 'w_out', 'q_norm_w', 'k_norm_w',
        'attn_sink', 'ret_decay_f', 'ret_decay_b', 'ret_gn_w', 'conv_w', 'conv_b', 'conv_ln_w', 'conv_ln_b',
        'ffn_w_gate', 'ffn_w_up', 'ffn_w_down', 'router_w', 'moe_w_gate', 'moe_w_up', 'moe_w_down']


def kernel(**inputs):
    import numpy as _np
    import concourse.bacc as _bacc
    from concourse import mybir as _mybir
    from concourse.bass_utils import run_bass_kernel_spmd as _run

    nc = _bacc.Bacc("TRN2", target_bir_lowering=False, num_devices=1)
    arrays, io = {}, {}
    tables, place = shape_constants()
    for name in _INS + ['shape_tables']:
        a = tables if name == 'shape_tables' else _np.ascontiguousarray(inputs[name])
        arrays[f"in_{name}_dram"] = a
        io[name] = nc.dram_tensor(f"in_{name}_dram", a.shape, _mybir.dt.from_np(a.dtype), kind="ExternalInput").ap()
    io["out"] = nc.dram_tensor("out_0_dram", (1, SEQ, D_MODEL), _mybir.dt.float32, kind="ExternalOutput").ap()
    build(nc, io, place)
    r = _run(nc, [arrays], core_ids=[0])
    return r.results[0]["out_0_dram"]
```
